# Optimizing a Trainium2 kernel written in Bass

```python
import jax
import jax.numpy as jnp
from jax import lax
import numpy as np

D_MODEL = 1024
BATCH = 1
SEQ = 512
DEPTH = 1
DEC_BATCH = 8
DEC_SEQ = 1
PAST_LEN = 2048
PAGE_SIZE = 128

HEAD_DIM = 64
D_MIX = D_MODEL
GROUP_W = D_MIX // 4
C_CONV = GROUP_W
H_NSA = GROUP_W // HEAD_DIM
H_MOBA = GROUP_W // HEAD_DIM
C_POOL = GROUP_W
CONV_W = 31
L_CMP = 32
CMP_STRIDE = 16
L_SEL = 64
N_SEL = 16
WINDOW = 512
MOBA_BLOCK = 256
MOBA_TOPK = 3
POOL_WINDOWS = (2, 4, 8, 16)
POOL_GROUPS = len(POOL_WINDOWS)
POOL_GW = C_POOL // POOL_GROUPS
POOL_MAX = max(POOL_WINDOWS)
D_FF = 4 * D_MODEL
ALPHA = (2 * DEPTH) ** 0.25
BETA = (8 * DEPTH) ** -0.25
LN_EPS = 1e-5
Q_CHUNK = 64
WIN_QBLOCK = 128
ATTN_SCALE = HEAD_DIM ** -0.5
N_CONV_IN = 2 * C_CONV
N_NSA_Q = H_NSA * HEAD_DIM
N_NSA_KV = 6 * HEAD_DIM
N_NSA_G = 3 * H_NSA
N_MOBA_IN = 3 * H_MOBA * HEAD_DIM
N_POOL_IN = C_POOL
N_IN = N_CONV_IN + N_NSA_Q + N_NSA_KV + N_NSA_G + N_MOBA_IN + N_POOL_IN
IN_SPLITS = tuple(int(s) for s in np.cumsum([N_CONV_IN, N_NSA_Q, N_NSA_KV, N_NSA_G, N_MOBA_IN]))

kernel_name = 'hymba_conv_nsa_moba_pool_decode_step'

def layer_norm(x, g, b):
    xf = x.astype(jnp.float32)
    mu = jnp.mean(xf, axis=-1, keepdims=True)
    var = jnp.mean(jnp.square(xf - mu), axis=-1, keepdims=True)
    return ((xf - mu) * lax.rsqrt(var + LN_EPS)).astype(x.dtype) * g + b

def masked_softmax(s, mask):
    s = jnp.where(mask, s.astype(jnp.float32), -jnp.inf)
    m = jnp.max(s, axis=-1, keepdims=True)
    m = jnp.where(jnp.isfinite(m), m, 0.0)
    e = jnp.exp(s - m)
    d = jnp.sum(e, axis=-1, keepdims=True)
    return e / jnp.where(d > 0, d, 1.0)

def map_query_chunks(fn, q, qpos, chunk):
    b, tq = q.shape[:2]
    if tq <= chunk:
        return fn(q, qpos)
    n = -(-tq // chunk)
    pad = n * chunk - tq
    qp = jnp.pad(q, [(0, 0), (0, pad)] + [(0, 0)] * (q.ndim - 2))
    pp = jnp.concatenate([qpos, jnp.full((pad,), qpos[-1], qpos.dtype)])
    qc = jnp.moveaxis(qp.reshape(b, n, chunk, *q.shape[2:]), 1, 0)
    out = lax.map(lambda a: fn(a[0], a[1]), (qc, pp.reshape(n, chunk)))
    out = jnp.moveaxis(out, 0, 1)
    return out.reshape(b, n * chunk, *out.shape[3:])[:, :tq]

def conv_module(u, buf, dw, dw_b, ln_g, ln_b, pw):
    a, g = jnp.split(u, 2, axis=-1)
    z = a * jax.nn.sigmoid(g)
    zc = jnp.concatenate([buf, z], axis=1)
    y = lax.conv_general_dilated(zc, dw[:, None, :], window_strides=(1,), padding='VALID',
                                 dimension_numbers=('NWC', 'WIO', 'NWC'),
                                 feature_group_count=C_CONV) + dw_b
    y = jax.nn.silu(layer_norm(y, ln_g, ln_b))
    return y @ pw, zc[:, -(CONV_W - 1):]

def pool_mixer(p, buf, qpos, pool_w, pool_scale):
    b, t, c = p.shape
    rows = jnp.concatenate([buf, p], axis=1)
    rf = rows.astype(jnp.float32)
    cs = jnp.concatenate([jnp.zeros((b, 1, c), jnp.float32), jnp.cumsum(rf, axis=1)], axis=1)
    means = []
    for g, w in enumerate(POOL_WINDOWS):
        lo, hi = g * POOL_GW, (g + 1) * POOL_GW
        s = cs[:, POOL_MAX:POOL_MAX + t, lo:hi] - cs[:, POOL_MAX - w:POOL_MAX - w + t, lo:hi]
        cnt = jnp.minimum(w, qpos + 1).astype(jnp.float32)[None, :, None]
        means.append(s / cnt)
    d = (jnp.concatenate(means, axis=-1) - rf[:, POOL_MAX - 1:]).astype(p.dtype)
    y = jnp.einsum('btgc,gcd->btgd', d.reshape(b, t, POOL_GROUPS, POOL_GW), pool_w).reshape(b, t, c)
    return y * pool_scale, rows[:, -(POOL_MAX - 1):]

def nsa_compress(k, pos_emb, w1, w2):
    b, tk, d = k.shape
    n_s = tk // CMP_STRIDE
    chunks = k[:, :n_s * CMP_STRIDE].reshape(b, n_s, CMP_STRIDE * d)
    w1r = w1.reshape(2, CMP_STRIDE * d, -1)
    bias = pos_emb.reshape(-1) @ w1
    hid = (chunks @ w1r[0])[:, :-1] + (chunks @ w1r[1])[:, 1:] + bias
    return jax.nn.silu(hid) @ w2

def nsa_chunk(q, qpos, kc, vc, ks, vs):
    n_cmp, n_sel = kc.shape[1], ks.shape[1]
    s = jnp.einsum('bqhd,bnd->bqhn', q, kc) * ATTN_SCALE
    cmp_last = jnp.arange(n_cmp) * CMP_STRIDE + (L_CMP - 1)
    p = masked_softmax(s, (cmp_last[None, :] <= qpos[:, None])[None, :, None, :])
    o_cmp = jnp.einsum('bqhn,bnd->bqhd', p.astype(q.dtype), vc)
    j = jnp.arange(n_cmp)[:, None]
    i = jnp.arange(n_sel)[None, :]
    cover = ((j * CMP_STRIDE < (i + 1) * L_SEL) & (j * CMP_STRIDE + L_CMP > i * L_SEL)).astype(jnp.float32)
    imp = jnp.einsum('bqn,ns->bqs', p.sum(axis=2), cover)
    blk = jnp.arange(n_sel)[None, :]
    cur = (qpos // L_SEL)[:, None]
    imp = jnp.where(((blk == 0) | (blk == cur) | (blk == cur - 1))[None], jnp.inf, imp)
    imp = jnp.where((blk * L_SEL > qpos[:, None])[None], -jnp.inf, imp)
    _, idx = lax.top_k(imp, min(N_SEL, n_sel))
    bi = jnp.arange(q.shape[0])[:, None, None]
    kg, vg = ks[bi, idx], vs[bi, idx]
    kpos = idx[..., None] * L_SEL + jnp.arange(L_SEL)
    mask = kpos <= qpos[None, :, None, None]
    sc = jnp.einsum('bqhd,bqjsd->bqhjs', q, kg) * ATTN_SCALE
    b, c, h, k, l = sc.shape
    p2 = masked_softmax(sc.reshape(b, c, h, k * l), mask.reshape(b, c, 1, k * l))
    o_sel = jnp.einsum('bqhjs,bqjsd->bqhd', p2.reshape(sc.shape).astype(q.dtype), vg)
    return o_cmp, o_sel

def nsa_compressed_selected(q, qpos, rows, cmp_pos, cmp_w1, cmp_w2):
    b, tk = rows.shape[:2]
    kc = nsa_compress(rows[:, :, 0], cmp_pos[0], cmp_w1[0], cmp_w2[0])
    vc = nsa_compress(rows[:, :, 1], cmp_pos[1], cmp_w1[1], cmp_w2[1])
    n_sel = -(-tk // L_SEL)
    sel = jnp.pad(rows[:, :, 2:], ((0, 0), (0, n_sel * L_SEL - tk), (0, 0), (0, 0)))
    sel = sel.reshape(b, n_sel, L_SEL, 2, HEAD_DIM)
    ks, vs = sel[:, :, :, 0], sel[:, :, :, 1]

    def chunk(qc, pc):
        return jnp.stack(nsa_chunk(qc, pc, kc, vc, ks, vs), axis=2)
    return map_query_chunks(chunk, q, qpos, Q_CHUNK)

def window_attend(q, qpos, k, v, kpos):
    s = jnp.einsum('bqhd,bkd->bqhk', q, k) * ATTN_SCALE
    rel = qpos[:, None] - kpos[None, :]
    mask = (rel >= 0) & (rel <= WINDOW) & (kpos >= 0)[None, :]
    p = masked_softmax(s, mask[None, :, None, :])
    return jnp.einsum('bqhk,bkd->bqhd', p.astype(q.dtype), v)

def window_banded(q, k, v):
    b, t = q.shape[:2]
    nb = t // WIN_QBLOCK
    kp = jnp.pad(k, ((0, 0), (WINDOW, 0), (0, 0)))
    vp = jnp.pad(v, ((0, 0), (WINDOW, 0), (0, 0)))
    idx = jnp.arange(nb)[:, None] * WIN_QBLOCK + jnp.arange(WINDOW + WIN_QBLOCK)
    qb = q.reshape(b, nb, WIN_QBLOCK, *q.shape[2:])
    qpos = jnp.arange(t).reshape(nb, WIN_QBLOCK)
    out = jax.vmap(window_attend, in_axes=(1, 0, 1, 1, 0), out_axes=1)(qb, qpos, kp[:, idx], vp[:, idx], idx - WINDOW)
    return out.reshape(q.shape)

def moba_chunk(q, qpos, kp, vp, kmean):
    b, c, h, _ = q.shape
    nb = kmean.shape[1]
    s = jnp.einsum('bqhd,bnhd->bqhn', q, kmean).astype(jnp.float32)
    cur = qpos // MOBA_BLOCK
    past = jnp.arange(nb)[None, :] < cur[:, None]
    s = jnp.where(past[None, :, None, :], s, -jnp.inf)
    _, top = lax.top_k(s, min(MOBA_TOPK, nb))
    cur_b = cur[None, :, None, None]
    own = jnp.broadcast_to(cur_b, (b, c, h, 1))
    idx = jnp.concatenate([top, own], axis=-1)
    ok = jnp.concatenate([top < cur_b, jnp.ones((b, c, h, 1), bool)], axis=-1)
    bi = jnp.arange(b)[:, None, None, None]
    hi = jnp.arange(h)[None, None, :, None]
    kg = kp[bi, idx, :, hi]
    vg = vp[bi, idx, :, hi]
    kpos = idx[..., None] * MOBA_BLOCK + jnp.arange(MOBA_BLOCK)
    mask = ok[..., None] & (kpos <= qpos[None, :, None, None, None])
    sc = jnp.einsum('bqhd,bqhjsd->bqhjs', q, kg) * ATTN_SCALE
    p = masked_softmax(sc.reshape(b, c, h, -1), mask.reshape(b, c, h, -1))
    return jnp.einsum('bqhjs,bqhjsd->bqhd', p.reshape(sc.shape).astype(q.dtype), vg)

def moba_attend(q, qpos, k, v):
    b, tk, h, d = k.shape
    nb = -(-tk // MOBA_BLOCK)
    pad = ((0, 0), (0, nb * MOBA_BLOCK - tk), (0, 0), (0, 0))
    kp = jnp.pad(k, pad).reshape(b, nb, MOBA_BLOCK, h, d)
    vp = jnp.pad(v, pad).reshape(b, nb, MOBA_BLOCK, h, d)
    kmean = jnp.mean(kp.astype(jnp.float32), axis=2).astype(k.dtype)
    return map_query_chunks(lambda qc, pc: moba_chunk(qc, pc, kp, vp, kmean), q, qpos, Q_CHUNK)

def decoder_layer(x, pos0, conv_buf, pool_buf, win_buf, nsa_past, moba_past, lw, win_len):
    b, t, _ = x.shape
    z = x @ lw['w_in']
    u_conv, q_nsa, kv_nsa, g_nsa, qkv_moba, u_pool = jnp.split(z, IN_SPLITS, axis=-1)
    qpos = pos0 + jnp.arange(t)

    y_conv, conv_new = conv_module(u_conv, conv_buf, lw['conv_dw'], lw['conv_dw_b'],
                                   lw['conv_ln_g'], lw['conv_ln_b'], lw['conv_pw'])

    qn = q_nsa.reshape(b, t, H_NSA, HEAD_DIM)
    kv = kv_nsa.reshape(b, t, 6, HEAD_DIM)
    nsa_rows = kv[:, :, :4]
    win_rows = kv[:, :, 4:]
    nsa_all = nsa_rows if nsa_past is None else jnp.concatenate([nsa_past, nsa_rows], axis=1)
    o_cs = nsa_compressed_selected(qn, qpos, nsa_all, lw['nsa_cmp_pos'], lw['nsa_cmp_w1'], lw['nsa_cmp_w2'])
    if win_buf is None:
        o_win = window_banded(qn, win_rows[:, :, 0], win_rows[:, :, 1])
        win_new = jnp.pad(win_rows, ((0, 0), (win_len, 0), (0, 0), (0, 0)))[:, -win_len:]
    else:
        win_all = jnp.concatenate([win_buf, win_rows], axis=1)
        kpos = pos0 - win_len + jnp.arange(win_len + t)
        o_win = window_attend(qn, qpos, win_all[:, :, 0], win_all[:, :, 1], kpos)
        win_new = win_all[:, -win_len:]
    gates = jax.nn.sigmoid(g_nsa.reshape(b, t, 3, H_NSA, 1))
    o_nsa = gates[:, :, 0] * o_cs[:, :, 0] + gates[:, :, 1] * o_cs[:, :, 1] + gates[:, :, 2] * o_win

    m = qkv_moba.reshape(b, t, 3, H_MOBA, HEAD_DIM)
    moba_rows = m[:, :, 1:]
    moba_all = moba_rows if moba_past is None else jnp.concatenate([moba_past, moba_rows], axis=1)
    o_moba = moba_attend(m[:, :, 0], qpos, moba_all[:, :, 0], moba_all[:, :, 1])

    y_pool, pool_new = pool_mixer(u_pool, pool_buf, qpos, lw['pool_w'], lw['pool_scale'])

    mix = jnp.concatenate([y_conv, o_nsa.reshape(b, t, -1), o_moba.reshape(b, t, -1), y_pool], axis=-1) @ lw['w_out']
    x = layer_norm(ALPHA * x + mix, lw['ln1_g'], lw['ln1_b'])
    ff = jnp.square(jax.nn.relu(x @ lw['w_up'])) @ lw['w_down']
    x = layer_norm(ALPHA * x + ff, lw['ln2_g'], lw['ln2_b'])
    return x, (moba_rows, nsa_rows, win_new, conv_new, pool_new)

def setup_inputs(seed: int = 0) -> dict:
    key = jax.random.key(seed)
    ks = iter(jax.random.split(key, 40))
    n_pages = PAST_LEN // PAGE_SIZE
    n_pool = (DEC_BATCH * n_pages * 5) // 4
    win_len = min(WINDOW, PAST_LEN)

    def nrm(shape, scale):
        return jax.random.normal(next(ks), shape, jnp.float32) * scale

    perm = jax.random.permutation(next(ks), n_pool)
    page_table = perm[:DEC_BATCH * n_pages].reshape(DEC_BATCH, n_pages).astype(jnp.int32)
    return {
        'x_prompt': nrm((BATCH, SEQ, D_MODEL), 1.0),
        'x_sample': nrm((DEC_BATCH, DEC_SEQ, D_MODEL), 1.0),
        'cache_moba_kv': nrm((DEPTH, n_pool, PAGE_SIZE, 2, H_MOBA, HEAD_DIM), 1.0),
        'cache_nsa_kv': nrm((DEPTH, n_pool, PAGE_SIZE, 4, HEAD_DIM), 1.0),
        'state_nsa_win': nrm((DEPTH, DEC_BATCH, win_len, 2, HEAD_DIM), 1.0),
        'state_conv': nrm((DEPTH, DEC_BATCH, CONV_W - 1, C_CONV), 0.5),
        'state_pool': nrm((DEPTH, DEC_BATCH, POOL_MAX - 1, C_POOL), 1.0),
        'page_table': page_table,
        'w_in': nrm((DEPTH, D_MODEL, N_IN), D_MODEL ** -0.5),
        'conv_dw': nrm((DEPTH, CONV_W, C_CONV), CONV_W ** -0.5),
        'conv_dw_b': nrm((DEPTH, C_CONV), 0.01),
        'conv_ln_g': 1.0 + nrm((DEPTH, C_CONV), 0.05),
        'conv_ln_b': nrm((DEPTH, C_CONV), 0.01),
        'conv_pw': nrm((DEPTH, C_CONV, C_CONV), C_CONV ** -0.5),
        'nsa_cmp_pos': nrm((DEPTH, 2, L_CMP, HEAD_DIM), 0.5),
        'nsa_cmp_w1': nrm((DEPTH, 2, L_CMP * HEAD_DIM, HEAD_DIM), (L_CMP * HEAD_DIM) ** -0.5),
        'nsa_cmp_w2': nrm((DEPTH, 2, HEAD_DIM, HEAD_DIM), HEAD_DIM ** -0.5),
        'pool_w': nrm((DEPTH, POOL_GROUPS, POOL_GW, POOL_GW), POOL_GW ** -0.5),
        'pool_scale': 1.0 + nrm((DEPTH, C_POOL), 0.1),
        'w_out': nrm((DEPTH, D_MIX, D_MODEL), BETA * D_MIX ** -0.5),
        'ln1_g': 1.0 + nrm((DEPTH, D_MODEL), 0.05),
        'ln1_b': nrm((DEPTH, D_MODEL), 0.01),
        'w_up': nrm((DEPTH, D_MODEL, D_FF), BETA * D_MODEL ** -0.5),
        'w_down': nrm((DEPTH, D_FF, D_MODEL), BETA * D_FF ** -0.5),
        'ln2_g': 1.0 + nrm((DEPTH, D_MODEL), 0.05),
        'ln2_b': nrm((DEPTH, D_MODEL), 0.01),
    }

def reference(x_prompt, x_sample, cache_moba_kv, cache_nsa_kv, state_nsa_win, state_conv, state_pool, page_table,
              w_in, conv_dw, conv_dw_b, conv_ln_g, conv_ln_b, conv_pw, nsa_cmp_pos, nsa_cmp_w1, nsa_cmp_w2,
              pool_w, pool_scale, w_out, ln1_g, ln1_b, w_up, w_down, ln2_g, ln2_b):
    past_len = page_table.shape[1] * cache_nsa_kv.shape[2]
    win_len = state_nsa_win.shape[2]
    bp, bs = x_prompt.shape[0], x_sample.shape[0]
    yp, ys = x_prompt, x_sample
    st_p, st_s = [], []
    for l in range(DEPTH):
        lw = {'w_in': w_in[l], 'conv_dw': conv_dw[l], 'conv_dw_b': conv_dw_b[l], 'conv_ln_g': conv_ln_g[l],
              'conv_ln_b': conv_ln_b[l], 'conv_pw': conv_pw[l], 'nsa_cmp_pos': nsa_cmp_pos[l],
              'nsa_cmp_w1': nsa_cmp_w1[l], 'nsa_cmp_w2': nsa_cmp_w2[l], 'pool_w': pool_w[l],
              'pool_scale': pool_scale[l], 'w_out': w_out[l], 'ln1_g': ln1_g[l], 'ln1_b': ln1_b[l],
              'w_up': w_up[l], 'w_down': w_down[l], 'ln2_g': ln2_g[l], 'ln2_b': ln2_b[l]}
        yp, st = decoder_layer(yp, 0, jnp.zeros((bp, CONV_W - 1, C_CONV), yp.dtype),
                               jnp.zeros((bp, POOL_MAX - 1, C_POOL), yp.dtype), None, None, None, lw, win_len)
        st_p.append(st)
        nsa_past = cache_nsa_kv[l, page_table].reshape(bs, past_len, 4, HEAD_DIM)
        moba_past = cache_moba_kv[l, page_table].reshape(bs, past_len, 2, H_MOBA, HEAD_DIM)
        ys, st = decoder_layer(ys, past_len, state_conv[l], state_pool[l], state_nsa_win[l],
                               nsa_past, moba_past, lw, win_len)
        st_s.append(st)

    def stk(sts, i):
        return jnp.stack([s[i] for s in sts], axis=0)

    return (yp, ys, stk(st_p, 0), stk(st_s, 0), stk(st_p, 1), stk(st_s, 1), stk(st_p, 2), stk(st_s, 2),
            stk(st_p, 3), stk(st_s, 3), stk(st_p, 4), stk(st_s, 4))


_drawn_inputs = setup_inputs


def setup_inputs(seed=0):
    import zlib

    import numpy as np

    out = dict(_drawn_inputs(seed))
    spreads = {}
    factors = {'cache_moba_kv': 4.011,
     'cache_nsa_kv': 5.542,
     'conv_dw_b': 8.0,
     'conv_ln_g': 6.33,
     'conv_ln_b': 51.189,
     'pool_scale': 2.788,
     'ln1_b': 5.427,
     'ln2_b': 5.617}
    for name, (base, spread) in spreads.items():
        noise = np.random.default_rng([zlib.crc32(name.encode()), seed]).standard_normal(out[name].shape)
        drawn = base * np.exp(spread * noise) if base else spread * noise
        out[name] = jnp.asarray(drawn.astype(out[name].dtype))
    for name, factor in factors.items():
        out[name] = (out[name] * factor).astype(out[name].dtype)
    return out
```

```python
import concourse.bass as bass
from concourse import mybir
from contextlib import ExitStack
import numpy as np

F32 = mybir.dt.float32
F32R = mybir.dt.float32r
I32 = mybir.dt.int32
ALU = mybir.AluOpType
ACT = mybir.ActivationFunctionType
AX = mybir.AxisListType

P = 128
D = 1024
KT = D // P
T, B = 512, 8
NT = T + B
HALF = NT // 2
H, HD = 4, 64
PAGE, PAGES = 128, 16
NPOOL = 160
NCHUNK = 128
NCMP = NCHUNK - 1
NCMP_P = T // 16 - 1
NSELB = 33
CW = 31
ALPHA = 2.0 ** 0.25
EPS = 1e-5
NEG = -1e30
FF = 4 * D
NG = 4
QT = T // P

S_CMP, S_Q, S_KSEL, S_KWIN, S_V, S_GATE, S_CA, S_CG, S_PO, S_MQ, S_MK, S_MV = 0, 1, 3, 4, 5, 6, 7, 9, 11, 13, 15, 17
NSLOT = 19
PANEL_SLOT = [S_CMP, S_Q, S_Q + 1, S_KSEL, S_V, S_GATE, S_CA, S_CA + 1, S_CG, S_CG + 1, S_PO, S_PO + 1,
              S_MQ, S_MQ + 1, S_MK, S_MK + 1, S_MV, S_MV + 1]
N_IN_PANELS = len(PANEL_SLOT)
GATE_PANEL = PANEL_SLOT.index(S_GATE)
NGATE = 12
MIX_SLOT = [S_CA, S_CA + 1, S_Q, S_Q + 1, S_MQ, S_MQ + 1, S_PO, S_PO + 1]
OUT0 = N_IN_PANELS
FFN = []
for _kind, _g in (("up", 0), ("up", 1), ("down", 0), ("up", 2), ("down", 1), ("up", 3), ("down", 2), ("down", 3)):
    FFN += [(_kind, _g, _n) for _n in range(KT)]
FF0 = OUT0 + KT
N_PANELS = FF0 + len(FFN)
NRAW, NW = 3, 2
NCONSTS = 7

C_ID, C_CAUS, C_CMPM, C_COVER, C_DELTA, C_HM, C_INVC, C_INVW = 0, 128, 256, 380, 413, 421, 425, 457
NCONST = 459
V_DW, V_DWB, V_CG, V_CB, V_PS, V_G1, V_B1, V_G2, V_B2, V_POS, V_W2, V_PW, V_PO = (
    0, 62, 64, 66, 68, 70, 78, 86, 94, 102, 134, 198, 710)
NVEC = 966

UNITS = []
for _i in range(QT):
    for _h in range(H):
        UNITS += [("cmp", _h, _i), ("sel", _h, _i), ("win", _h, _i)]
    for _h in range(H):
        UNITS += [("moba", _h, _i)]
NU = len(UNITS)
GROUP = [(u // 16) * 8 + ((u % 16) // 3 if u % 16 < 12 else 4 + u % 16 - 12) for u in range(NU)]
NGROUP = GROUP[-1] + 1
FIRST = [u == 0 or GROUP[u] != GROUP[u - 1] for u in range(NU)]
LAST = [u == NU - 1 or GROUP[u] != GROUP[u + 1] for u in range(NU)]
MU = B * 4
TAPS = [(k, t) for k in range(CW) for t in range(2)]


def timeline():
    tl = [("load_panel", 0), ("load_x", 0), ("load_panel", 1), ("load_small", 0), ("load_panel", 2), ("load_nsa", 0)]
    tl += [("xsplit", k) for k in range(KT)]
    tl += [("split", 0)]

    def panel(i, mid=()):
        out = []
        if i + 1 < N_PANELS:
            out.append(("split", i + 1))
            if i + 1 + NRAW - 1 < N_PANELS:
                out.append(("load_panel", i + NRAW))
        out.append(("mm", i))
        out += list(mid)
        out.append(("evac", i))
        return out

    per = -(-len(TAPS) // 6)
    pending = []
    for i in range(N_IN_PANELS):
        tl += panel(i, pending)
        pending = [("kv", i - 3 + 1)] if 3 <= i < 11 else []
        if i == 0:
            tl.append(("cmpp", 0))
            pending = [("kv", 0)]
        if i == 2:
            tl.append(("qn", 0))
        if 3 <= i < 11:
            tl.append(("nsa", i - 3))
            if i < 10:
                tl.append(("load_nsa", i - 2))
        if i == 9:
            tl.append(("glu", 0))
        if i >= 10 and i < 16:
            tl.append(("taps", (per * (i - 10), min(per * (i - 9), len(TAPS)))))
        if i == 13:
            tl.append(("qm", 0))
    tl += [("load_post", 0), ("zrows", 0), ("out_z", 0)]
    side = [("pool", 0), ("pool", 1), ("cmean", 0), ("cvar", 0), ("cpw", 0), ("csc", 0), ("ctr", 0), ("cimp", 0), ("win", 0)]
    side += [("mu", u) for u in range(MU + 2)]
    side += [("stat", k) for k in range(3)] + [("comb", 0), ("back", 0)]
    side += [("spv", b) for b in range(B)] + [("mpv", 0), ("fin", 0)]
    n = len(side)
    done = 0
    for u in range(NU + 3):
        tl.append(("att", u))
        want = (u + 1) * n // (NU + 3)
        tl += side[done:want]
        done = want
    tl += side[done:]
    tl += [("load_x", 1)]
    tl += [("msplit", k) for k in range(KT)]
    for i in range(OUT0, FF0):
        tl += panel(i)
    tl += [("ln", 0)]
    for i in range(FF0, N_PANELS):
        tl += panel(i)
    tl += [("ln", 1)]
    return tl


TL = timeline()
ACC = [("mm", i) for i in range(N_IN_PANELS)] + [("pool", 0), ("pool", 1), ("cmean", 0), ("cvar", 0), ("cpw", 0), ("cpw", 1)]
NACC1 = len(ACC)
ACC += [("mm", i) for i in range(OUT0, FF0)] + [("lnm", 0), ("lnv", 0)]
ACC += [("mm", i) for i in range(FF0, N_PANELS)] + [("lnm", 1), ("lnv", 1)]
ACC_NO = {k: n for n, k in enumerate(ACC)}
def reader(key):
    kind, n = key
    if kind == "mm":
        if OUT0 <= n < FF0 or (n >= FF0 and FFN[n - FF0][0] == "down"):
            return 1
        return 0
    return {"pool": 0, "cmean": 1, "cvar": 0, "cpw": 0, "lnm": 1, "lnv": 0}[kind]


def nread(key):
    r = reader(key)
    return sum(reader(k) == r for k in ACC[:ACC_NO[key] + 1])


USES = [[], [], [], []]
for _s in [s for s in TL if s[0] in ("csc", "ctr", "cimp", "win", "mu", "stat", "back", "spv", "mpv", "fin")]:
    _k, _n = _s
    _banks = {"csc": (0,), "ctr": (1,), "cimp": (0, 2), "win": (0, 1), "back": (0, 1), "fin": (0, 1)}.get(_k, ())
    if _k == "mu":
        _banks = ((_n % 2,) if _n < MU else ()) + ((2,) if 1 <= _n <= MU else ()) + ((3,) if _n >= 2 else ())
    if _k == "stat":
        _banks = ((0, 1, 2, 3), (0, 1, 2), (0,))[_n]
    if _k == "spv":
        _banks = (0, 1, 2)
    if _k == "mpv":
        _banks = (2,)
    for _b in _banks:
        USES[_b].append(_s)


def nth(bank, step):
    return USES[bank].index(step)


def build(nc, a, o):
    ctx = ExitStack()
    with ctx:
        def sem(name):
            return ctx.enter_context(nc.semaphore(name))

        at = [16512]

        def place(name, shape, dt=F32, offset=None):
            size = 4
            for s in shape[1:]:
                size *= s
            if offset is None:
                offset = at[0]
                at[0] += (size + 31) // 32 * 32
            return nc.alloc_sbuf_tensor_at(name, shape, dt, offset=offset)

        o_xres = at[0]
        xres = place("xres", [P, KT, NT])
        o_op = at[0]
        opH = place("opH", [P, KT, NT], F32R)
        opL = place("opL", [P, KT, NT], F32R)
        raw = place("raw", [P, NRAW, KT * P])
        wH = place("wH", [P, NW, KT, P], F32R)
        wL = place("wL", [P, NW, KT, P], F32R)
        o_z = at[0]
        zT = place("zT", [P, NSLOT, NT])
        o_a = at[0]
        w1 = place("w1", [P, 32, P])
        nsa_ring = place("nsa_ring", [P, 2, PAGES, 192])
        o_m = at[0]
        moba_lo = place("moba_lo", [P, 2, 4, 512])
        winK = place("winK", [P, B, 256], F32, o_a)
        winV = place("winV", [P, B, 4, HD], F32, o_a + 8192)
        PB = place("PB", [P, 2, T], F32, o_a + 16384)
        PT = place("PT", [P, 2, T], F32, o_a + 16384 + 4096)
        moba_hi = place("moba_hi", [P, 2, 4, 512], F32, o_a + 24576)
        moba_ring = [moba_lo[:, 0], moba_lo[:, 1], moba_hi[:, 0], moba_hi[:, 1]]
        selV_lo = place("selV_lo", [P, 4, PAGES, HD], F32, o_m)
        selV_hi = place("selV_hi", [P, 4, PAGES, HD], F32, o_a + 24576)
        WB = place("WB", [B, 13, P], F32, o_a)
        hidH = [place(f"hidH{g}", [P, KT, NT], F32R, o_z + g * 2 * KT * NT * 4) for g in range(2)]
        hidL = [place(f"hidL{g}", [P, KT, NT], F32R, o_z + (2 * g + 1) * KT * NT * 4) for g in range(2)]
        o_after_hid = o_z + 4 * KT * NT * 4
        relu = place("relu", [P, 2, NT], F32, o_after_hid)
        hsq = place("hsq", [P, 2, NT], F32, o_after_hid + 2 * NT * 4)
        sqb = place("sqb", [P, 2, NT], F32, o_after_hid + 4 * NT * 4)
        rstd = place("rstd", [P, NT], F32, o_after_hid + 6 * NT * 4)
        zc = place("zc", [P, 2, CW - 1 + T], F32, o_m)
        sc = place("sc", [P, 2, B, CW], F32, o_m + 4352)
        yc = place("yc", [P, 2, NT], F32, o_m + 6336)
        pa = place("pa", [P, T], F32, o_m + 10496)
        pb = place("pb", [P, NT], F32, o_m + 12544)
        sp = place("sp", [P, 2, B, 16], F32, o_m + 14624)
        Psel = place("Psel", [P, B, 512], F32, o_xres)
        OM = place("OM", [P, MU, 256], F32, o_op)
        kcT = place("kcT", [HD, B, P])
        Pwin = place("Pwin", [P, B, P], F32, at[0] - 4096)
        Vn = place("Vn", [P, 3, QT, P])
        zs = place("zs", [B, 12, P])
        cst = place("cst", [P, NCONST])
        vec = place("vec", [P, NVEC])
        QNa = place("QNa", [P, B, 32])
        QNb = place("QNb", [P, B, 32])
        QM = place("QM", [P, 2, B, 32])
        vc = place("vc", [P, B, HD])
        kcp = place("kcp", [P, 32])
        vcp = place("vcp", [P, HD])
        xc = place("xc", [P, 16, 34], F32, o_a + 16384 + 12288)
        hu = place("hu", [P, 3, P])
        bias = place("bias", [P, 1])
        gT = place("gT", [P, QT, NGATE])
        Pc = place("Pc", [P, 2, P])
        PcT = place("PcT", [P, 2, P])
        PTm2 = place("PTm2", [P, 2, P], F32, o_z + 1024)
        PTs = place("PTs", [P, 2, 2, 8, H], F32, o_a + 7584)
        PTw = place("PTw", [P, 2, 4, H])
        st = place("st", [P, 256])
        ps_small = place("ps_small", [P, 32])
        mean1024 = place("mean1024", [P, P])
        mean256 = place("mean256", [P, P])
        zeros = place("zeros", [P, P], F32, o_a + 2560)
        onesc = place("onesc", [P, 2])
        epsc = onesc[:, 1:2]
        onesc = onesc[:, 0:1]
        Pm = place("Pm", [P, 2, P], F32, o_z)
        o_g = o_z + S_CG * NT * 4
        gdiag = place("gdiag", [B, B, 32], F32, o_g)
        wnew = place("wnew", [B, 3, B, H], F32, o_g + 1024)
        eb = place("eb", [B, 3, H, 55], F32, o_g + 1408)
        Wd = place("Wd", [P, B, 4, H], F32, o_a + 6656)
        Wt = place("Wt", [P, 13, B], F32, o_a + 7168)
        oc = place("oc", [P, 2, HD])
        On = place("On", [P, 2, HD], F32, o_a + 2048)
        Om = place("Om", [P, 2, 256], F32, o_a)
        sm = place("sm", [B, 376])
        page_ids = place("page_ids", [1, B * PAGES], I32)
        nmS, lS = st[:, 0:64].rearrange("p (b s) -> p b s", b=B), st[:, 64:128].rearrange("p (b s) -> p b s", b=B)
        nmW, lW = st[:, 128:136], st[:, 136:144]
        nmM, gM, lM = st[:, 144:176], st[:, 176:208], st[:, 208:240]
        nmC, lC = st[:, 240:242], st[:, 242:244]
        g0 = st[:, 244:246]
        ident = cst[:, C_ID:C_ID + P]
        stats = ([nmS[:, :, p] for p in range(8)] + [lS[:, :, p] for p in range(8)],
                 [nmW, lW] + [nmM.rearrange("p (b s) -> p s b", s=4)[:, k, :] for k in range(4)]
                 + [gM.rearrange("p (b s) -> p s b", s=4)[:, k, :] for k in range(4)],
                 [lM.rearrange("p (b s) -> p s b", s=4)[:, k, :] for k in range(4)])
        assert at[0] <= 229344, at[0]

        psum = ctx.enter_context(nc.psum_tensor("psum", [P, 8, 512], F32))

        def acc(key):
            p = ACC_NO[key] % 2
            return psum[:, 2 * p:2 * p + 2, :]

        def read(eng, key):
            eng.wait_ge(acc_read[reader(key)], nread(key))

        def bank_read(eng, k, step):
            eng.wait_ge(bfree[k], nth(k, step) + 1)

        raw_in = [sem(f"raw_in{i}") for i in range(NRAW)]
        x_in, small_in, w1_in, ids_in = sem("x_in"), sem("small_in"), sem("w1_in"), sem("ids_in")
        nsa_in = [sem(f"nsa_in{i}") for i in range(2)]
        moba_in = [sem(f"moba_in{i}") for i in range(4)]
        win_in, selv_in, state_in = sem("win_in"), sem("selv_in"), sem("state_in")
        out_state, out_z, out_y = sem("out_state"), sem("out_z"), sem("out_y")
        xh_done, xl_done = sem("xh_done"), sem("xl_done")
        h_done, l_done, mm_done = sem("h_done"), sem("l_done"), sem("mm_done")
        acc_read = [sem("acc_read_by_scalar"), sem("acc_read_by_vector")]
        const_done = sem("const_done")
        vch, ach, vtap, vln = sem("vector_chain"), sem("scalar_chain"), sem("tap_done"), sem("ln_scaled")
        xc_done, cmp_mm, cmp_t1, cmp_u, cmp_th, hid_done, kv_mm, kc_done = (
            sem("xc_done"), sem("cmp_mm"), sem("cmp_t1"), sem("cmp_u"), sem("cmp_th"), sem("hid_done"), sem("kv_mm"), sem("kc_done"))
        qn_done, qm_done = sem("qn_done"), sem("qm_done")
        ssel_mm, ssel_sub, ssel_exp = sem("ssel_mm"), sem("ssel_sub"), sem("ssel_exp")
        glu_done, conv_done = sem("glu_done"), sem("conv_done")
        zr_mm, zr_done, gate_t, gate_done = sem("zr_mm"), sem("zr_done"), sem("gate_t"), sem("gate_done")
        qk_done, max_done, exp_done, scaled, tr_done, pt_done, pv_done, o_done, r_done = (
            sem("qk_done"), sem("max_done"), sem("exp_done"), sem("scaled"), sem("tr_done"), sem("pt_done"),
            sem("pv_done"), sem("o_done"), sem("r_done"))
        pool_d, pool_mm, pool_done = sem("pool_d"), sem("pool_mm"), sem("pool_done")
        cm_mm, cd_done, csq_done, cv_mm, cstd, cn_done, cth, cact, cpw_mm, cpw_done = (
            sem("cm_mm"), sem("cd_done"), sem("csq_done"), sem("cv_mm"), sem("cstd"), sem("cn_done"), sem("cth"),
            sem("cact"), sem("cpw_mm"), sem("cpw_done"))
        bfree = [sem(f"bank_free{k}") for k in range(4)]
        csc_mm, csc_sub, csc_exp, csc_done, ctr_mm, ctr_done, cimp_mm, sel_done = (
            sem("csc_mm"), sem("csc_sub"), sem("csc_exp"), sem("csc_done"), sem("ctr_mm"), sem("ctr_done"),
            sem("cimp_mm"), sem("sel_done"))
        win_mm, win_sub, win_exp, win_l = sem("win_mm"), sem("win_sub"), sem("win_exp"), sem("win_l")
        ms_mm, mmax, mexp, mt_mm, mpt, mp_mm, om_done = (
            sem("ms_mm"), sem("mmax"), sem("mexp"), sem("mt_mm"), sem("mpt"), sem("mp_mm"), sem("om_done"))
        stat_mm, stat_done, comb_sub, comb_exp, wb_done, back_mm, back_done = (
            sem("stat_mm"), sem("stat_done"), sem("comb_sub"), sem("comb_exp"), sem("wb_done"), sem("back_mm"),
            sem("back_done"))
        pscaled, st_mm, spt, spt2, spv_mm, md_done, mpv_mm, fin_o, fin_mm, fin_done = (
            sem("pscaled"), sem("st_mm"), sem("spt"), sem("spt2"), sem("spv_mm"), sem("md_done"), sem("mpv_mm"),
            sem("fin_o"), sem("fin_mm"), sem("fin_done"))
        mixh, mixl = sem("mixh"), sem("mixl")
        xr_done = sem("xr_done")
        ln_mm, ln_d, ln_sq, lnv_mm, ln_std, ln_n, ln_h, ln_l = (
            sem("ln_mm"), sem("ln_d"), sem("ln_sq"), sem("lnv_mm"), sem("ln_std"), sem("ln_n"), sem("ln_h"), sem("ln_l"))
        relu_done, sq_done, hidh_done, hid_l_done = sem("relu_done"), sem("sq_done"), sem("hidh_done"), sem("hid_l_done")

        block = ctx.enter_context(nc.Block())

        @block.sync
        def _(sp_):
            def load_panel(i):
                if i >= NRAW:
                    sp_.wait_ge(l_done, i - NRAW + 1)
                dst = raw[:, i % NRAW, :]
                if i == GATE_PANEL:
                    sp_.dma_start(dst[:, 0:KT * NGATE], a["w_gate"]).then_inc(raw_in[i % NRAW], 16)
                else:
                    sp_.dma_start(dst, a["panels"][i - (i > GATE_PANEL)]).then_inc(raw_in[i % NRAW], 16)

            ids = {}

            def page(b, n):
                return sp_.value_load(page_ids[0:1, b * PAGES + n:b * PAGES + n + 1], min_val=0, max_val=NPOOL - 1)

            for kind, n in TL:
                if kind == "load_panel":
                    load_panel(n)
                elif kind == "load_x" and n == 0:
                    sp_.dma_start(xres[:, :, :], a["xT"]).then_inc(x_in, 16)
                elif kind == "load_small":
                    sp_.dma_start(page_ids[:, :], a["page_table"]).then_inc(ids_in, 16)
                    sp_.dma_start(cst[:, :], a["consts"]).then_inc(small_in, 16)
                    sp_.dma_start(vec[:, :], a["vecs"]).then_inc(small_in, 16)
                    sp_.dma_start(w1[:, :, :], a["w1"]).then_inc(w1_in, 16)
                    sp_.dma_start(sc[:, :, :, 0:CW - 1], a["state_convT"]).then_inc(state_in, 16)
                    sp_.dma_start(sp[:, :, :, 0:15], a["state_poolT"]).then_inc(state_in, 16)
                    sp_.dma_start(o["win_sample"][:, 0:T - 1, :], a["state_win"][:, 1:T, :]).then_inc(out_state, 16)
                    sp_.wait_ge(ids_in, 16)
                elif kind == "load_nsa":
                    if n == 1:
                        sp_.wait_ge(cmp_mm, 1)
                    if n >= 2:
                        sp_.wait_ge(ssel_mm, n - 1)
                    for p in range(PAGES):
                        v = page(n, p)
                        sp_.dma_start(nsa_ring[:, n % 2, p, :],
                                      a["nsa_pages"][bass.ds(v, 1)].rearrange("a p n -> (a p) n")).then_inc(nsa_in[n % 2], 16)
                elif kind == "load_post":
                    sp_.wait_ge(ssel_mm, B)
                    sp_.wait_ge(kc_done, B + 1)
                    sp_.dma_start(winK[:, :, :], a["winK"]).then_inc(win_in, 16)
                    sp_.dma_start(winV[:, :, :, :], a["winV"]).then_inc(win_in, 16)
                elif kind == "load_moba":
                    pass
                elif kind == "out_z":
                    read(sp_, ("mm", N_IN_PANELS - 1))
                    sp_.dma_start(o["z_cmp"], zT[:, S_CMP, :]).then_inc(out_z, 16)
                    sp_.dma_start(o["z_ksel"], zT[0:HD, S_KSEL, :]).then_inc(out_z, 16)
                    sp_.dma_start(o["z_kwin"], zT[0:HD, S_KWIN, :]).then_inc(out_z, 16)
                    sp_.dma_start(o["z_v"], zT[:, S_V, :]).then_inc(out_z, 16)
                    sp_.dma_start(o["z_moba"], zT[:, S_MK:S_MK + 4, :]).then_inc(out_z, 16)
                    sp_.dma_start(o["pool_prompt"], zT[:, S_PO:S_PO + 2, T - 15:T]).then_inc(out_z, 16)
                    sp_.wait_ge(glu_done, 2)
                    sp_.dma_start(o["conv_prompt"], zc[:, :, T:T + CW - 1]).then_inc(out_z, 16)
                    sp_.dma_start(o["conv_sample"], sc[:, :, :, 1:CW]).then_inc(out_z, 16)
                    sp_.wait_ge(pool_d, 1)
                    sp_.dma_start(o["pool_sample"], sp[:, :, :, 1:16]).then_inc(out_z, 16)
                    sp_.wait_ge(zr_done, 3)
                    sp_.dma_start(o["win_sample"][:, T - 1, 0:HD], zs[:, 3, 0:HD]).then_inc(out_z, 16)
                    sp_.dma_start(o["win_sample"][:, T - 1, HD:P], zs[:, 2, HD:P]).then_inc(out_z, 16)
                    sp_.wait_ge(out_z, 16 * 11)
                elif kind == "mu" and n < MU:
                    u = n
                    if u == 0:
                        sp_.wait_ge(cpw_mm, 2)
                        sp_.wait_ge(pool_mm, 2)
                        for q in range(3):
                            for p in range(4):
                                v = page(q // 4, q % 4 * 4 + p)
                                sp_.dma_start(moba_ring[q][:, p, :],
                                              a["moba_pages"][bass.ds(v, 1)].rearrange("a p n -> (a p) n")).then_inc(moba_in[q], 16)
                    q = u + 3
                    if q < MU:
                        if q >= 4:
                            sp_.wait_ge(mp_mm, q - 3)
                        for p in range(4):
                            v = page(q // 4, q % 4 * 4 + p)
                            sp_.dma_start(moba_ring[q % 4][:, p, :],
                                          a["moba_pages"][bass.ds(v, 1)].rearrange("a p n -> (a p) n")).then_inc(moba_in[q % 4], 16)
                elif kind == "stat" and n == 0:
                    sp_.wait_ge(mp_mm, MU)
                    for b in range(B):
                        dst = (selV_lo if b < 4 else selV_hi)[:, b % 4]
                        for p in range(PAGES):
                            v = page(b, p)
                            sp_.dma_start(dst[:, p, :],
                                          a["selv_pages"][bass.ds(v, 1)].rearrange("a p n -> (a p) n")).then_inc(selv_in, 16)
                elif kind == "load_x" and n == 1:
                    sp_.wait_ge(st_mm, B)
                    sp_.dma_start(xres[:, :, :], a["xT"]).then_inc(x_in, 16)
                elif kind == "ln" and n == 1:
                    for k in range(KT):
                        sp_.wait_ge(ln_n, KT + k + 1)
                        sp_.dma_start(o["y"][:, k, :], xres[:, k, :]).then_inc(out_y, 16)
            sp_.wait_ge(out_state, 16)
            sp_.wait_ge(out_z, 16 * 11)
            sp_.wait_ge(out_y, 16 * KT)

        @block.tensor
        def _(pe):
            mm = nc.tensor.matmul

            def acc_wait(key):
                n = ACC_NO[key]
                if n >= 2:
                    read(pe, ACC[n - 2])
                if n in (NACC1, NACC1 + 1):
                    for k in range(4):
                        pe.wait_ge(bfree[k], len(USES[k]))

            def panel(i):
                key = ("mm", i)
                acc_wait(key)
                out = acc(key)
                pe.wait_ge(l_done, i + 1)
                M = P
                if i < N_IN_PANELS:
                    xh, xl = opH, opL
                    if i == 0:
                        pe.wait_ge(xl_done, KT)
                    if i == GATE_PANEL:
                        M = NGATE
                elif i < FF0:
                    xh, xl = opH, opL
                    if i == OUT0:
                        pe.wait_ge(mixl, KT)
                else:
                    kind, g, n = FFN[i - FF0]
                    if kind == "up":
                        xh, xl = opH, opL
                        if i == FF0:
                            pe.wait_ge(ln_l, KT)
                    else:
                        xh, xl = hidH[g % 2], hidL[g % 2]
                        pe.wait_ge(hid_l_done, (g + 1) * KT)
                s = i % NW
                for k in range(KT):
                    if M == P:
                        a_h, a_l = wH[:, s, k, :], wL[:, s, k, :]
                    else:
                        a_h = wH[:, s].rearrange("p a b -> p (a b)")[:, k * NGATE:(k + 1) * NGATE]
                        a_l = wL[:, s].rearrange("p a b -> p (a b)")[:, k * NGATE:(k + 1) * NGATE]
                    for j, (w, x) in enumerate(((a_h, xh), (a_h, xl), (a_l, xh))):
                        for hf in range(2):
                            last = mm(out[0:M, hf, 0:HALF], w, x[:, k, hf * HALF:(hf + 1) * HALF],
                                      start=(k == 0 and j == 0), stop=(k == KT - 1 and j == 2))
                last.then_inc(mm_done, 1)

            def compress(rhs0, rhs1, n0, n1):
                for half, rhs, n in ((0, rhs0, n0), (1, rhs1, n1)):
                    for r in range(16):
                        last = mm(psum[:, 4, half * 256:half * 256 + n], w1[:, half * 16 + r, :], rhs(r),
                                  start=(r == 0), stop=(r == 15))
                last.then_inc(cmp_mm, 1)

            def cmp_kv(idx, n):
                pe.wait_ge(hid_done, idx + 1)
                if idx:
                    pe.wait_ge(kc_done, idx)
                mm(psum[0:HD, 5, 0:n], vec[0:HD, V_W2:V_W2 + HD], hu[0:HD, 0, 0:n], start=True, stop=True)
                mm(psum[0:n, 5, 256:256 + HD], hu[HD:P, 0, 0:n], vec[HD:P, V_W2:V_W2 + HD], start=True, stop=True).then_inc(kv_mm, 1)

            def sel_scores(b):
                if b >= 2:
                    pe.wait_ge(ssel_sub, b - 1)
                for j in range(4):
                    half, pg = j // 2, j % 2
                    last = mm(psum[32 * j:32 * j + 32, 6 + b % 2, :], (QNa, QNb)[half][:, b, :],
                              nsa_ring[:, b % 2, pg * 8:pg * 8 + 8, P:192], start=True, stop=True, skip_group_check=True)
                last.then_inc(ssel_mm, 1)

            def qk(u):
                kind, h, i = UNITS[u]
                if u >= 2:
                    pe.wait_ge(exp_done, u - 1)
                base = HD * (h % 2)
                n = NCMP_P if kind == "cmp" else P * (i + 1)
                if kind == "moba":
                    q, k = zT[base:base + HD, S_MQ + h // 2, i * P:(i + 1) * P], zT[base:base + HD, S_MK + h // 2, 0:n]
                else:
                    q = zT[base:base + HD, S_Q + h // 2, i * P:(i + 1) * P]
                    k = kcp[base:base + HD, 0:n] if kind == "cmp" else zT[base:base + HD, S_KSEL if kind == "sel" else S_KWIN, 0:n]
                mm(psum[:, 4 + u % 2, 0:n], q, k, start=True, stop=True).then_inc(qk_done, 1)

            def tr(u):
                kind, h, i = UNITS[u]
                pe.wait_ge(scaled, u + 1)
                if u:
                    pe.wait_ge(pt_done, u)
                if kind == "cmp":
                    nc.tensor.transpose(psum[0:NCMP_P, 6, 0:P], PB[:, u % 2, 0:NCMP_P], ident).then_inc(tr_done, 1)
                    return
                for j in range(i + 1):
                    last = nc.tensor.transpose(psum[:, 6, j * P:(j + 1) * P], PB[:, u % 2, j * P:(j + 1) * P], ident)
                last.then_inc(tr_done, 1)

            def pv(u):
                kind, h, i = UNITS[u]
                pe.wait_ge(pt_done, u + 1)
                g = GROUP[u]
                if FIRST[u] and g >= 2:
                    pe.wait_ge(o_done, g - 1)
                base = HD * (h % 2)
                out = psum[base:base + HD, 7, 0:P]
                if kind == "cmp":
                    last = mm(out, vcp[0:NCMP_P, :], PT[0:NCMP_P, u % 2, 0:P], start=True, stop=False, skip_group_check=True)
                else:
                    src, off = {"sel": (0, 0), "win": (0, HD), "moba": (1 + h // 2, base)}[kind]
                    for j in range(i + 1):
                        last = mm(out, Vn[:, src, j, off:off + HD], PT[:, u % 2, j * P:(j + 1) * P],
                                  start=(FIRST[u] and j == 0), stop=(LAST[u] and j == i), skip_group_check=True)
                last.then_inc(pv_done, 1)

            def bank(k, step):
                n = nth(k, step)
                if n:
                    pe.wait_ge(bfree[k], n)

            for step in TL:
                kind, n = step
                if kind == "mm":
                    panel(n)
                elif kind == "cmpp":
                    pe.wait_ge(xc_done, 1)
                    pe.wait_ge(w1_in, 16)
                    compress(lambda r: xc[:, r, :], lambda r: xc[:, r, :], 34, 34)
                elif kind == "kv":
                    cmp_kv(n, NCMP if n else NCMP_P)
                elif kind == "nsa":
                    pe.wait_ge(nsa_in[n % 2], 16 * PAGES * (n // 2 + 1))
                    pe.wait_ge(cmp_u, n + 1)
                    rhs = lambda r: nsa_ring[:, n % 2, :, r * 8:r * 8 + 8]
                    compress(rhs, rhs, NCHUNK, NCHUNK)
                    if n == 0:
                        pe.wait_ge(qn_done, 1)
                    sel_scores(n)
                elif kind == "zrows":
                    read(pe, ("mm", N_IN_PANELS - 1))
                    pe.wait_ge(const_done, NCONSTS)
                    pe.wait_ge(ssel_sub, B)
                    pe.wait_ge(kc_done, B + 1)
                    pe.wait_ge(cmp_u, B + 1)
                    for j, slot in enumerate((S_GATE, S_KSEL, S_V, S_KWIN, S_Q, S_Q + 1, S_MQ, S_MQ + 1, S_MK, S_MK + 1, S_MV, S_MV + 1)):
                        m = NGATE if j == 0 else P
                        last = nc.tensor.transpose(psum[0:B, 5 + j // 4, j % 4 * P:j % 4 * P + m], zT[0:m, slot, T:NT], ident[0:m, 0:m])
                    last.then_inc(zr_mm, 1)
                    for src, slot in enumerate((S_V, S_MV, S_MV + 1)):
                        pe.wait_ge(zr_done, src + 1)
                        for t in range(QT):
                            last = nc.tensor.transpose(psum[:, 5 + src, t * P:(t + 1) * P], zT[:, slot, t * P:(t + 1) * P], ident)
                        last.then_inc(zr_mm, 1)
                    for t in range(QT):
                        last = nc.tensor.transpose(psum[:, 4, t * NGATE:(t + 1) * NGATE], zT[0:NGATE, S_GATE, t * P:(t + 1) * P], ident[0:NGATE, 0:NGATE])
                    last.then_inc(zr_mm, 1)
                    pe.wait_ge(gate_t, 1)
                    pe.wait_ge(zr_done, 6)
                elif kind == "att":
                    if n < NU:
                        qk(n)
                    if 2 <= n < NU + 2:
                        tr(n - 2)
                    if n >= 3:
                        pv(n - 3)
                elif kind == "pool":
                    acc_wait(step)
                    pe.wait_ge(pool_d, n + 1)
                    for hf in range(2):
                        last = mm(acc(step)[:, hf, 0:HALF], vec[:, V_PO + n * P:V_PO + (n + 1) * P], pb[:, hf * HALF:(hf + 1) * HALF],
                                  start=True, stop=True)
                    last.then_inc(pool_mm, 1)
                elif kind in ("cmean", "cvar"):
                    acc_wait(step)
                    if kind == "cmean":
                        pe.wait_ge(conv_done, 1)
                    else:
                        pe.wait_ge(csq_done, 1)
                    for hf in range(2):
                        for t in range(2):
                            x = yc[:, t, hf * HALF:(hf + 1) * HALF] if kind == "cmean" else zT[:, S_CG + t, hf * HALF:(hf + 1) * HALF]
                            last = mm(acc(step)[:, hf, 0:HALF], mean256[:, :], x, start=(t == 0), stop=(t == 1))
                    last.then_inc(cm_mm if kind == "cmean" else cv_mm, 1)
                elif kind == "cpw":
                    pe.wait_ge(cact, 1)
                    for m in range(2):
                        acc_wait(("cpw", m))
                        for hf in range(2):
                            for t in range(2):
                                last = mm(acc(("cpw", m))[:, hf, 0:HALF], vec[:, V_PW + t * 256 + m * P:V_PW + t * 256 + (m + 1) * P],
                                          yc[:, t, hf * HALF:(hf + 1) * HALF], start=(t == 0), stop=(t == 1))
                        last.then_inc(cpw_mm, 1)
                elif kind == "csc":
                    read(pe, ACC[NACC1 - 1])
                    read(pe, ACC[NACC1 - 2])
                    bank(0, step)
                    for b in range(B):
                        last = mm(psum[32 * (b % 4):32 * (b % 4) + 32, 0, b // 4 * P:b // 4 * P + NCMP], QNa[0:HD, b, :],
                                  kcT[:, b, 0:NCMP], start=True, stop=True, skip_group_check=True)
                    last.then_inc(csc_mm, 1)
                elif kind == "ctr":
                    bank(1, step)
                    pe.wait_ge(csc_done, 1)
                    for c in range(2):
                        last = nc.tensor.transpose(psum[0:NCMP, 1, c * P:(c + 1) * P], Pc[:, c, 0:NCMP], ident)
                    last.then_inc(ctr_mm, 1)
                elif kind == "cimp":
                    bank(0, step)
                    bank(2, step)
                    pe.wait_ge(ctr_done, 1)
                    mm(psum[0:B, 0, 0:NSELB], ps_small[0:NCMP, 16:16 + B], cst[0:NCMP, C_COVER:C_COVER + NSELB], start=True, stop=True)
                    for b in range(B):
                        c, j = b // 4, b % 4
                        last = mm(psum[32 * j:32 * j + 32, 2, c * HD:(c + 1) * HD], PcT[0:NCMP, c, 32 * j:32 * j + 32],
                                  vc[0:NCMP, b, :], start=True, stop=True, skip_group_check=True)
                    last.then_inc(cimp_mm, 1)
                elif kind == "win":
                    bank(0, step)
                    bank(1, step)
                    pe.wait_ge(win_in, 32)
                    for b in range(B):
                        for j in range(4):
                            half, g = j // 2, j % 2
                            last = mm(psum[32 * j:32 * j + 32, b // 4, b % 4 * P:(b % 4 + 1) * P], (QNa, QNb)[half][:, b, :],
                                      winK[:, b, g * P:(g + 1) * P], start=True, stop=True, skip_group_check=True)
                    last.then_inc(win_mm, 1)
                elif kind == "mu":
                    u = n
                    if u < MU:
                        bank(u % 2, step)
                        pe.wait_ge(moba_in[u % 4], 64 * (u // 4 + 1))
                        if u == 0:
                            pe.wait_ge(qm_done, 1)
                        for hp in range(2):
                            for j in range(4):
                                last = mm(psum[32 * j:32 * j + 32, u % 2, 0:P], QM[:, hp, u // 4, :],
                                          moba_ring[u % 4][:, j, hp * P:(hp + 1) * P], start=(hp == 0), stop=(hp == 1),
                                          skip_group_check=True)
                        last.then_inc(ms_mm, 1)
                    if 1 <= u <= MU:
                        bank(2, step)
                        bank_read(pe, (u - 1) % 2, ("mu", u - 1))
                        nc.tensor.transpose(psum[:, 2, 0:P], Pm[:, (u - 1) % 2, :], ident).then_inc(mt_mm, 1)
                    if u >= 2:
                        v = u - 2
                        bank(3, step)
                        bank_read(pe, 2, ("mu", v + 1))
                        for j in range(4):
                            last = mm(psum[32 * j:32 * j + 32, 3, 0:256], PTm2[:, v % 2, 32 * j:32 * j + 32],
                                      moba_ring[v % 4][:, j, 256:512], start=True, stop=True, skip_group_check=True)
                        last.then_inc(mp_mm, 1)
                elif kind == "stat":
                    for k in ((0, 1, 2, 3), (0, 1, 2), (0,))[n]:
                        bank(k, step)
                    if n == 0:
                        pe.wait_ge(bfree[3], MU)
                        pe.wait_ge(win_l, 1)
                    for s, src in enumerate(stats[n]):
                        last = nc.tensor.transpose(psum[0:B, s // 4, s % 4 * P:(s % 4 + 1) * P], src, ident)
                    last.then_inc(stat_mm, 1)
                elif kind == "back":
                    bank(0, step)
                    bank(1, step)
                    pe.wait_ge(wb_done, 1)
                    for s in range(13):
                        nc.tensor.transpose(psum[:, 0, s * B:(s + 1) * B], WB[:, s, :], ident[0:B, 0:B])
                    for c in range(2):
                        last = mm(psum[:, 1, c:c + 1], gdiag[:, 4 * c:4 * c + 4, :], onesc[0:B, :], start=True, stop=True)
                    last.then_inc(back_mm, 1)
                elif kind == "spv":
                    b = n
                    for k in range(3):
                        bank(k, step)
                    pe.wait_ge(pscaled, 1)
                    for p in range(8):
                        nc.tensor.transpose(psum[0:HD, p // 4, p % 4 * P:(p % 4 + 1) * P], Psel[:, b, p * HD:(p + 1) * HD], ident)
                    nc.tensor.transpose(psum[:, 2, 0:P], Pwin[:, b, :], ident).then_inc(st_mm, 1)
                    if b == 0:
                        pe.wait_ge(bfree[3], len(USES[3]))
                        mm(psum[:, 3, 0:P], zeros[:, :], ident, start=True, stop=False, skip_group_check=True)
                        pe.wait_ge(selv_in, 16 * PAGES * B)
                    c, j = b // 4, b % 4
                    out = psum[32 * j:32 * j + H, 3, c * HD:(c + 1) * HD]
                    V = (selV_lo if b < 4 else selV_hi)[:, b % 4]
                    for k in range(3):
                        bank_read(pe, k, step)
                    for p in range(PAGES):
                        mm(out, PTs[:, b % 2, p // 8, p % 8, :], V[:, p, :], start=False, stop=False, skip_group_check=True)
                    for w in range(4):
                        mm(out, PTw[:, b % 2, w, :], winV[:, b, w, :], start=False, stop=False, skip_group_check=True)
                    mm(out, wnew[:, 0, b, :], zs[:, 2, 0:HD], start=False, stop=False, skip_group_check=True)
                    mm(out, wnew[:, 2, b, :], zs[:, 2, HD:P], start=False, stop=(b == B - 1), skip_group_check=True).then_inc(spv_mm, 1)
                elif kind == "mpv":
                    bank(2, step)
                    pe.wait_ge(md_done, 1)
                    mm(psum[:, 2, :], zeros[:, :], OM[:, 0:2, :], start=True, stop=False, skip_group_check=True)
                    for pos in range(4):
                        for b in range(B):
                            c, j = b // 4, b % 4
                            mm(psum[32 * j:32 * j + H, 2, c * 256:(c + 1) * 256], Wd[:, b, pos, :], OM[:, b * 4 + pos, :],
                               start=False, stop=False, skip_group_check=True)
                    for b in range(B):
                        c, j = b // 4, b % 4
                        last = mm(psum[32 * j:32 * j + H, 2, c * 256:(c + 1) * 256], wnew[:, 1, b, :], zs[:, 10:12, :],
                                  start=False, stop=(b == B - 1), skip_group_check=True)
                    last.then_inc(mpv_mm, 1)
                elif kind == "fin":
                    bank(0, step)
                    bank(1, step)
                    pe.wait_ge(fin_o, 1)
                    bank_read(pe, 2, ("mpv", 0))
                    for c in range(2):
                        nc.tensor.transpose(psum[0:HD, 0, c * P:(c + 1) * P], On[:, c, :], ident)
                        for hp in range(2):
                            last = nc.tensor.transpose(psum[:, 1, (c * 2 + hp) * P:(c * 2 + hp + 1) * P], Om[:, c, hp * P:(hp + 1) * P], ident)
                    last.then_inc(fin_mm, 1)
                elif kind == "ln":
                    read(pe, ("mm", FF0 - 1 if n == 0 else N_PANELS - 1))
                    acc_wait(("lnm", n))
                    for hf in range(2):
                        for k in range(KT):
                            last = mm(acc(("lnm", n))[:, hf, 0:HALF], mean1024[:, :], xres[:, k, hf * HALF:(hf + 1) * HALF],
                                      start=(k == 0), stop=(k == KT - 1))
                    last.then_inc(ln_mm, 1)
                    acc_wait(("lnv", n))
                    for k in range(KT):
                        pe.wait_ge(ln_sq, n * KT + k + 1)
                        for hf in range(2):
                            last = mm(acc(("lnv", n))[:, hf, 0:HALF], mean1024[:, :], sqb[:, k % 2, hf * HALF:(hf + 1) * HALF],
                                      start=(k == 0), stop=(k == KT - 1))
                        last.then_inc(lnv_mm, 1)

        @block.scalar
        def _(act):
            fn = nc.scalar.activation
            steps = [0]

            def chain(ins):
                steps[0] += 1
                ins.then_inc(ach, 1)
                act.wait_ge(ach, steps[0])

            def zview(ap):
                return ap.rearrange("p (a b) -> p a b", a=2)

            up_no = 0
            for step in TL:
                kind, n = step
                if kind == "xsplit":
                    if n == 0:
                        act.wait_ge(x_in, 16)
                    fn(opH[:, n, :], xres[:, n, :], ACT.Copy).then_inc(xh_done, 1)
                elif kind == "split":
                    act.wait_ge(raw_in[n % NRAW], 16 * (n // NRAW + 1))
                    if n >= NW:
                        act.wait_ge(mm_done, n - NW + 1)
                    m = KT * (NGATE if n == GATE_PANEL else P)
                    fn(wH[:, n % NW].rearrange("p a b -> p (a b)")[:, 0:m], raw[:, n % NRAW, 0:m], ACT.Copy).then_inc(h_done, 1)
                elif kind == "evac" and n < N_IN_PANELS:
                    act.wait_ge(mm_done, n + 1)
                    slot, src = PANEL_SLOT[n], acc(("mm", n))[:, :, 0:HALF]
                    if slot in (S_Q, S_Q + 1, S_MQ, S_MQ + 1):
                        last = fn(zview(zT[:, slot, :]), src, ACT.Copy, scale=HD ** -0.5)
                    elif slot in (S_CA, S_CA + 1):
                        last = fn(zview(zT[:, slot, :]), src, ACT.Copy, scale=0.5)
                    elif slot in (S_CG, S_CG + 1):
                        last = fn(zview(zT[:, slot, :]), src, ACT.Tanh, scale=0.5)
                    elif slot == S_GATE:
                        last = fn(zview(zT[0:NGATE, slot, :]), src[0:NGATE], ACT.Copy)
                    elif slot == S_KSEL:
                        for lo in (0, HD):
                            fn(zview(zT[lo:lo + HD, S_KSEL, :]), src[0:HD], ACT.Copy)
                            last = fn(zview(zT[lo:lo + HD, S_KWIN, :]), src[HD:P], ACT.Copy)
                    else:
                        last = fn(zview(zT[:, slot, :]), src, ACT.Copy)
                    last.then_inc(acc_read[0], 1)
                elif kind in ("cmpp", "nsa"):
                    idx = 0 if kind == "cmpp" else n + 1
                    m = NCMP if idx else NCMP_P
                    act.wait_ge(cmp_mm, idx + 1)
                    if idx == 0:
                        act.wait_ge(small_in, 32)
                        chain(fn(hu[:, 2, 0:1], psum[:, 4, 32:33], ACT.Copy))
                        chain(fn(bias[:, :], psum[:, 4, 256 + 33:256 + 34], ACT.Identity, bias=hu[:, 2, 0:1]))
                    else:
                        act.wait_ge(hid_done, idx)
                    fn(hu[:, 1, 0:m], psum[:, 4, 257:257 + m], ACT.Identity, bias=bias[:, :]).then_inc(cmp_t1, 1)
                    act.wait_ge(cmp_u, idx + 1)
                    fn(hu[:, 1, 0:m], hu[:, 2, 0:m], ACT.Tanh, scale=0.5).then_inc(cmp_th, 1)
                    if kind == "nsa":
                        act.wait_ge(ssel_sub, n + 1)
                        fn(Psel[:, n, :], Psel[:, n, :], ACT.Exp).then_inc(ssel_exp, 1)
                elif kind == "kv":
                    act.wait_ge(kv_mm, n + 1)
                    if n == 0:
                        fn(kcp[0:HD, 0:NCMP_P], psum[0:HD, 5, 0:NCMP_P], ACT.Copy, scale=0.5)
                        fn(kcp[HD:P, 0:NCMP_P], psum[0:HD, 5, 0:NCMP_P], ACT.Copy, scale=0.5)
                        fn(vcp[0:NCMP_P, :], psum[0:NCMP_P, 5, 256:256 + HD], ACT.Copy, scale=0.5).then_inc(kc_done, 1)
                    else:
                        fn(kcT[:, n - 1, 0:NCMP], psum[0:HD, 5, 0:NCMP], ACT.Copy, scale=0.5)
                        fn(vc[0:NCMP, n - 1, :], psum[0:NCMP, 5, 256:256 + HD], ACT.Copy, scale=0.5).then_inc(kc_done, 1)
                elif kind == "zrows":
                    act.wait_ge(zr_mm, 1)
                    fn(zs[:, 0, 0:NGATE], psum[0:B, 5, 0:NGATE], ACT.Copy)
                    fn(zs[:, 1:4, :], psum[0:B, 5, P:512].rearrange("p (a b) -> p a b", a=3), ACT.Copy).then_inc(zr_done, 1)
                    for j in (1, 2):
                        fn(zs[:, 4 * j:4 * j + 4, :], psum[0:B, 5 + j, :].rearrange("p (a b) -> p a b", a=4), ACT.Copy).then_inc(zr_done, 1)
                    for src in range(3):
                        act.wait_ge(zr_mm, src + 2)
                        fn(Vn[:, src, :, :], psum[:, 5 + src, :].rearrange("p (a b) -> p a b", a=QT), ACT.Copy).then_inc(zr_done, 1)
                    act.wait_ge(zr_mm, 5)
                    fn(gT[:, :, :], psum[:, 4, 0:QT * NGATE].rearrange("p (a b) -> p a b", a=QT), ACT.Tanh, scale=0.5).then_inc(gate_t, 1)
                elif kind == "att":
                    if n < NU:
                        u = n
                        ukind, h, i = UNITS[u]
                        m = NCMP_P if ukind == "cmp" else P * (i + 1)
                        act.wait_ge(max_done, u + 1)
                        if u >= 2:
                            act.wait_ge(tr_done, u - 1)
                            act.wait_ge(r_done, u - 1)
                        fn(PB[:, u % 2, 0:m], psum[:, 4 + u % 2, 0:m], ACT.Exp, bias=ps_small[:, u % 2:u % 2 + 1],
                           accum_out=ps_small[:, 4 + u % 2:5 + u % 2]).then_inc(exp_done, 1)
                    if 2 <= n < NU + 2:
                        u = n - 2
                        ukind, h, i = UNITS[u]
                        act.wait_ge(tr_done, u + 1)
                        if u >= 2:
                            act.wait_ge(pv_done, u - 1)
                        if ukind == "cmp":
                            fn(PT[0:NCMP_P, u % 2, 0:P], psum[0:NCMP_P, 6, 0:P], ACT.Copy).then_inc(pt_done, 1)
                        else:
                            fn(PT[:, u % 2, 0:P * (i + 1)], psum[:, 6, 0:P * (i + 1)], ACT.Copy).then_inc(pt_done, 1)
                    if n >= 3 and LAST[n - 3]:
                        u = n - 3
                        ukind, h, i = UNITS[u]
                        base = HD * (h % 2)
                        slot = (S_MQ if ukind == "moba" else S_Q) + h // 2
                        act.wait_ge(pv_done, u + 1)
                        fn(zT[base:base + HD, slot, i * P:(i + 1) * P], psum[base:base + HD, 7, 0:P], ACT.Copy).then_inc(o_done, 1)
                elif kind == "pool":
                    act.wait_ge(pool_mm, n + 1)
                    act.wait_ge(out_z, 16 * 11)
                    fn(zview(zT[:, S_PO + n, :]), acc(step)[:, :, 0:HALF], ACT.Copy, scale=vec[:, V_PS + n:V_PS + n + 1]).then_inc(acc_read[0], 1)
                elif kind == "cmean":
                    read(act, step)
                    for t in range(2):
                        last = fn(zT[:, S_CG + t, :], yc[:, t, :], ACT.Square)
                    last.then_inc(csq_done, 1)
                elif kind == "cvar":
                    act.wait_ge(cv_mm, 1)
                    act.wait_ge(const_done, NCONSTS)
                    fn(zview(zT[:, S_CG, :]), acc(step)[:, :, 0:HALF], ACT.Sqrt, bias=epsc).then_inc(acc_read[0], 1)
                    act.wait_ge(cn_done, 1)
                    fn(zT[:, S_CG:S_CG + 2, :], yc[:, :, :], ACT.Tanh, scale=0.5).then_inc(cth, 1)
                elif kind == "cpw":
                    for m in range(2):
                        act.wait_ge(cpw_mm, m + 1)
                        fn(zview(zT[:, S_CA + m, :]), acc(("cpw", m))[:, :, 0:HALF], ACT.Copy, scale=0.5).then_inc(acc_read[0], 1)
                elif kind == "csc":
                    bank_read(act, 0, step)
                    fn(Pc[:, :, 0:NCMP], Pc[:, :, 0:NCMP], ACT.Exp).then_inc(csc_exp, 1)
                elif kind == "cimp":
                    act.wait_ge(cimp_mm, 1)
                    fn(oc[:, :, :], psum[:, 2, 0:P].rearrange("p (a b) -> p a b", a=2), ACT.Copy).then_inc(bfree[2], 1)
                elif kind == "win":
                    bank_read(act, 0, step)
                    bank_read(act, 1, step)
                    fn(Pwin[:, :, :], Pwin[:, :, :], ACT.Exp).then_inc(win_exp, 1)
                elif kind == "mu":
                    u = n
                    if u < MU:
                        act.wait_ge(mmax, u + 1)
                        if u >= 2:
                            act.wait_ge(mt_mm, u - 1)
                        fn(Pm[:, u % 2, :], psum[:, u % 2, 0:P], ACT.Exp, bias=nmM[:, u:u + 1],
                           accum_out=lM[:, u:u + 1]).then_inc(bfree[u % 2], 1)
                    if u >= 2:
                        act.wait_ge(mp_mm, u - 1)
                        fn(OM[:, u - 2, :], psum[:, 3, 0:256], ACT.Copy).then_inc(bfree[3], 1)
                elif kind == "comb":
                    act.wait_ge(comb_sub, 1)
                    fn(sm[:, 0:NGATE], zs[:, 0, 0:NGATE], ACT.Tanh, scale=0.5)
                    fn(eb[:, 2].rearrange("p h s -> p (h s)"), eb[:, 2].rearrange("p h s -> p (h s)"), ACT.Exp).then_inc(comb_exp, 1)
                elif kind == "back":
                    act.wait_ge(back_mm, 1)
                    fn(Wt[:, :, :], psum[:, 0, 0:13 * B].rearrange("p (s b) -> p s b", b=B), ACT.Copy).then_inc(bfree[0], 1)
                    fn(g0, psum[:, 1, 0:2], ACT.Copy).then_inc(bfree[1], 1)
                elif kind == "spv":
                    act.wait_ge(st_mm, n + 1)
                    if n >= 2:
                        act.wait_ge(spv_mm, n - 1)
                    fn(PTw[:, n % 2, :, :], psum[:, 2, 0:P].rearrange("p (j h) -> p j h", j=4)[:, :, 0:H], ACT.Copy).then_inc(bfree[2], 1)
                elif kind == "mpv":
                    act.wait_ge(mpv_mm, 1)
                    fn(Om[:, :, :], psum[:, 2, :].rearrange("p (c x) -> p c x", c=2), ACT.Copy).then_inc(bfree[2], 1)
                elif kind == "fin":
                    act.wait_ge(fin_mm, 1)
                    for h in range(H):
                        base = HD * (h % 2)
                        last = fn(zT[base:base + HD, S_Q + h // 2, T:NT],
                                  psum[0:HD, 0, 0:256].rearrange("p (b x) -> p b x", x=32)[:, :, h], ACT.Copy)
                    last.then_inc(bfree[0], 1)
                elif kind == "msplit":
                    if n == 0:
                        act.wait_ge(o_done, NGROUP)
                        read(act, ACC[NACC1 - 1])
                        bank_read(act, 0, ("fin", 0))
                        bank_read(act, 1, ("fin", 0))
                    fn(opH[:, n, :], zT[:, MIX_SLOT[n], :], ACT.Copy).then_inc(mixh, 1)
                elif kind == "evac" and n >= FF0 and FFN[n - FF0][0] == "up":
                    g, m = FFN[n - FF0][1:]
                    act.wait_ge(mm_done, n + 1)
                    if up_no >= 2:
                        act.wait_ge(hid_l_done, up_no - 1)
                    chain_to = nread(("mm", n))
                    fn(zview(relu[:, up_no % 2, :]), acc(("mm", n))[:, :, 0:HALF], ACT.Relu).then_inc(acc_read[0], 1)
                    act.wait_ge(acc_read[0], chain_to)
                    if m == 0 and g >= 2:
                        act.wait_ge(mm_done, FF0 + FFN.index(("down", g - 2, KT - 1)) + 1)
                    fn(hidH[g % 2][:, m, :], relu[:, up_no % 2, :], ACT.Square).then_inc(hidh_done, 1)
                    up_no += 1
                elif kind == "ln":
                    for k in range(KT):
                        if k < KT - 1:
                            act.wait_ge(ln_d, n * (KT - 1) + k + 1)
                        else:
                            read(act, ("lnm", n))
                        if k >= 2:
                            act.wait_ge(lnv_mm, n * KT + k - 1)
                        fn(sqb[:, k % 2, :], xres[:, k, :], ACT.Square).then_inc(ln_sq, 1)
                    act.wait_ge(lnv_mm, (n + 1) * KT)
                    fn(zview(rstd[:, :]), acc(("lnv", n))[:, :, 0:HALF], ACT.Sqrt, bias=epsc).then_inc(acc_read[0], 1)
                    if n == 0:
                        for k in range(KT):
                            act.wait_ge(ln_n, k + 1)
                            fn(opH[:, k, :], xres[:, k, :], ACT.Copy).then_inc(ln_h, 1)

        @block.gpsimd
        def _(pool):
            for buf, value in ((mean1024[:, :], 1.0 / D), (mean256[:, :], 1.0 / 256), (onesc, 1.0), (epsc, EPS),
                               (QNa[:, :, :], 0.0), (QNb[:, :, :], 0.0), (QM[:, :, :, :], 0.0)):
                nc.gpsimd.memset(buf, value).then_inc(const_done, 1)
            up_no = 0
            for kind, n in TL:
                if kind == "att" and 1 <= n <= NU:
                    u = n - 1
                    ukind, h, i = UNITS[u]
                    m = NCMP_P if ukind == "cmp" else P * (i + 1)
                    pool.wait_ge(r_done, u + 1)
                    nc.gpsimd.tensor_scalar(PB[:, u % 2, 0:m], PB[:, u % 2, 0:m], ps_small[:, 8 + u % 2:9 + u % 2], None, ALU.mult).then_inc(scaled, 1)
                elif kind == "evac" and n >= FF0 and FFN[n - FF0][0] == "up":
                    read(pool, ("mm", n))
                    if up_no >= 2:
                        pool.wait_ge(hid_l_done, up_no - 1)
                    nc.gpsimd.tensor_tensor(hsq[:, up_no % 2, :], relu[:, up_no % 2, :], relu[:, up_no % 2, :], ALU.mult).then_inc(sq_done, 1)
                    up_no += 1

        @block.vector
        def _(dve):
            tt, ts, stt, red = nc.vector.tensor_tensor, nc.vector.tensor_scalar, nc.vector.scalar_tensor_tensor, nc.vector.tensor_reduce
            steps = [0]

            def chain(ins):
                steps[0] += 1
                ins.then_inc(vch, 1)
                dve.wait_ge(vch, steps[0])

            def zview(ap):
                return ap.rearrange("p (a b) -> p a b", a=2)

            def spread(ap, m):
                return ap.unsqueeze(len(ap.shape)).to_broadcast(list(ap.shape) + [m])

            def spread_at(ap, axis, m):
                shape = list(ap.shape)
                return ap.unsqueeze(axis).to_broadcast(shape[:axis] + [m] + shape[axis:])

            up_no = 0
            taps = 0
            for step in TL:
                kind, n = step
                if kind == "xsplit":
                    dve.wait_ge(xh_done, n + 1)
                    tt(opL[:, n, :], xres[:, n, :], opH[:, n, :].bitcast(F32), ALU.subtract).then_inc(xl_done, 1)
                elif kind == "split":
                    dve.wait_ge(h_done, n + 1)
                    m = KT * (NGATE if n == GATE_PANEL else P)
                    tt(wL[:, n % NW].rearrange("p a b -> p (a b)")[:, 0:m], raw[:, n % NRAW, 0:m],
                       wH[:, n % NW].rearrange("p a b -> p (a b)")[:, 0:m].bitcast(F32), ALU.subtract).then_inc(l_done, 1)
                elif kind == "cmpp" or kind == "nsa":
                    idx = 0 if kind == "cmpp" else n + 1
                    m = NCMP if idx else NCMP_P
                    if idx == 0:
                        read(dve, ("mm", 0))
                        dve.wait_ge(small_in, 32)
                        nc.vector.tensor_copy(xc[:, :, 0:32], zT[:, S_CMP, 0:T].rearrange("p (c r) -> p r c", r=16))
                        nc.vector.tensor_copy(xc[:, :, 32], vec[:, V_POS:V_POS + 16])
                        nc.vector.tensor_copy(xc[:, :, 33], vec[:, V_POS + 16:V_POS + 32]).then_inc(xc_done, 1)
                    dve.wait_ge(cmp_t1, idx + 1)
                    tt(hu[:, 2, 0:m], psum[:, 4, 0:m], hu[:, 1, 0:m], ALU.add).then_inc(cmp_u, 1)
                    if kind == "nsa":
                        dve.wait_ge(ssel_mm, n + 1)
                        s = psum[:, 6 + n % 2, :].rearrange("p (s r) -> p s r", s=8)
                        chain(red(nmS[:, n, :], s, AX.X, ALU.max, negate=True))
                        if n == 0:
                            dve.wait_ge(xh_done, KT)
                            dve.wait_ge(xl_done, KT)
                        tt(Psel[:, n, :].rearrange("p (s r) -> p s r", s=8), s, spread(nmS[:, n, :], HD), ALU.add).then_inc(ssel_sub, 1)
                    dve.wait_ge(cmp_th, idx + 1)
                    if idx:
                        dve.wait_ge(kv_mm, idx)
                    stt(hu[:, 0, 0:m], hu[:, 1, 0:m], 1.0, hu[:, 2, 0:m], ALU.add, ALU.mult).then_inc(hid_done, 1)
                elif kind == "kv" and n:
                    dve.wait_ge(ssel_exp, n)
                    red(lS[:, n - 1, :], Psel[:, n - 1, :].rearrange("p (s r) -> p s r", s=8), AX.X, ALU.add)
                elif kind in ("qn", "qm"):
                    read(dve, ("mm", PANEL_SLOT.index(S_Q + 1) if kind == "qn" else PANEL_SLOT.index(S_MQ + 1)))
                    dve.wait_ge(const_done, NCONSTS)
                    for h in range(H):
                        base = HD * (h % 2)
                        if kind == "qn":
                            nc.vector.tensor_copy(QNa[0:HD, :, h], zT[base:base + HD, S_Q + h // 2, T:NT])
                            last = nc.vector.tensor_copy(QNb[HD:P, :, h], zT[base:base + HD, S_Q + h // 2, T:NT])
                        else:
                            last = nc.vector.tensor_copy(QM[base:base + HD, h // 2, :, h], zT[base:base + HD, S_MQ + h // 2, T:NT])
                    last.then_inc(qn_done if kind == "qn" else qm_done, 1)
                elif kind == "glu":
                    read(dve, ("mm", PANEL_SLOT.index(S_CG + 1)))
                    dve.wait_ge(state_in, 32)
                    nc.vector.memset(zc[:, :, 0:CW - 1], 0.0)
                    for t in range(2):
                        stt(zc[:, t, CW - 1:], zT[:, S_CG + t, 0:T], 1.0, zT[:, S_CA + t, 0:T], ALU.add, ALU.mult)
                        stt(sc[:, t, :, CW - 1], zT[:, S_CG + t, T:NT], 1.0, zT[:, S_CA + t, T:NT], ALU.add, ALU.mult).then_inc(glu_done, 1)
                    dve.wait_ge(glu_done, 2)
                elif kind == "taps":
                    for k, t in TAPS[n[0]:n[1]]:
                        w = vec[:, V_DW + t * CW + k:V_DW + t * CW + k + 1]
                        if k == 0:
                            ts(yc[:, t, 0:T], zc[:, t, 0:T], w, vec[:, V_DWB + t:V_DWB + t + 1], ALU.mult, ALU.add).then_inc(vtap, 1)
                        else:
                            dve.wait_ge(vtap, taps - 1)
                            stt(yc[:, t, 0:T], zc[:, t, k:k + T], w, yc[:, t, 0:T], ALU.mult, ALU.add).then_inc(vtap, 1)
                        taps += 1
                    if n[1] == len(TAPS):
                        tmp = pa[:, 0:B * CW].rearrange("p (b k) -> p b k", b=B)
                        for t in range(2):
                            chain(tt(tmp, sc[:, t], spread_at(vec[:, V_DW + t * CW:V_DW + (t + 1) * CW], 1, B), ALU.mult))
                            chain(red(yc[:, t, T:NT], tmp, AX.X, ALU.add))
                            last = ts(yc[:, t, T:NT], yc[:, t, T:NT], vec[:, V_DWB + t:V_DWB + t + 1], None, ALU.add)
                        last.then_inc(conv_done, 1)
                elif kind == "zrows":
                    dve.wait_ge(gate_t, 1)
                    ts(gT[:, :, :], gT[:, :, :], 0.5, 0.5, ALU.mult, ALU.add).then_inc(gate_done, 1)
                elif kind == "att":
                    if n < NU:
                        u = n
                        ukind, h, i = UNITS[u]
                        bk = psum[:, 4 + u % 2, :]
                        nm = ps_small[:, u % 2:u % 2 + 1]
                        dve.wait_ge(qk_done, u + 1)
                        if ukind == "cmp":
                            chain(tt(bk[:, 0:NCMP_P], bk[:, 0:NCMP_P], cst[:, C_CMPM + i * NCMP_P:C_CMPM + (i + 1) * NCMP_P], ALU.add))
                            if u >= 2:
                                dve.wait_ge(exp_done, u - 1)
                            chain(red(nm, bk[:, 0:NCMP_P], AX.X, ALU.max, negate=True))
                            ts(nm, nm, 1e20, None, ALU.min).then_inc(max_done, 1)
                        else:
                            m = P * (i + 1)
                            chain(tt(bk[:, m - P:m], bk[:, m - P:m], cst[:, C_CAUS:C_CAUS + P], ALU.add))
                            if u >= 2:
                                dve.wait_ge(exp_done, u - 1)
                            red(nm, bk[:, 0:m], AX.X, ALU.max, negate=True).then_inc(max_done, 1)
                    if 1 <= n <= NU:
                        u = n - 1
                        ukind, h, i = UNITS[u]
                        l, r = ps_small[:, 4 + u % 2:5 + u % 2], ps_small[:, 8 + u % 2:9 + u % 2]
                        dve.wait_ge(exp_done, u + 1)
                        if u >= 2:
                            dve.wait_ge(scaled, u - 1)
                        if ukind == "cmp":
                            chain(ts(l, l, 1e-30, None, ALU.max))
                        if ukind == "moba":
                            nc.vector.reciprocal(r, l).then_inc(r_done, 1)
                        else:
                            if u == 0:
                                dve.wait_ge(gate_done, 1)
                            c = {"cmp": 0, "sel": H, "win": 2 * H}[ukind] + h
                            chain(nc.vector.reciprocal(r, l))
                            ts(r, r, gT[:, i, c:c + 1], None, ALU.mult).then_inc(r_done, 1)
                elif kind == "pool":
                    read(dve, ("mm", PANEL_SLOT.index(S_PO + 1)))
                    x = zT[:, S_PO + n, :]
                    if n == 0:
                        for t in range(2):
                            nc.vector.tensor_copy(sp[:, t, :, 15], zT[:, S_PO + t, T:NT])
                    else:
                        dve.wait_ge(pool_mm, 1)
                    def double(dst, src, w):
                        nc.vector.tensor_copy(dst[:, 0:w], src[:, 0:w])
                        chain(tt(dst[:, w:T], src[:, w:T], src[:, 0:T - w], ALU.add))
                    double(pa, x, 1)
                    double(pb, pa, 2)
                    if n == 1:
                        double(pa, pb, 4)
                        double(pb, pa, 8)
                    w0, w1_ = ((2, 4), (8, 16))[n]
                    for lo, s in ((0, pa), (HD, pb)):
                        q = slice(lo, lo + HD)
                        tt(pb[q, 0:16], s[q, 0:16], cst[q, C_INVC + 16 * n:C_INVC + 16 * n + 16], ALU.mult)
                        chain(stt(pb[q, 16:T], s[q, 16:T], cst[q, C_INVW + n:C_INVW + n + 1], x[q, 16:T], ALU.mult, ALU.subtract))
                        tt(pb[q, 0:16], pb[q, 0:16], x[q, 0:16], ALU.subtract)
                    for lo, w in ((0, w0), (HD, w1_)):
                        red(pb[lo:lo + HD, T:NT], sp[lo:lo + HD, n, :, 16 - w:16], AX.X, ALU.add)
                    chain(nc.vector.tensor_copy(st[:, 250:251], cst[:, C_INVW:C_INVW + 1]))
                    stt(pb[:, T:NT], pb[:, T:NT], cst[:, C_INVW + n:C_INVW + n + 1], x[:, T:NT], ALU.mult, ALU.subtract).then_inc(pool_d, 1)
                elif kind == "cmean":
                    dve.wait_ge(cm_mm, 1)
                    for t in range(2):
                        last = tt(zview(yc[:, t, :]), zview(yc[:, t, :]), acc(step)[:, :, 0:HALF], ALU.subtract)
                    last.then_inc(acc_read[1], 1)
                elif kind == "cvar":
                    read(dve, step)
                    chain(nc.vector.reciprocal(zT[:, S_CG, :], zT[:, S_CG, :]))
                    for t in range(2):
                        chain(stt(yc[:, t, :], yc[:, t, :], vec[:, V_CG + t:V_CG + t + 1], zT[:, S_CG, :], ALU.mult, ALU.mult))
                        last = ts(yc[:, t, :], yc[:, t, :], vec[:, V_CB + t:V_CB + t + 1], None, ALU.add)
                    last.then_inc(cn_done, 1)
                    dve.wait_ge(cth, 1)
                    stt(yc[:, :, :], zT[:, S_CG:S_CG + 2, :], 1.0, yc[:, :, :], ALU.add, ALU.mult).then_inc(cact, 1)
                elif kind == "csc":
                    dve.wait_ge(csc_mm, 1)
                    s = psum[:, 0, 0:2 * P].rearrange("p (c x) -> p c x", c=2)[:, :, 0:NCMP]
                    chain(red(nmC, s, AX.X, ALU.max, negate=True))
                    tt(Pc[:, :, 0:NCMP], s, spread(nmC, NCMP), ALU.add).then_inc(bfree[0], 1)
                    dve.wait_ge(csc_exp, 1)
                    chain(red(lC, Pc[:, :, 0:NCMP], AX.X, ALU.add))
                    chain(nc.vector.reciprocal(lC, lC))
                    tt(Pc[:, :, 0:NCMP], Pc[:, :, 0:NCMP], spread(lC, NCMP), ALU.mult).then_inc(csc_done, 1)
                elif kind == "ctr":
                    dve.wait_ge(ctr_mm, 1)
                    nc.vector.tensor_copy(PcT[0:NCMP, :, :], psum[0:NCMP, 1, 0:2 * P].rearrange("p (c x) -> p c x", c=2)).then_inc(bfree[1], 1)
                    bank_read(dve, 1, step)
                    red(ps_small[0:NCMP, 16:16 + B].rearrange("p (c j) -> p c j", c=2),
                        PcT[0:NCMP, :, :].rearrange("p c (j h) -> p c j h", j=4)[:, :, :, 0:H], AX.X, ALU.add).then_inc(ctr_done, 1)
                elif kind == "cimp":
                    dve.wait_ge(cimp_mm, 1)
                    imp, m8, imp2, imp3, nsel = sm[:, 16:49], sm[:, 56:64], sm[:, 64:97], sm[:, 100:133], sm[:, 136:169]
                    nc.vector.tensor_copy(imp, psum[0:B, 0, 0:NSELB]).then_inc(bfree[0], 1)
                    bank_read(dve, 0, step)
                    nc.vector.memset(imp[:, 0:1], 1e30)
                    chain(nc.vector.memset(imp[:, NSELB - 2:NSELB], 1e30))
                    chain(nc.vector.max(m8, imp))
                    chain(nc.vector.match_replace(imp2, m8, imp, -1.0))
                    chain(nc.vector.max(m8, imp2))
                    chain(nc.vector.match_replace(imp3, m8, imp2, -1.0))
                    chain(tt(nsel, imp3, imp, ALU.is_equal))
                    chain(ts(nsel, nsel, -NEG, None, ALU.mult))
                elif kind == "win":
                    dve.wait_ge(win_mm, 1)
                    dve.wait_ge(csc_mm, 1)
                    for c in range(2):
                        s = psum[:, c, :].rearrange("p (b x) -> p b x", b=4)
                        chain(red(nmW[:, 4 * c:4 * c + 4], s, AX.X, ALU.max, negate=True))
                        tt(Pwin[:, 4 * c:4 * c + 4, :], s, spread(nmW[:, 4 * c:4 * c + 4], P), ALU.add).then_inc(bfree[c], 1)
                    dve.wait_ge(win_exp, 1)
                    red(lW, Pwin[:, :, :], AX.X, ALU.add).then_inc(win_l, 1)
                elif kind == "mu":
                    u = n
                    if u < MU:
                        dve.wait_ge(ms_mm, u + 1)
                        red(nmM[:, u:u + 1], psum[:, u % 2, 0:P], AX.X, ALU.max, negate=True)
                        red(gM[:, u:u + 1], psum[:, u % 2, 0:P], AX.X, ALU.add).then_inc(mmax, 1)
                    if 1 <= u <= MU:
                        dve.wait_ge(mt_mm, u)
                        if u >= 3:
                            dve.wait_ge(mp_mm, u - 2)
                        nc.vector.tensor_copy(PTm2[:, (u - 1) % 2, :], psum[:, 2, 0:P]).then_inc(bfree[2], 1)
                elif kind == "stat":
                    NM, LL = eb[:, 0], eb[:, 1]
                    G4 = sm[:, 176:240].rearrange("p (h s) -> p h s", h=H)
                    dve.wait_ge(stat_mm, n + 1)

                    def seg(k, q):
                        return psum[0:B, k, q * P:(q + 1) * P].rearrange("p (j x) -> p j x", j=4)[:, :, 0:H]

                    if n == 0:
                        for k in range(4):
                            for half in range(2):
                                s = psum[0:B, k, :].rearrange("p (s j x) -> p s j x", s=4, j=4)[:, :, 2 * half:2 * half + 2, 0:H]
                                lo = half * 16 + (k % 2) * 8
                                dst = (NM if k < 2 else LL)[:, :, lo:lo + 8].rearrange("p h (s g) -> p s g h", g=2)
                                if k < 2:
                                    blk = sm[:, 136 + half:136 + half + 32:2].rearrange("p (g s) -> p s g", g=2)[:, 4 * k:4 * k + 4, :]
                                    last = tt(dst, s, spread(blk, H), ALU.add)
                                else:
                                    last = nc.vector.tensor_copy(dst, s)
                            last.then_inc(bfree[k], 1)
                    elif n == 1:
                        items = [(NM, 50), (LL, 50)] + [(NM, 33 + 4 * k) for k in range(4)] + [(G4, 4 * k) for k in range(4)]
                        for q, (dst, lo) in enumerate(items):
                            last = nc.vector.tensor_copy(dst[:, :, lo:lo + 4].rearrange("p h j -> p j h"), seg(q // 4, q % 4))
                            if q % 4 == 3 or q == len(items) - 1:
                                last.then_inc(bfree[q // 4], 1)
                    else:
                        for k in range(4):
                            last = nc.vector.tensor_copy(LL[:, :, 33 + 4 * k:37 + 4 * k].rearrange("p h j -> p j h"), seg(0, k))
                        last.then_inc(bfree[0], 1)
                elif kind == "comb":
                    NM, LL, E = eb[:, 0], eb[:, 1], eb[:, 2]
                    G4 = sm[:, 176:240].rearrange("p (h s) -> p h s", h=H)
                    G13 = sm[:, 240:292].rearrange("p (h s) -> p h s", h=H)
                    R13 = sm[:, 292:344].rearrange("p (h s) -> p h s", h=H)
                    m8, MN, L3 = sm[:, 344:352], sm[:, 352:364].rearrange("p (a h) -> p a h", a=3), sm[:, 364:376].rearrange("p (a h) -> p a h", a=3)
                    bank_read(dve, 0, ("stat", 2))
                    tmp = WB[:, 0:2, :].rearrange("p a b -> p (a b)").rearrange("p (h d) -> p h d", h=H)
                    q = zs[:, 4:6, :].rearrange("p a b -> p (a b)").rearrange("p (h d) -> p h d", h=H)
                    mq = zs[:, 6:8, :].rearrange("p a b -> p (a b)").rearrange("p (h d) -> p h d", h=H)
                    mk = zs[:, 8:10, :].rearrange("p a b -> p (a b)").rearrange("p (h d) -> p h d", h=H)
                    dve.wait_ge(zr_done, 6)
                    for x, k, at_ in ((q, spread_at(zs[:, 1, 0:HD], 1, H), 32), (mq, mk, 49), (q, spread_at(zs[:, 3, 0:HD], 1, H), 54)):
                        chain(tt(tmp, x, k, ALU.mult))
                        chain(red(NM[:, :, at_], tmp, AX.X, ALU.add, negate=True))
                        nc.vector.memset(LL[:, :, at_], 1.0)
                    nc.vector.memset(G13[:, :, 8:13], 3e38)
                    g2 = G4.rearrange("p h (s e) -> p h s e", e=2)
                    chain(tt(G13[:, :, 0:8], g2[:, :, :, 0], g2[:, :, :, 1], ALU.add))
                    for h in range(H):
                        chain(nc.vector.max(m8, G13[:, h, :]))
                        chain(nc.vector.match_replace(R13[:, h, :], m8, G13[:, h, :], -3e38))
                    chain(tt(R13[:, :, 0:8], R13[:, :, 0:8], G13[:, :, 0:8], ALU.is_equal))
                    chain(ts(R13[:, :, 0:8], R13[:, :, 0:8], -NEG, None, ALU.mult))
                    mm_ = NM[:, :, 33:49].rearrange("p h (s e) -> p h s e", e=2)
                    for e in range(2):
                        last = tt(mm_[:, :, :, e], mm_[:, :, :, e], R13[:, :, 0:8], ALU.add)
                    chain(last)
                    parts = ((0, 33), (33, 50), (50, 55))
                    for br, (lo, hi) in enumerate(parts):
                        last = red(MN[:, br, :], NM[:, :, lo:hi], AX.X, ALU.min)
                    chain(last)
                    for br, (lo, hi) in enumerate(parts):
                        last = tt(E[:, :, lo:hi], spread(MN[:, br, :], hi - lo), NM[:, :, lo:hi], ALU.subtract)
                    last.then_inc(comb_sub, 1)
                    dve.wait_ge(comb_exp, 1)
                    nc.vector.memset(WB[:, :, :], 0.0)
                    nc.vector.memset(gdiag[:, :, :], 0.0)
                    ts(sm[:, 0:NGATE], sm[:, 0:NGATE], 0.5, 0.5, ALU.mult, ALU.add)
                    chain(tt(NM, E, LL, ALU.mult))
                    for br, (lo, hi) in enumerate(parts):
                        last = red(L3[:, br, :], NM[:, :, lo:hi], AX.X, ALU.add)
                    chain(last)
                    chain(nc.vector.reciprocal(L3, L3))
                    tt(L3[:, 0, :], L3[:, 0, :], sm[:, H:2 * H], ALU.mult)
                    chain(tt(L3[:, 2, :], L3[:, 2, :], sm[:, 2 * H:3 * H], ALU.mult))
                    for br, (lo, hi) in enumerate(parts):
                        last = tt(E[:, :, lo:hi], E[:, :, lo:hi], spread(L3[:, br, :], hi - lo), ALU.mult)
                    chain(last)
                    for half in range(2):
                        nc.vector.tensor_copy(
                            WB[:, 0:8, 64 * half:64 * half + 64].rearrange("p s (g x) -> p s g x", g=2)[:, :, :, 0:H],
                            E[:, :, 16 * half:16 * half + 16].rearrange("p h (s g) -> p s g h", g=2))
                    nc.vector.tensor_copy(WB[:, 8, :].rearrange("p (j x) -> p j x", j=4)[:, :, 0:H], E[:, :, 50:54].rearrange("p h j -> p j h"))
                    nc.vector.tensor_copy(WB[:, 9:13, :].rearrange("p s (j x) -> p s j x", j=4)[:, :, :, 0:H],
                                          E[:, :, 33:49].rearrange("p h (s j) -> p s j h", j=4))
                    delta = cst[0:B, C_DELTA:C_DELTA + B]
                    for br, at_ in enumerate((32, 49, 54)):
                        tt(wnew[:, br, :, :], spread_at(E[:, :, at_], 1, B), spread(delta, H), ALU.mult)
                    tt(gdiag[:, :, 0:H], spread_at(sm[:, 0:H], 1, B), spread(delta, H), ALU.mult).then_inc(wb_done, 1)
                elif kind == "back":
                    bank_read(dve, 0, step)
                    nc.vector.memset(zeros[:, :], 0.0)
                    wv = Wt[:, :, :].rearrange("p s b -> p b s")
                    tt(Psel[:, :, :].rearrange("p b (s r) -> p b s r", s=8), Psel[:, :, :].rearrange("p b (s r) -> p b s r", s=8),
                       spread(wv[:, :, 0:8], HD), ALU.mult)
                    tt(Pwin[:, :, :], Pwin[:, :, :], spread(Wt[:, 8, :], P), ALU.mult).then_inc(pscaled, 1)
                    hm = cst[:, C_HM:C_HM + H]
                    for b in range(B):
                        last = tt(Wd[:, b, :, :], spread(wv[:, b, 9:13], H), spread_at(hm, 1, 4), ALU.mult)
                    last.then_inc(md_done, 1)
                elif kind == "spv":
                    dve.wait_ge(st_mm, n + 1)
                    if n >= 2:
                        dve.wait_ge(spv_mm, n - 1)
                    for k in range(2):
                        s = psum[0:HD, k, :].rearrange("p (s j x) -> p s j x", s=4, j=4)
                        for half in range(2):
                            last = nc.vector.tensor_copy(
                                PTs[HD * half:HD * half + HD, n % 2, :, 4 * k:4 * k + 4, :].rearrange("p g s h -> p s g h"),
                                s[:, :, 2 * half:2 * half + 2, 0:H])
                        last.then_inc(bfree[k], 1)
                elif kind == "mpv":
                    dve.wait_ge(spv_mm, B)
                    bank_read(dve, 1, ("back", 0))
                    bank_read(dve, 2, ("cimp", 0))
                    for c in range(2):
                        last = stt(On[:, c, :], oc[:, c, :], g0[:, c:c + 1], psum[:, 3, c * HD:(c + 1) * HD], ALU.mult, ALU.add)
                    last.then_inc(fin_o, 1)
                elif kind == "fin":
                    dve.wait_ge(fin_mm, 1)
                    v = psum[:, 1, :].rearrange("p (c e x) -> p c e x", c=2, e=2)
                    for h in range(H):
                        base = HD * (h % 2)
                        last = nc.vector.tensor_copy(
                            zT[base:base + HD, S_MQ + h // 2, T:NT].rearrange("p (c j) -> p c j", c=2),
                            v[base:base + HD, :, h // 2, :].rearrange("p c (j x) -> p c j x", x=32)[:, :, :, h])
                    last.then_inc(bfree[1], 1)
                elif kind == "msplit":
                    dve.wait_ge(mixh, n + 1)
                    tt(opL[:, n, :], zT[:, MIX_SLOT[n], :], opH[:, n, :].bitcast(F32), ALU.subtract).then_inc(mixl, 1)
                elif kind == "evac" and OUT0 <= n < FF0:
                    dve.wait_ge(mm_done, n + 1)
                    dve.wait_ge(x_in, 32)
                    x = zview(xres[:, n - OUT0, :])
                    stt(x, x, ALPHA, acc(("mm", n))[:, :, 0:HALF], ALU.mult, ALU.add).then_inc(acc_read[1], 1)
                elif kind == "evac" and n >= FF0:
                    fkind, g, m = FFN[n - FF0]
                    if fkind == "up":
                        dve.wait_ge(sq_done, up_no + 1)
                        dve.wait_ge(hidh_done, up_no + 1)
                        tt(hidL[g % 2][:, m, :], hsq[:, up_no % 2, :], hidH[g % 2][:, m, :].bitcast(F32), ALU.subtract).then_inc(hid_l_done, 1)
                        up_no += 1
                    else:
                        dve.wait_ge(mm_done, n + 1)
                        dve.wait_ge(acc_read[1], nread(("mm", n)) - 1)
                        if g == 0 and m == 0:
                            dve.wait_ge(ln_n, KT)
                        x = zview(xres[:, m, :])
                        stt(x, x, ALPHA if g == 0 else 1.0, acc(("mm", n))[:, :, 0:HALF], ALU.mult, ALU.add).then_inc(acc_read[1], 1)
                elif kind == "ln":
                    G, Bc = (V_G1, V_B1) if n == 0 else (V_G2, V_B2)
                    dve.wait_ge(ln_mm, n + 1)
                    read(dve, ("mm", FF0 - 1 if n == 0 else N_PANELS - 1))
                    for k in range(KT):
                        tt(zview(xres[:, k, :]), zview(xres[:, k, :]), acc(("lnm", n))[:, :, 0:HALF], ALU.subtract)\
                            .then_inc(ln_d if k < KT - 1 else acc_read[1], 1)
                    read(dve, ("lnv", n))
                    dve.wait_ge(ln_sq, (n + 1) * KT)
                    chain(nc.vector.reciprocal(rstd[:, :], rstd[:, :]))
                    for k in range(KT + 1):
                        if k < KT:
                            stt(xres[:, k, :], xres[:, k, :], vec[:, G + k:G + k + 1], rstd[:, :], ALU.mult, ALU.mult).then_inc(vln, 1)
                        if k:
                            dve.wait_ge(vln, n * KT + k)
                            ts(xres[:, k - 1, :], xres[:, k - 1, :], vec[:, Bc + k - 1:Bc + k], None, ALU.add).then_inc(ln_n, 1)
                    if n == 0:
                        for k in range(KT):
                            dve.wait_ge(ln_h, k + 1)
                            tt(opL[:, k, :], xres[:, k, :], opH[:, k, :].bitcast(F32), ALU.subtract).then_inc(ln_l, 1)


def layouts(x):
    f = lambda v: np.ascontiguousarray(v)
    xT = np.concatenate([x["x_prompt"].reshape(T, D), x["x_sample"].reshape(B, D)], 0).T
    w_in = x["w_in"][0]
    c0 = np.cumsum([0, 512, 256, 384, 12, 768, 256])
    kv, mo = c0[2], c0[4]
    r = lambda lo, n=P: list(range(lo, lo + n))
    cols = {S_CMP: r(kv), S_KSEL: r(kv + 128, 64) + r(kv + 256, 64), S_V: r(kv + 192, 64) + r(kv + 320, 64)}
    for t in range(2):
        cols[S_Q + t] = r(c0[1] + t * P)
        cols[S_CA + t] = r(c0[0] + t * P)
        cols[S_CG + t] = r(c0[0] + 256 + t * P)
        cols[S_PO + t] = r(c0[5] + t * P)
        for s, base in ((S_MQ, 0), (S_MK, 256), (S_MV, 512)):
            cols[s + t] = r(mo + base + t * P)

    def panel(w, rows, c):
        return w[rows][:, c].reshape(KT, P, len(c)).transpose(1, 0, 2)

    allr = slice(0, D)
    panels = [panel(w_in, allr, cols[s]) for s in PANEL_SLOT if s != S_GATE]
    panels += [panel(x["w_out"][0], allr, r(t * P)) for t in range(KT)]
    for kind, g, n in FFN:
        if kind == "up":
            panels.append(panel(x["w_up"][0], allr, r((g * KT + n) * P)))
        else:
            panels.append(panel(x["w_down"][0], slice(g * D, (g + 1) * D), r(n * P)))
    nsa = x["cache_nsa_kv"][0]
    cmpT = nsa[:, :, 0:2].reshape(NPOOL, 8, 16, 2, HD).transpose(0, 3, 4, 2, 1).reshape(NPOOL, P, P)
    selK = nsa[:, :, 2].reshape(NPOOL, 2, HD, HD).transpose(0, 1, 3, 2).reshape(NPOOL, P, HD)
    mob = x["cache_moba_kv"][0]
    mK = mob[:, :, 0].transpose(0, 2, 3, 1).reshape(NPOOL, 2, P, PAGE).transpose(0, 2, 1, 3).reshape(NPOOL, P, 256)
    mV = mob[:, :, 1].reshape(NPOOL, PAGE, 256)
    win = x["state_nsa_win"][0]
    winK = win[:, :, 0].reshape(B, 2, 256, HD).transpose(1, 3, 0, 2).reshape(P, B, 256)
    winV = win[:, :, 1].reshape(B, 4, P, HD).transpose(2, 0, 1, 3)
    w1 = x["nsa_cmp_w1"][0].reshape(2, 32, HD, HD)
    w1d = np.zeros((P, 32, P), np.float32)
    w1d[0:HD, :, 0:HD] = w1[0].transpose(1, 0, 2)
    w1d[HD:P, :, HD:P] = w1[1].transpose(1, 0, 2)
    vec = np.zeros((P, NVEC), np.float32)

    def put(at, v, rows=slice(0, P)):
        v = np.asarray(v).reshape(v.shape[0], -1)
        vec[rows, at:at + v.shape[1]] = v

    tiles = lambda v: v.reshape(-1, P).T
    put(V_DW, x["conv_dw"][0].T.reshape(2, P, CW).transpose(1, 0, 2))
    put(V_DWB, tiles(x["conv_dw_b"][0]))
    put(V_CG, tiles(x["conv_ln_g"][0]))
    put(V_CB, tiles(x["conv_ln_b"][0]))
    put(V_PS, tiles(x["pool_scale"][0]))
    put(V_G1, tiles(x["ln1_g"][0]))
    put(V_B1, tiles(x["ln1_b"][0]))
    put(V_G2, tiles(x["ln2_g"][0]))
    put(V_B2, tiles(x["ln2_b"][0]))
    put(V_POS, x["nsa_cmp_pos"][0].transpose(0, 2, 1).reshape(P, 32))
    put(V_W2, x["nsa_cmp_w2"][0].reshape(P, HD))
    put(V_PW, x["conv_pw"][0].reshape(2, P, 256).transpose(1, 0, 2))
    for g in range(4):
        lo = HD * (g % 2)
        put(V_PO + g // 2 * P + lo, x["pool_w"][0, g], slice(lo, lo + HD))
    cst = np.zeros((P, NCONST), np.float32)
    p_ = np.arange(P)
    cst[:, C_ID:C_ID + P] = np.eye(P)
    cst[:, C_CAUS:C_CAUS + P] = np.where(p_[None, :] <= p_[:, None], 0.0, NEG)
    for i in range(QT):
        last = 16 * np.arange(NCMP_P) + 31
        cst[:, C_CMPM + i * NCMP_P:C_CMPM + (i + 1) * NCMP_P] = np.where(last[None, :] <= (i * P + p_)[:, None], 0.0, NEG)
    j, s = np.arange(NCMP)[:, None], np.arange(NSELB)[None, :]
    cst[0:NCMP, C_COVER:C_COVER + NSELB] = (j * 16 < (s + 1) * 64) & (j * 16 + 32 > s * 64)
    cst[0:B, C_DELTA:C_DELTA + B] = np.eye(B)
    for h in range(H):
        cst[:, C_HM + h] = p_ % 32 == h
    for n in range(2):
        w = np.where(p_ < HD, 2 * 4 ** n, 4 * 4 ** n)
        cst[:, C_INVC + 16 * n:C_INVC + 16 * n + 16] = 1.0 / np.minimum(w[:, None], np.arange(16)[None, :] + 1)
        cst[:, C_INVW + n] = 1.0 / w
    return {
        "xT": f(xT.reshape(KT, P, NT).transpose(1, 0, 2)),
        "panels": f(np.stack([p.reshape(P, D) for p in panels])),
        "w_gate": f(panel(w_in, allr, r(c0[3], NGATE)).reshape(P, KT * NGATE)),
        "nsa_pages": f(np.concatenate([cmpT, selK], 2)),
        "selv_pages": f(nsa[:, :, 3]),
        "moba_pages": f(np.concatenate([mK, mV], 2)),
        "winK": f(winK), "winV": f(winV), "state_win": f(win.reshape(B, T, P)),
        "state_convT": f(x["state_conv"][0].transpose(2, 0, 1).reshape(2, P, B, CW - 1).transpose(1, 0, 2, 3)),
        "state_poolT": f(x["state_pool"][0].transpose(2, 0, 1).reshape(2, P, B, 15).transpose(1, 0, 2, 3)),
        "page_table": f(x["page_table"].reshape(1, B * PAGES).astype(np.int32)),
        "w1": w1d, "vecs": vec, "consts": cst,
    }


OUTS = {"y": (P, KT, NT), "z_cmp": (P, NT), "z_ksel": (HD, NT), "z_kwin": (HD, NT), "z_v": (P, NT), "z_moba": (P, 4, NT),
        "win_sample": (B, T, P), "conv_prompt": (P, 2, CW - 1), "conv_sample": (P, 2, B, CW - 1),
        "pool_prompt": (P, 2, 15), "pool_sample": (P, 2, B, 15)}


def kernel(**inputs):
    import concourse.bacc as bacc
    from concourse.bass_utils import run_bass_kernel_spmd

    x = {k: np.asarray(v) for k, v in inputs.items()}
    arrays = {"in_" + k: v for k, v in layouts(x).items()}
    nc = bacc.Bacc("TRN2", target_bir_lowering=False, num_devices=1)
    a = {k[3:]: nc.dram_tensor(k, v.shape, mybir.dt.from_np(v.dtype), kind="ExternalInput").ap() for k, v in arrays.items()}
    o = {k: nc.dram_tensor("out_" + k, s, F32, kind="ExternalOutput").ap() for k, s in OUTS.items()}
    build(nc, a, o)
    r = run_bass_kernel_spmd(nc, [arrays], core_ids=[0]).results[0]
    g = {k: np.asarray(r["out_" + k]) for k in OUTS}
    y = g["y"].transpose(2, 1, 0).reshape(NT, D)
    mz = g["z_moba"].transpose(2, 1, 0).reshape(NT, 2, H, HD)
    nz = np.stack([g["z_cmp"][0:HD].T, g["z_cmp"][HD:P].T, g["z_ksel"].T, g["z_v"][0:HD].T], 1)
    wz = np.stack([g["z_kwin"][:, 0:T].T, g["z_v"][HD:P, 0:T].T], 1)
    up = lambda v: np.ascontiguousarray(v)
    chan = lambda v: v.transpose(1, 0, *range(2, v.ndim)).reshape(2 * P, *v.shape[2:])
    return (up(y[:T].reshape(1, T, D)), up(y[T:].reshape(B, 1, D)),
            up(mz[:T].reshape(1, 1, T, 2, H, HD)), up(mz[T:].reshape(1, B, 1, 2, H, HD)),
            up(nz[:T].reshape(1, 1, T, 4, HD)), up(nz[T:].reshape(1, B, 1, 4, HD)),
            up(wz.reshape(1, 1, T, 2, HD)), up(g["win_sample"].reshape(1, B, T, 2, HD)),
            up(chan(g["conv_prompt"]).T.reshape(1, 1, CW - 1, 256)),
            up(chan(g["conv_sample"]).transpose(1, 2, 0).reshape(1, B, CW - 1, 256)),
            up(chan(g["pool_prompt"]).T.reshape(1, 1, 15, 256)),
            up(chan(g["pool_sample"]).transpose(1, 2, 0).reshape(1, B, 15, 256)))
```

```python
import concourse.bass as bass
from concourse import mybir
from contextlib import ExitStack
import numpy as np

F32 = mybir.dt.float32
F32R = mybir.dt.float32r
I32 = mybir.dt.int32
ALU = mybir.AluOpType
ACT = mybir.ActivationFunctionType
AX = mybir.AxisListType

P = 128
D = 1024
KT = D // P
T, B = 512, 8
NT = T + B
HALF = NT // 2
H, HD = 4, 64
PAGE, PAGES = 128, 16
NPOOL = 160
NCHUNK = 128
NCMP = NCHUNK - 1
NCMP_P = T // 16 - 1
NSELB = 33
CW = 31
ALPHA = 2.0 ** 0.25
EPS = 1e-5
NEG = -1e30
FF = 4 * D
NG = 4
QT = T // P

S_CMP, S_Q, S_KSEL, S_KWIN, S_V, S_GATE, S_CA, S_CG, S_PO, S_MQ, S_MK, S_MV = 0, 1, 3, 4, 5, 6, 7, 9, 11, 13, 15, 17
NSLOT = 19
PANEL_SLOT = [S_CMP, S_CA, S_CA + 1, S_CG, S_CG + 1, S_Q, S_Q + 1, S_PO, S_PO + 1, S_MQ, S_MQ + 1,
              S_GATE, S_KSEL, S_V, S_MK, S_MK + 1, S_MV, S_MV + 1]
NSA_PANEL = PANEL_SLOT.index(S_Q + 1)
N_IN_PANELS = len(PANEL_SLOT)
GATE_PANEL = PANEL_SLOT.index(S_GATE)
NGATE = 12
ROW_SLOTS = [(S_GATE, S_KSEL, S_V, S_KWIN), (S_Q, S_Q + 1, S_MQ, S_MQ + 1), (S_MK, S_MK + 1, S_MV, S_MV + 1)]
MIX_SLOT = [S_CA, S_CA + 1, S_Q, S_Q + 1, S_MQ, S_MQ + 1, S_PO, S_PO + 1]
MIX_ORDER = [0, 1, 6, 7, 2, 3, 4, 5]
OUT0 = N_IN_PANELS
FFN = []
for _kind, _g in (("up", 0), ("up", 1), ("down", 0), ("up", 2), ("down", 1), ("up", 3), ("down", 2), ("down", 3)):
    FFN += [(_kind, _g, _n) for _n in range(KT)]
FF0 = OUT0 + KT
N_PANELS = FF0 + len(FFN)
NRAW, NW = 3, 2
NCONSTS = 7

C_ID, C_CAUS, C_CMPM, C_COVER, C_DELTA, C_HM, C_INVC, C_INVW = 0, 128, 256, 380, 413, 421, 425, 457
NCONST = 459
V_DW, V_DWB, V_CG, V_CB, V_PS, V_G1, V_B1, V_G2, V_B2, V_POS, V_W2, V_PW, V_PO = (
    0, 62, 64, 66, 68, 70, 78, 86, 94, 102, 134, 198, 710)
NVEC = 966

UNITS = [(_k, _h, _i) for _i in range(QT) for _h in range(H) for _k in ("cmp", "sel", "win")]
UNITS += [("moba", _h, _i) for _i in range(QT) for _h in range(H)]
NU = len(UNITS)
NNSA = 3 * H * QT
GROUP = [u // 3 if u < NNSA else NNSA // 3 + u - NNSA for u in range(NU)]
NGROUP = GROUP[-1] + 1
FIRST = [u == 0 or GROUP[u] != GROUP[u - 1] for u in range(NU)]
LAST = [u == NU - 1 or GROUP[u] != GROUP[u + 1] for u in range(NU)]
MU = B * 4
LAG = 3
ATT_PANEL = 15
PAD = ("pad", 0)
PADS = (0, 0, 0, 0, 0)
PER_PANEL = 7
TAPS = [(k, t) for k in range(CW) for t in range(2)]


def timeline():
    tl = [("load_x", 0), ("load_panel", 1), ("load_small", 0), ("load_panel", 2), ("load_w1", 0), ("load_nsa", 0)]
    tl += [("split", 0)]
    tl += [("xsplit", k) for k in range(KT)]

    def panel(i, mid=()):
        out = []
        if i + 1 < N_PANELS and i + 1 != OUT0:
            out.append(("split", i + 1))
        if i + NRAW < N_PANELS and (i >= OUT0 or i + NRAW < OUT0):
            out.append(("load_panel", i + NRAW))
        out.append(("mm", i))
        out += list(mid)
        out.append(("evac", i))
        return out

    def spread(first, n, extras):
        out = []
        for q in range(n):
            out.append(("att", first + q))
            out += [s for s in extras[q * len(extras) // n:(q + 1) * len(extras) // n] if s != PAD]
        return out

    def pieces(i, first, n, extras):
        out = [s for s in panel(i) if s[0] not in ("mm", "evac")]
        q = 0
        for s in spread(first, n, extras):
            if s[0] == "att":
                out.append(("mm", i, q, n))
                q += 1
            out.append(s)
        return out + [("evac", i)]

    nt = 2 * CW
    taps = [0, nt // 10, nt // 5, nt // 5 + 13, nt // 5 + 26, nt // 5 + 38, nt]
    pending = []
    att = 0
    M = lambda lo, hi: [s for u in range(lo, hi) for s in (("mu", u), ("mp", u - 1))]
    extras = {15: M(1, 2) + [("ctr", 0), ("zrow", 0)] + M(2, 3) + [("cimp", 0)],
              16: M(3, 4) + [("zrow", 1)] + M(4, 7),
              17: M(7, 11)}
    for i in range(N_IN_PANELS):
        b = i - NSA_PANEL
        if i >= ATT_PANEL:
            tl += pieces(i, att, PER_PANEL, extras[i])
            att += PER_PANEL
        else:
            tl += panel(i, pending)
        pending = []
        if i == 2:
            tl.append(("cmpp", 0))
            pending = [("kv", 0)]
        if i == NSA_PANEL:
            tl.append(("qn", 0))
        if 0 <= b < B:
            tl.append(("nsa", b))
            pending = [("kv", b + 1)]
            if b < B - 1:
                tl.append(("load_nsa", b + 1))
        if b == B - 1:
            tl.append(("load_post", 0))
        if i == 4:
            tl.append(("glu", 0))
        if 4 <= i < 10:
            tl.append(("taps", (taps[i - 4], taps[i - 3])))
        if i == 8:
            tl += [("out_early", 0), ("pdiff", 0)]
        if i == 10:
            tl += [("cmean", 0), ("pool", 0), ("pdiff", 1), ("qm", 0), ("out_conv", 0)]
        if i == 11:
            tl += [("cvar", 0)]
        if i == 12:
            tl += [("cpw", 0), ("pool", 1), ("load_lo", 0)]
        if i == 14:
            tl += [("csc", 0), ("zcols", 0), ("win", 0), ("mu", 0)]
    tl += [("out_z", 0)]
    side = [("zrow", 2), ("own", 0), ("vrow", 0), ("vrow", 1), ("msplit", 0), ("msplit", 1), ("msplit", 2), ("msplit", 3)]
    for u in range(11, MU + 1):
        side += [("mu", u), ("selv", u - 11), ("mp", u - 1)]
    side += [("selv", k) for k in range(MU + 1 - 11, 4 * (B - 1))]
    side += [("stat", k) for k in range(3)] + [PAD] * PADS[0] + [("comb", 0)] + [PAD] * PADS[1] + [("comb", 1)] + [PAD] * PADS[2] + [("back", 0)] + [PAD] * PADS[3]
    for b in range(B + 1):
        side += [PAD] * PADS[4] + [("spv", b)] + ([("load_panel", OUT0 + b - 1)] if 1 <= b <= NRAW else [])
    side += [("split", OUT0), ("mpv", 0), ("fin", 0)]
    tl += spread(att, NU + LAG - att, side)
    tl += [("load_x", 1)]
    tl += [("msplit", q) for q in range(4, KT)]
    for i in range(OUT0, FF0):
        tl += panel(i, [("mean", 0, i - OUT0 - 1)] if i > OUT0 else [])
    tl += [("mean", 0, KT - 1), ("ln", 0)]
    for i in range(FF0, N_PANELS):
        k = i - (N_PANELS - KT)
        tl += panel(i, [("mean", 1, k - 1)] if k > 0 else [])
    tl += [("mean", 1, KT - 1), ("ln", 1)]
    return tl


TL = timeline()
ACC = []
for _s in TL:
    if _s[0] == "mm" and (len(_s) == 2 or _s[2] == 0):
        ACC.append(("mm", _s[1]))
    if _s[0] in ("pool", "cmean", "cvar"):
        ACC.append(_s)
    if _s[0] == "cpw":
        ACC += [("cpw", 0), ("cpw", 1)]
NACC1 = ACC.index(("mm", OUT0))
NACC0 = ACC.index(("mm", 14))
PAIR = [1 if NACC0 <= n < NACC1 else n % 2 for n in range(len(ACC))]
ACC_NO = {k: n for n, k in enumerate(ACC)}
def reader(key):
    kind, n = key
    if kind == "mm":
        if OUT0 <= n < FF0 or (n >= FF0 and FFN[n - FF0][0] == "down"):
            return 1
        return 0
    return {"pool": 0, "cmean": 1, "cvar": 0, "cpw": 0}[kind]


def nread(key):
    r = reader(key)
    return sum(reader(k) == r for k in ACC[:ACC_NO[key] + 1])


USES = [[], [], [], []]
for _s in [s for s in TL if s[0] in ("zrow", "vrow", "csc", "ctr", "cimp", "win", "mu", "mp", "stat", "back", "spv", "mpv", "fin")]:
    _k, _n = _s
    _banks = {"csc": (0,), "ctr": (1,), "cimp": (0, 1), "win": (0, 1), "back": (0, 1), "fin": (0, 1)}.get(_k, ())
    if _k in ("zrow", "vrow"):
        _banks = (_n % 2,)
    if _k == "mu":
        _banks = ((0,) if _n < MU else ()) + ((1,) if _n >= 1 else ())
    if _k == "mp":
        _banks = (1,)
    if _k == "stat":
        _banks = ((0, 1, 2, 3), (0, 1, 2), (0,))[_n]
    if _k == "spv" and _n < B:
        _banks = (0, 1, 2)
    if _k == "mpv":
        _banks = (1, 2)
    for _b in _banks:
        USES[_b].append(_s)


def nth(bank, step):
    return USES[bank].index(step)


def build(nc, a, o):
    ctx = ExitStack()
    with ctx:
        def sem(name):
            return ctx.enter_context(nc.semaphore(name))

        at = [16512]

        def place(name, shape, dt=F32, offset=None):
            size = 4
            for s in shape[1:]:
                size *= s
            if offset is None:
                offset = at[0]
                at[0] += (size + 31) // 32 * 32
            return nc.alloc_sbuf_tensor_at(name, shape, dt, offset=offset)

        o_xres = at[0]
        xres = place("xres", [P, KT, NT])
        o_op = at[0]
        opH = place("opH", [P, KT, NT], F32R)
        opL = place("opL", [P, KT, NT], F32R)
        o_raw = at[0]
        raw = place("raw", [P, NRAW, KT * P])
        wH = place("wH", [P, NW, KT, P], F32R)
        wL = place("wL", [P, NW, KT, P], F32R)
        o_z = at[0]
        zT = place("zT", [P, NSLOT, NT])
        o_a = at[0]
        w1 = place("w1", [P, 32, P])
        nsa_ring = place("nsa_ring", [P, 2, PAGES, 192])
        o_m = at[0]
        moba_lo = place("moba_lo", [P, 2, 4, 512])
        winK = place("winK", [P, B, 256], F32, o_a)
        winV = place("winV", [P, B, 4, HD], F32, o_a + 8192)
        PB = place("PB", [P, 2, T], F32, o_a + 16384)
        PT = place("PT", [P, 2, T], F32, o_a + 16384 + 4096)
        moba_hi = place("moba_hi", [P, 2, 4, 512], F32, o_a + 24576)
        moba_ring = [moba_lo[:, 0], moba_lo[:, 1], moba_hi[:, 0], moba_hi[:, 1]]
        selV = [place(f"selV{b}", [P, PAGES, HD], F32, o_raw + b * PAGES * HD * 4 if b < B - 1 else o_m) for b in range(B)]
        WB = place("WB", [B, 13, P], F32, o_op + 2 * NT * 4)
        hidH = [place(f"hidH{g}", [P, KT, NT], F32R, o_z + g * 2 * KT * NT * 4) for g in range(2)]
        hidL = [place(f"hidL{g}", [P, KT, NT], F32R, o_z + (2 * g + 1) * KT * NT * 4) for g in range(2)]
        o_after_hid = o_z + 4 * KT * NT * 4
        relu = place("relu", [P, 2, NT], F32, o_after_hid)
        hsq = place("hsq", [P, 2, NT], F32, o_after_hid + 2 * NT * 4)
        sqb = place("sqb", [P, 2, NT], F32, o_after_hid + 4 * NT * 4)
        std = place("std", [P, NT], F32, o_after_hid + 6 * NT * 4)
        lnt = place("lnt", [P, 4, NT], F32, o_after_hid + 7 * NT * 4)
        zc = place("zc", [P, 2, CW - 1 + T], F32, o_m)
        sc = place("sc", [P, 2, B, CW], F32, o_m + 4352)
        yc = place("yc", [P, 2, NT], F32, o_m + 6336)
        pa = place("pa", [P, T], F32, o_m + 10496)
        pb = place("pb", [P, NT], F32, o_m + 12544)
        sp = place("sp", [P, 2, B, 16], F32, o_m + 14624)
        Psel = place("Psel", [P, B, 512], F32, o_xres)
        OM = place("OM", [P, MU, HD], F32, o_a)
        kcT = place("kcT", [HD, B, P])
        Pwin = place("Pwin", [P, B, P], F32, at[0] - 4096)
        Vn = place("Vn", [P, 3, QT, P])
        zs = place("zs", [B, 12, P])
        cst = place("cst", [P, NCONST])
        vec = place("vec", [P, NVEC])
        QNa = place("QNa", [P, B, 32])
        QNb = place("QNb", [P, B, 32])
        QM = place("QM", [P, 2, B, 32])
        vc = place("vc", [P, B, HD])
        kcp = place("kcp", [P, 32])
        vcp = place("vcp", [P, HD])
        xc = place("xc", [P, 16, 34], F32, o_a + 16384 + 12288)
        o_hu = at[0]
        hu = place("hu", [P, 3, P])
        own = place("own", [P, 256], F32, o_hu)
        bias = place("bias", [P, 1])
        gT = place("gT", [P, QT, NGATE])
        Pc = place("Pc", [P, 2, P])
        PcT = place("PcT", [P, 2, P])
        PTm2 = place("PTm2", [P, 2, P], F32, o_z + 1024)
        PTs = place("PTs", [P, 2, 2, 8, H], F32, o_op + (KT + 2) * NT * 4 + 512)
        PTw = place("PTw", [P, 2, 4, H])
        st = place("st", [P, 256])
        ps_small = place("ps_small", [P, 32])
        mean1024 = place("mean1024", [P, P])
        mean256 = place("mean256", [P, P])
        zeros = place("zeros", [P, P], F32, o_op + (KT + 2) * NT * 4)
        onesc = place("onesc", [P, 2])
        epsc = onesc[:, 1:2]
        onesc = onesc[:, 0:1]
        Pm = place("Pm", [P, 2, P], F32, o_z)
        o_g = o_z + S_CG * NT * 4
        gdiag = place("gdiag", [B, B, 32], F32, o_g)
        wnew = place("wnew", [B, 3, B, H], F32, o_g + 1024)
        eb = place("eb", [B, 3, H, 55], F32, o_g + 1408)
        Wd = place("Wd", [P, B, 4, H], F32, o_op + 2 * NT * 4 + 6656)
        Wt = place("Wt", [P, 13, B], F32, o_op + 2 * NT * 4 + 7168)
        oc = place("oc", [P, 2, HD])
        On = place("On", [P, 2, HD], F32, o_op + (KT + 2) * NT * 4 + 1024)
        Om = place("Om", [P, 2, HD], F32, o_op + (KT + 2) * NT * 4 + 1536)
        newV = place("newV", [P, 2, 256], F32, o_op + (KT + 2) * NT * 4 + 2048)
        sm = place("sm", [B, 376])
        page_ids = place("page_ids", [1, B * PAGES], I32)
        nmS, lS = st[:, 0:64].rearrange("p (b s) -> p b s", b=B), st[:, 64:128].rearrange("p (b s) -> p b s", b=B)
        nmW, lW = st[:, 128:136], st[:, 136:144]
        nmM, gM, lM = st[:, 144:176], st[:, 176:208], st[:, 208:240]
        nmC, lC = st[:, 240:242], st[:, 242:244]
        g0 = st[:, 244:246]
        ident = cst[:, C_ID:C_ID + P]
        stats = ([nmS[:, :, p] for p in range(8)] + [lS[:, :, p] for p in range(8)],
                 [nmW, lW] + [nmM.rearrange("p (b s) -> p s b", s=4)[:, k, :] for k in range(4)]
                 + [gM.rearrange("p (b s) -> p s b", s=4)[:, k, :] for k in range(4)],
                 [lM.rearrange("p (b s) -> p s b", s=4)[:, k, :] for k in range(4)])
        assert at[0] <= 229344, at[0]

        psum = ctx.enter_context(nc.psum_tensor("psum", [P, 8, 512], F32))

        def acc(key):
            p = PAIR[ACC_NO[key]]
            return psum[:, 2 * p:2 * p + 2, :]

        def read(eng, key):
            eng.wait_ge(acc_read[reader(key)], nread(key))

        def bank_read(eng, k, step):
            eng.wait_ge(bfree[k], nth(k, step) + 1)

        raw_in = [sem(f"raw_in{i}") for i in range(NRAW)]
        xk_in = [sem(f"x_in{k}") for k in range(KT)]
        x_in, small_in, w1_in, ids_in = sem("x_in"), sem("small_in"), sem("w1_in"), sem("ids_in")
        nsa_in = [sem(f"nsa_in{i}") for i in range(2)]
        moba_in = [sem(f"moba_in{i}") for i in range(4)]
        win_in, selv_in, state_in = sem("win_in"), sem("selv_in"), sem("state_in")
        out_state, out_z, out_y, out_early, out_conv, out_rows = (
            sem("out_state"), sem("out_z"), sem("out_y"), sem("out_early"), sem("out_conv"), sem("out_rows"))
        xh_done, xl_done = sem("xh_done"), sem("xl_done")
        h_done, l_done, mm_done = sem("h_done"), sem("l_done"), sem("mm_done")
        acc_read = [sem("acc_read_by_scalar"), sem("acc_read_by_vector")]
        const_done = sem("const_done")
        vch, ach, pch, vtap, vln = sem("vector_chain"), sem("scalar_chain"), sem("gpsimd_chain"), sem("tap_done"), sem("ln_scaled")
        xc_done, cmp_mm, cmp_t1, cmp_u, cmp_th, hid_done, kv_mm, kc_done = (
            sem("xc_done"), sem("cmp_mm"), sem("cmp_t1"), sem("cmp_u"), sem("cmp_th"), sem("hid_done"), sem("kv_mm"), sem("kc_done"))
        qn_done, qm_done = sem("qn_done"), sem("qm_done")
        ssel_mm, ssel_sub, ssel_exp = sem("ssel_mm"), sem("ssel_sub"), sem("ssel_exp")
        glu_done, conv_done = sem("glu_done"), sem("conv_done")
        zr_mm, zr_done, zc_mm, vn_done, gate_t, gate_done = sem("zr_mm"), sem("zr_done"), sem("zc_mm"), sem("vn_done"), sem("gate_t"), sem("gate_done")
        qk_done, max_done, exp_done, scaled, tr_done, pt_done, pv_done, o_done, r_done = (
            sem("qk_done"), sem("max_done"), sem("exp_done"), sem("scaled"), sem("tr_done"), sem("pt_done"),
            sem("pv_done"), sem("o_done"), sem("r_done"))
        pool_d, pool_mm, pool_done = sem("pool_d"), sem("pool_mm"), sem("pool_done")
        cm_mm, cd_done, csq_done, cv_mm, cstd, cn_done, cth, cact, cpw_mm, cpw_done = (
            sem("cm_mm"), sem("cd_done"), sem("csq_done"), sem("cv_mm"), sem("cstd"), sem("cn_done"), sem("cth"),
            sem("cact"), sem("cpw_mm"), sem("cpw_done"))
        bfree = [sem(f"bank_free{k}") for k in range(4)]
        csc_mm, csc_sub, csc_exp, csc_done, ctr_mm, ctr_done, cimp_mm, sel_done = (
            sem("csc_mm"), sem("csc_sub"), sem("csc_exp"), sem("csc_done"), sem("ctr_mm"), sem("ctr_done"),
            sem("cimp_mm"), sem("sel_done"))
        win_mm, win_sub, win_exp, win_l = sem("win_mm"), sem("win_sub"), sem("win_exp"), sem("win_l")
        ms_mm, mmax, mexp, mt_mm, mpt, mp_mm, om_done = (
            sem("ms_mm"), sem("mmax"), sem("mexp"), sem("mt_mm"), sem("mpt"), sem("mp_mm"), sem("om_done"))
        stat_mm, stat_done, comb_sub, comb_exp, wb_done, back_mm, back_done = (
            sem("stat_mm"), sem("stat_done"), sem("comb_sub"), sem("comb_exp"), sem("wb_done"), sem("back_mm"),
            sem("back_done"))
        pscaled, st_mm, spt, spt2, spv_mm, md_done, mpv_mm, fin_o, fin_mm, fin_done = (
            sem("pscaled"), sem("st_mm"), sem("spt"), sem("spt2"), sem("spv_mm"), sem("md_done"), sem("mpv_mm"),
            sem("fin_o"), sem("fin_mm"), sem("fin_done"))
        mixh, mixl = sem("mixh"), sem("mixl")
        xr_done = sem("xr_done")
        ln_mm, ln_d, ln_sq, lnv_mm, ln_std, ln_n, ln_h, ln_l = (
            sem("ln_mm"), sem("ln_d"), sem("ln_sq"), sem("lnv_mm"), sem("ln_std"), sem("ln_n"), sem("ln_h"), sem("ln_l"))
        relu_done, sq_done, hidh_done, hid_l_done = sem("relu_done"), sem("sq_done"), sem("hidh_done"), sem("hid_l_done")

        block = ctx.enter_context(nc.Block())

        @block.sync
        def _(sp_):
            def load_panel(i):
                if i >= NRAW:
                    sp_.wait_ge(l_done, i - NRAW + 1)
                if OUT0 <= i < OUT0 + NRAW:
                    sp_.wait_ge(spv_mm, i - OUT0 + 1)
                dst = raw[:, i % NRAW, :]
                if i == GATE_PANEL:
                    sp_.dma_start(dst[:, 0:KT * NGATE], a["w_gate"]).then_inc(raw_in[i % NRAW], 16)
                else:
                    sp_.dma_start(dst, a["panels"][i - (i > GATE_PANEL)]).then_inc(raw_in[i % NRAW], 16)

            ids = {}

            def page(b, n):
                return sp_.value_load(page_ids[0:1, b * PAGES + n:b * PAGES + n + 1])

            def load_unit(q):
                b = q // 4
                for p in range(4):
                    v = page(b, q % 4 * 4 + p)
                    sp_.dma_start(moba_ring[q % 4][:, p, :],
                                  a["moba_pages"][bass.ds(v, 1)].rearrange("a p n -> (a p) n")).then_inc(moba_in[q % 4], 16)

            for kind, n, *part in TL:
                if kind == "load_panel":
                    load_panel(n)
                elif kind == "load_x" and n == 0:
                    for k in range(KT):
                        sp_.dma_start(xres[:, k, :], a["xT"][:, k, :]).then_inc(xk_in[k], 16)
                        if k == 0:
                            load_panel(0)
                elif kind == "load_small":
                    sp_.dma_start(page_ids[:, :], a["page_table"]).then_inc(ids_in, 16)
                    sp_.dma_start(cst[:, :], a["consts"]).then_inc(small_in, 16)
                    sp_.dma_start(vec[:, :], a["vecs"]).then_inc(small_in, 16)
                elif kind == "load_w1":
                    sp_.dma_start(w1[:, :, :], a["w1"]).then_inc(w1_in, 16)
                    sp_.dma_start(sc[:, :, :, 0:CW - 1], a["state_convT"]).then_inc(state_in, 16)
                    sp_.dma_start(sp[:, :, :, 0:15], a["state_poolT"]).then_inc(state_in, 16)
                    sp_.wait_ge(ids_in, 16)
                elif kind == "load_nsa":
                    if n == 1:
                        sp_.wait_ge(cmp_mm, 1)
                    if n >= 2:
                        sp_.wait_ge(ssel_mm, n - 1)
                    for p in range(PAGES):
                        v = page(n, p)
                        sp_.dma_start(nsa_ring[:, n % 2, p, :],
                                      a["nsa_pages"][bass.ds(v, 1)].rearrange("a p n -> (a p) n")).then_inc(nsa_in[n % 2], 16)
                elif kind == "load_post":
                    sp_.wait_ge(ssel_mm, B)
                    sp_.wait_ge(kc_done, B + 1)
                    sp_.dma_start(winK[:, :, :], a["winK"]).then_inc(win_in, 16)
                    sp_.dma_start(winV[:, :, :, :], a["winV"]).then_inc(win_in, 16)
                    load_unit(2)
                    load_unit(3)
                elif kind == "out_early":
                    read(sp_, ("mm", PANEL_SLOT.index(S_PO + 1)))
                    sp_.dma_start(o["z_cmp"], zT[:, S_CMP, :]).then_inc(out_early, 16)
                    sp_.dma_start(o["pool_prompt"], zT[:, S_PO:S_PO + 2, T - 15:T]).then_inc(out_early, 16)
                elif kind == "out_conv":
                    sp_.wait_ge(glu_done, 2)
                    sp_.dma_start(o["conv_prompt"], zc[:, :, T:T + CW - 1]).then_inc(out_conv, 16)
                    sp_.dma_start(o["conv_sample"], sc[:, :, :, 1:CW]).then_inc(out_conv, 16)
                    sp_.wait_ge(pool_d, 1)
                    sp_.dma_start(o["pool_sample"], sp[:, :, :, 1:16]).then_inc(out_conv, 16)
                elif kind == "load_lo":
                    sp_.wait_ge(conv_done, 1)
                    sp_.wait_ge(cpw_mm, 2)
                    sp_.wait_ge(pool_mm, 2)
                    sp_.wait_ge(out_conv, 16 * 3)
                    load_unit(0)
                    load_unit(1)
                elif kind == "out_z":
                    read(sp_, ("mm", N_IN_PANELS - 1))
                    sp_.dma_start(o["z_ksel"], zT[0:HD, S_KSEL, :]).then_inc(out_z, 16)
                    sp_.dma_start(o["z_kwin"], zT[0:HD, S_KWIN, :]).then_inc(out_z, 16)
                    sp_.dma_start(o["z_v"], zT[:, S_V, :]).then_inc(out_z, 16)
                    sp_.dma_start(o["z_moba"], zT[:, S_MK:S_MK + 4, :]).then_inc(out_z, 16)
                elif kind == "zrow" and n == 0:
                    bank_read(sp_, 0, ("zrow", 0))
                    sp_.dma_start(o["win_sample"][:, T - 1, 0:HD], zs[:, 3, 0:HD]).then_inc(out_rows, 16)
                    sp_.dma_start(o["win_sample"][:, T - 1, HD:P], zs[:, 2, HD:P]).then_inc(out_rows, 16)
                elif kind == "mp" and n + 4 < MU:
                    sp_.wait_ge(mp_mm, n + 1)
                    load_unit(n + 4)
                elif kind == "selv" and n % 2 == 0:
                    if n == 0:
                        sp_.wait_ge(mm_done, N_IN_PANELS)
                    for p in range(4 * n, 4 * n + 4):
                        v = page(p // PAGES, p % PAGES)
                        sp_.dma_start(selV[p // PAGES][:, p % PAGES, :],
                                      a["selv_pages"][bass.ds(v, 1)].rearrange("a p n -> (a p) n")).then_inc(selv_in, 16)
                elif kind == "stat" and n == 0:
                    sp_.wait_ge(mp_mm, MU - 3)
                    for p in range(PAGES):
                        v = page(B - 1, p)
                        sp_.dma_start(selV[B - 1][:, p, :],
                                      a["selv_pages"][bass.ds(v, 1)].rearrange("a p n -> (a p) n")).then_inc(selv_in, 16)
                elif kind == "load_x" and n == 1:
                    sp_.wait_ge(st_mm, B)
                    sp_.dma_start(xres[:, :, :], a["xT"]).then_inc(x_in, 16)
                elif kind == "ln" and n == 0:
                    sp_.dma_start(o["win_sample"][:, 0:T - 1, :], a["state_win"][:, 1:T, :]).then_inc(out_state, 16)
                elif kind == "ln" and n == 1:
                    for k in range(KT):
                        sp_.wait_ge(ln_n, KT + k + 1)
                        sp_.dma_start(o["y"][:, k, :], xres[:, k, :]).then_inc(out_y, 16)
            sp_.wait_ge(out_state, 16)
            sp_.wait_ge(out_z, 16 * 4)
            sp_.wait_ge(out_early, 32)
            sp_.wait_ge(out_conv, 48)
            sp_.wait_ge(out_rows, 32)
            sp_.wait_ge(out_y, 16 * KT)

        @block.tensor
        def _(pe):
            mm = nc.tensor.matmul

            def acc_wait(key):
                n = ACC_NO[key]
                last = [m for m in range(n) if PAIR[m] == PAIR[n]]
                if last:
                    read(pe, ACC[last[-1]])
                if n >= NACC1 and n < NACC1 + 2:
                    for k in range(4):
                        pe.wait_ge(bfree[k], len(USES[k]))

            def panel(i, q=0, parts=1):
                key = ("mm", i)
                out = acc(key)
                if q == 0:
                    acc_wait(key)
                    pe.wait_ge(l_done, i + 1)
                M = P
                if i < N_IN_PANELS:
                    xh, xl = opH, opL
                    if i == GATE_PANEL:
                        M = NGATE
                elif i < FF0:
                    xh, xl = opH, opL
                else:
                    kind, g, n = FFN[i - FF0]
                    if kind == "up":
                        xh, xl = opH, opL
                    else:
                        xh, xl = hidH[g % 2], hidL[g % 2]
                        pe.wait_ge(hid_l_done, (g + 1) * KT)
                s = i % NW
                order = MIX_ORDER if OUT0 <= i < FF0 else range(KT)
                for t, k in list(enumerate(order))[q * KT // parts:(q + 1) * KT // parts]:
                    if i == OUT0:
                        pe.wait_ge(mixl, t + 1)
                    if i == 0:
                        pe.wait_ge(xl_done, k + 1)
                    if i == FF0:
                        pe.wait_ge(ln_l, k + 1)
                    if M == P:
                        a_h, a_l = wH[:, s, k, :], wL[:, s, k, :]
                    else:
                        a_h = wH[:, s].rearrange("p a b -> p (a b)")[:, k * NGATE:(k + 1) * NGATE]
                        a_l = wL[:, s].rearrange("p a b -> p (a b)")[:, k * NGATE:(k + 1) * NGATE]
                    for j, (w, x) in enumerate(((a_h, xh), (a_h, xl), (a_l, xh))):
                        for hf in range(2):
                            last = mm(out[0:M, hf, 0:HALF], w, x[:, k, hf * HALF:(hf + 1) * HALF],
                                      start=(t == 0 and j == 0), stop=(t == KT - 1 and j == 2))
                if q == parts - 1:
                    last.then_inc(mm_done, 1)

            def compress(rhs0, rhs1, n0, n1):
                for half, rhs, n in ((0, rhs0, n0), (1, rhs1, n1)):
                    for r in range(16):
                        last = mm(psum[:, 4, half * 256:half * 256 + n], w1[:, half * 16 + r, :], rhs(r),
                                  start=(r == 0), stop=(r == 15))
                last.then_inc(cmp_mm, 1)

            def cmp_kv(idx, n):
                pe.wait_ge(hid_done, idx + 1)
                if idx:
                    pe.wait_ge(kc_done, idx)
                mm(psum[0:HD, 5, 0:n], vec[0:HD, V_W2:V_W2 + HD], hu[0:HD, 0, 0:n], start=True, stop=True)
                mm(psum[0:n, 5, 256:256 + HD], hu[HD:P, 0, 0:n], vec[HD:P, V_W2:V_W2 + HD], start=True, stop=True).then_inc(kv_mm, 1)

            def sel_scores(b):
                if b >= 2:
                    pe.wait_ge(ssel_sub, b - 1)
                for j in range(4):
                    half, pg = j // 2, j % 2
                    last = mm(psum[32 * j:32 * j + 32, 6 + b % 2, :], (QNa, QNb)[half][:, b, :],
                              nsa_ring[:, b % 2, pg * 8:pg * 8 + 8, P:192], start=True, stop=True, skip_group_check=True)
                last.then_inc(ssel_mm, 1)

            def qk(u):
                kind, h, i = UNITS[u]
                if u >= 2:
                    pe.wait_ge(exp_done, u - 1)
                elif u == 0:
                    pe.wait_ge(gate_t, 1)
                else:
                    pe.wait_ge(vn_done, 1)
                base = HD * (h % 2)
                n = NCMP_P if kind == "cmp" else P * (i + 1)
                if kind == "moba":
                    q, k = zT[base:base + HD, S_MQ + h // 2, i * P:(i + 1) * P], zT[base:base + HD, S_MK + h // 2, 0:n]
                else:
                    q = zT[base:base + HD, S_Q + h // 2, i * P:(i + 1) * P]
                    k = kcp[base:base + HD, 0:n] if kind == "cmp" else zT[base:base + HD, S_KSEL if kind == "sel" else S_KWIN, 0:n]
                mm(psum[:, 4 + u % 2, 0:n], q, k, start=True, stop=True).then_inc(qk_done, 1)

            def tr(u):
                kind, h, i = UNITS[u]
                pe.wait_ge(scaled, u + 1)
                if u:
                    pe.wait_ge(pt_done, u)
                if kind == "cmp":
                    nc.tensor.transpose(psum[0:NCMP_P, 6, 0:P], PB[:, u % 2, 0:NCMP_P], ident).then_inc(tr_done, 1)
                    return
                for j in range(i + 1):
                    last = nc.tensor.transpose(psum[:, 6, j * P:(j + 1) * P], PB[:, u % 2, j * P:(j + 1) * P], ident)
                last.then_inc(tr_done, 1)

            def pv(u):
                kind, h, i = UNITS[u]
                pe.wait_ge(pt_done, u + 1)
                if kind == "moba":
                    bank_read(pe, h // 2, ("vrow", h // 2))
                g = GROUP[u]
                if FIRST[u] and g >= 2:
                    pe.wait_ge(o_done, g - 1)
                base = HD * (h % 2)
                out = psum[base:base + HD, 7, 0:P]
                if kind == "cmp":
                    last = mm(out, vcp[0:NCMP_P, :], PT[0:NCMP_P, u % 2, 0:P], start=True, stop=False, skip_group_check=True)
                else:
                    src, off = {"sel": (0, 0), "win": (0, HD), "moba": (1 + h // 2, base)}[kind]
                    for j in range(i + 1):
                        last = mm(out, Vn[:, src, j, off:off + HD], PT[:, u % 2, j * P:(j + 1) * P],
                                  start=(FIRST[u] and j == 0), stop=(LAST[u] and j == i), skip_group_check=True)
                last.then_inc(pv_done, 1)

            def bank(k, step):
                n = nth(k, step)
                if n:
                    pe.wait_ge(bfree[k], n)
                else:
                    read(pe, ACC[max(m for m in range(NACC1) if PAIR[m] == k // 2)])

            for step in TL:
                kind, n, *part = step
                if kind == "mm":
                    panel(n, *part)
                elif kind == "cmpp":
                    pe.wait_ge(xc_done, 1)
                    pe.wait_ge(w1_in, 16)
                    compress(lambda r: xc[:, r, :], lambda r: xc[:, r, :], 34, 34)
                elif kind == "kv":
                    cmp_kv(n, NCMP if n else NCMP_P)
                elif kind == "nsa":
                    pe.wait_ge(nsa_in[n % 2], 16 * PAGES * (n // 2 + 1))
                    pe.wait_ge(cmp_u, n + 1)
                    rhs = lambda r: nsa_ring[:, n % 2, :, r * 8:r * 8 + 8]
                    compress(rhs, rhs, NCHUNK, NCHUNK)
                    if n == 0:
                        pe.wait_ge(qn_done, 1)
                    sel_scores(n)
                elif kind == "zcols":
                    read(pe, ("mm", PANEL_SLOT.index(S_V)))
                    pe.wait_ge(ssel_sub, B)
                    pe.wait_ge(kc_done, B + 1)
                    pe.wait_ge(cmp_u, B + 1)
                    for t in range(QT):
                        last = nc.tensor.transpose(psum[:, 4, t * NGATE:(t + 1) * NGATE], zT[0:NGATE, S_GATE, t * P:(t + 1) * P], ident[0:NGATE, 0:NGATE])
                    last.then_inc(zc_mm, 1)
                    for t in range(QT):
                        last = nc.tensor.transpose(psum[:, 5, t * P:(t + 1) * P], zT[:, S_V, t * P:(t + 1) * P], ident)
                    last.then_inc(zc_mm, 1)
                elif kind == "zrow":
                    bank(n % 2, step)
                    read(pe, ("mm", max(PANEL_SLOT.index(s - (s == S_KWIN)) for s in ROW_SLOTS[n])))
                    for j, slot in enumerate(ROW_SLOTS[n]):
                        m = NGATE if slot == S_GATE else P
                        last = nc.tensor.transpose(psum[0:B, n % 2, j * P:j * P + m], zT[0:m, slot, T:NT], ident[0:m, 0:m])
                    last.then_inc(zr_mm, 1)
                elif kind == "vrow":
                    bank(n % 2, step)
                    read(pe, ("mm", PANEL_SLOT.index(S_MV + n)))
                    for t in range(QT):
                        last = nc.tensor.transpose(psum[:, n % 2, t * P:(t + 1) * P], zT[:, S_MV + n, t * P:(t + 1) * P], ident)
                    last.then_inc(zc_mm, 1)
                elif kind == "att":
                    if n < NU:
                        qk(n)
                    if 2 <= n < NU + 2:
                        tr(n - 2)
                    if n >= 3:
                        pv(n - 3)
                elif kind == "pool":
                    acc_wait(step)
                    pe.wait_ge(pool_d, n + 1)
                    for hf in range(2):
                        last = mm(acc(step)[:, hf, 0:HALF], vec[:, V_PO + n * P:V_PO + (n + 1) * P], pb[:, hf * HALF:(hf + 1) * HALF],
                                  start=True, stop=True)
                    last.then_inc(pool_mm, 1)
                elif kind in ("cmean", "cvar"):
                    acc_wait(step)
                    if kind == "cmean":
                        pe.wait_ge(conv_done, 1)
                    else:
                        pe.wait_ge(csq_done, 1)
                    for hf in range(2):
                        for t in range(2):
                            x = yc[:, t, hf * HALF:(hf + 1) * HALF] if kind == "cmean" else zT[:, S_CG + t, hf * HALF:(hf + 1) * HALF]
                            last = mm(acc(step)[:, hf, 0:HALF], mean256[:, :], x, start=(t == 0), stop=(t == 1))
                    last.then_inc(cm_mm if kind == "cmean" else cv_mm, 1)
                elif kind == "cpw":
                    pe.wait_ge(cact, 1)
                    for m in range(2):
                        acc_wait(("cpw", m))
                        for hf in range(2):
                            for t in range(2):
                                last = mm(acc(("cpw", m))[:, hf, 0:HALF], vec[:, V_PW + t * 256 + m * P:V_PW + t * 256 + (m + 1) * P],
                                          yc[:, t, hf * HALF:(hf + 1) * HALF], start=(t == 0), stop=(t == 1))
                        last.then_inc(cpw_mm, 1)
                elif kind == "csc":
                    bank(0, step)
                    pe.wait_ge(kc_done, B + 1)
                    for b in range(B):
                        last = mm(psum[32 * (b % 4):32 * (b % 4) + 32, 0, b // 4 * P:b // 4 * P + NCMP], QNa[0:HD, b, :],
                                  kcT[:, b, 0:NCMP], start=True, stop=True, skip_group_check=True)
                    last.then_inc(csc_mm, 1)
                elif kind == "ctr":
                    bank(1, step)
                    pe.wait_ge(csc_done, 1)
                    for c in range(2):
                        last = nc.tensor.transpose(psum[0:NCMP, 1, c * P:(c + 1) * P], Pc[:, c, 0:NCMP], ident)
                    last.then_inc(ctr_mm, 1)
                elif kind == "cimp":
                    bank(0, step)
                    bank(1, step)
                    pe.wait_ge(ctr_done, 1)
                    mm(psum[0:B, 0, 0:NSELB], ps_small[0:NCMP, 16:16 + B], cst[0:NCMP, C_COVER:C_COVER + NSELB], start=True, stop=True)
                    for b in range(B):
                        c, j = b // 4, b % 4
                        last = mm(psum[32 * j:32 * j + 32, 1, c * HD:(c + 1) * HD], PcT[0:NCMP, c, 32 * j:32 * j + 32],
                                  vc[0:NCMP, b, :], start=True, stop=True, skip_group_check=True)
                    last.then_inc(cimp_mm, 1)
                elif kind == "win":
                    bank(0, step)
                    bank(1, step)
                    pe.wait_ge(win_in, 32)
                    for b in range(B):
                        for j in range(4):
                            half, g = j // 2, j % 2
                            last = mm(psum[32 * j:32 * j + 32, b // 4, b % 4 * P:(b % 4 + 1) * P], (QNa, QNb)[half][:, b, :],
                                      winK[:, b, g * P:(g + 1) * P], start=True, stop=True, skip_group_check=True)
                    last.then_inc(win_mm, 1)
                elif kind == "mu":
                    u = n
                    if u < MU:
                        bank(0, step)
                        pe.wait_ge(moba_in[u % 4], 64 * (u // 4 + 1))
                        if u == 0:
                            pe.wait_ge(qm_done, 1)
                        for hp in range(2):
                            for j in range(4):
                                last = mm(psum[32 * j:32 * j + 32, 0, 0:P], QM[:, hp, u // 4, :],
                                          moba_ring[u % 4][:, j, hp * P:(hp + 1) * P], start=(hp == 0), stop=(hp == 1),
                                          skip_group_check=True)
                        last.then_inc(ms_mm, 1)
                    if u >= 1:
                        bank(1, step)
                        bank_read(pe, 0, ("mu", u - 1))
                        nc.tensor.transpose(psum[:, 1, 0:P], Pm[:, (u - 1) % 2, :], ident).then_inc(mt_mm, 1)
                elif kind == "mp":
                    bank(1, step)
                    for j in range(4):
                        last = mm(psum[32 * j:32 * j + 32, 1, 0:256], PTm2[:, n % 2, 32 * j:32 * j + 32],
                                  moba_ring[n % 4][:, j, 256:512], start=True, stop=True, skip_group_check=True)
                    last.then_inc(mp_mm, 1)
                elif kind == "stat":
                    for k in ((0, 1, 2, 3), (0, 1, 2), (0,))[n]:
                        bank(k, step)
                    if n == 0:
                        pe.wait_ge(win_l, 1)
                    for s, src in enumerate(stats[n]):
                        last = nc.tensor.transpose(psum[0:B, s // 4, s % 4 * P:(s % 4 + 1) * P], src, ident)
                    last.then_inc(stat_mm, 1)
                elif kind == "back":
                    bank(0, step)
                    bank(1, step)
                    pe.wait_ge(wb_done, 1)
                    for s in range(13):
                        nc.tensor.transpose(psum[:, 0, s * B:(s + 1) * B], WB[:, s, :], ident[0:B, 0:B])
                    for c in range(2):
                        last = mm(psum[:, 1, c:c + 1], gdiag[:, 4 * c:4 * c + 4, :], onesc[0:B, :], start=True, stop=True)
                    last.then_inc(back_mm, 1)
                elif kind == "spv":
                    if n < B:
                        for k in range(3):
                            bank(k, step)
                        pe.wait_ge(pscaled, n + 1)
                        for p in range(8):
                            nc.tensor.transpose(psum[0:HD, p // 4, p % 4 * P:(p % 4 + 1) * P], Psel[:, n, p * HD:(p + 1) * HD], ident)
                        nc.tensor.transpose(psum[:, 2, 0:P], Pwin[:, n, :], ident).then_inc(st_mm, 1)
                    if n == 0:
                        pe.wait_ge(bfree[3], len(USES[3]))
                        mm(psum[:, 3, 0:P], zeros[:, :], ident, start=True, stop=False, skip_group_check=True)
                        continue
                    if n == 1:
                        pe.wait_ge(selv_in, 16 * PAGES * B)
                    b = n - 1
                    c, j = b // 4, b % 4
                    out = psum[32 * j:32 * j + H, 3, c * HD:(c + 1) * HD]
                    V = selV[b]
                    for k in range(3):
                        bank_read(pe, k, ("spv", b))
                    for p in range(PAGES):
                        mm(out, PTs[:, b % 2, p // 8, p % 8, :], V[:, p, :], start=False, stop=False, skip_group_check=True)
                    for w in range(4):
                        mm(out, PTw[:, b % 2, w, :], winV[:, b, w, :], start=False, stop=False, skip_group_check=True)
                    mm(out, wnew[:, 0, b, :], zs[:, 2, 0:HD], start=False, stop=False, skip_group_check=True)
                    mm(out, wnew[:, 2, b, :], zs[:, 2, HD:P], start=False, stop=(b == B - 1), skip_group_check=True).then_inc(spv_mm, 1)
                elif kind == "mpv":
                    bank(1, step)
                    bank(2, step)
                    pe.wait_ge(md_done, 1)
                    mm(psum[:, 2, 0:P], zeros[:, :], ident, start=True, stop=False, skip_group_check=True)
                    for pos in range(4):
                        for b in range(B):
                            c, j = b // 4, b % 4
                            mm(psum[32 * j:32 * j + H, 2, c * HD:(c + 1) * HD], Wd[:, b, pos, :], OM[:, b * 4 + pos, :],
                               start=False, stop=(pos == 3 and b == B - 1), skip_group_check=True)
                    mm(psum[:, 1, :], zeros[:, :], OM[:, 0:8, :], start=True, stop=False, skip_group_check=True)
                    for b in range(B):
                        c, j = b // 4, b % 4
                        last = mm(psum[32 * j:32 * j + H, 1, c * 256:(c + 1) * 256], wnew[:, 1, b, :], zs[:, 10:12, :],
                                  start=False, stop=(b == B - 1), skip_group_check=True)
                    last.then_inc(mpv_mm, 1)
                elif kind == "fin":
                    bank(0, step)
                    bank(1, step)
                    pe.wait_ge(fin_o, 1)
                    bank_read(pe, 2, ("mpv", 0))
                    for k, src in ((0, On), (1, Om)):
                        for c in range(2):
                            last = nc.tensor.transpose(psum[0:HD, k, c * P:(c + 1) * P], src[:, c, :], ident)
                    last.then_inc(fin_mm, 1)
                elif kind == "mean":
                    k = part[0]
                    m = ("mm", (OUT0 if n == 0 else N_PANELS - KT) + k)
                    read(pe, m)
                    if n == 0 and k == 0:
                        pe.wait_ge(exp_done, NU)
                        pe.wait_ge(pt_done, NU)
                        pe.wait_ge(o_done, NGROUP)
                    for hf in range(2):
                        last = mm(psum[:, 4 + hf, 0:HALF], mean1024[:, :], xres[:, k, hf * HALF:(hf + 1) * HALF],
                                  start=(k == 0), stop=(k == KT - 1))
                    if k == KT - 1:
                        last.then_inc(ln_mm, 1)
                elif kind == "ln":
                    for k in range(KT):
                        pe.wait_ge(ln_sq, n * KT + k + 1)
                        for hf in range(2):
                            last = mm(psum[:, 6 + hf, 0:HALF], mean1024[:, :], sqb[:, k % 2, hf * HALF:(hf + 1) * HALF],
                                      start=(k == 0), stop=(k == KT - 1))
                        last.then_inc(lnv_mm, 1)

        @block.scalar
        def _(act):
            fn = nc.scalar.activation
            steps = [0]

            def chain(ins):
                steps[0] += 1
                ins.then_inc(ach, 1)
                act.wait_ge(ach, steps[0])

            def zview(ap):
                return ap.rearrange("p (a b) -> p a b", a=2)

            up_no = 0
            for step in TL:
                kind, n, *part = step
                if kind == "xsplit":
                    act.wait_ge(xk_in[n], 16)
                    fn(opH[:, n, :], xres[:, n, :], ACT.Copy).then_inc(xh_done, 1)
                elif kind == "split":
                    act.wait_ge(raw_in[n % NRAW], 16 * (n // NRAW + 1))
                    if n >= NW:
                        act.wait_ge(mm_done, n - NW + 1)
                    if n in (OUT0, OUT0 + 1):
                        act.wait_ge(spv_mm, B - 1)
                    m = KT * (NGATE if n == GATE_PANEL else P)
                    fn(wH[:, n % NW].rearrange("p a b -> p (a b)")[:, 0:m], raw[:, n % NRAW, 0:m], ACT.Copy).then_inc(h_done, 1)
                elif kind == "evac" and n < N_IN_PANELS:
                    act.wait_ge(mm_done, n + 1)
                    slot, src = PANEL_SLOT[n], acc(("mm", n))[:, :, 0:HALF]
                    if slot in (S_Q, S_Q + 1, S_MQ, S_MQ + 1):
                        last = fn(zview(zT[:, slot, :]), src, ACT.Copy, scale=HD ** -0.5)
                    elif slot in (S_CA, S_CA + 1):
                        last = fn(zview(zT[:, slot, :]), src, ACT.Copy, scale=0.5)
                    elif slot in (S_CG, S_CG + 1):
                        last = fn(zview(zT[:, slot, :]), src, ACT.Tanh, scale=0.5)
                    elif slot == S_GATE:
                        last = fn(zview(zT[0:NGATE, slot, :]), src[0:NGATE], ACT.Copy)
                    elif slot == S_KSEL:
                        for lo in (0, HD):
                            fn(zview(zT[lo:lo + HD, S_KSEL, :]), src[0:HD], ACT.Copy)
                            last = fn(zview(zT[lo:lo + HD, S_KWIN, :]), src[HD:P], ACT.Copy)
                    else:
                        last = fn(zview(zT[:, slot, :]), src, ACT.Copy)
                    last.then_inc(acc_read[0], 1)
                elif kind in ("cmpp", "nsa"):
                    idx = 0 if kind == "cmpp" else n + 1
                    m = NCMP if idx else NCMP_P
                    act.wait_ge(cmp_mm, idx + 1)
                    if idx == 0:
                        act.wait_ge(small_in, 32)
                        chain(fn(hu[:, 2, 0:1], psum[:, 4, 32:33], ACT.Copy))
                        chain(fn(bias[:, :], psum[:, 4, 256 + 33:256 + 34], ACT.Identity, bias=hu[:, 2, 0:1]))
                    else:
                        act.wait_ge(hid_done, idx)
                    fn(hu[:, 1, 0:m], psum[:, 4, 257:257 + m], ACT.Identity, bias=bias[:, :]).then_inc(cmp_t1, 1)
                    act.wait_ge(cmp_u, idx + 1)
                    fn(hu[:, 1, 0:m], hu[:, 2, 0:m], ACT.Tanh, scale=0.5).then_inc(cmp_th, 1)
                    if kind == "nsa":
                        act.wait_ge(ssel_sub, n + 1)
                        fn(Psel[:, n, :], Psel[:, n, :], ACT.Exp).then_inc(ssel_exp, 1)
                elif kind == "kv":
                    act.wait_ge(kv_mm, n + 1)
                    if n == 0:
                        fn(kcp[0:HD, 0:NCMP_P], psum[0:HD, 5, 0:NCMP_P], ACT.Copy, scale=0.5)
                        fn(kcp[HD:P, 0:NCMP_P], psum[0:HD, 5, 0:NCMP_P], ACT.Copy, scale=0.5)
                        fn(vcp[0:NCMP_P, :], psum[0:NCMP_P, 5, 256:256 + HD], ACT.Copy, scale=0.5).then_inc(kc_done, 1)
                    else:
                        fn(kcT[:, n - 1, 0:NCMP], psum[0:HD, 5, 0:NCMP], ACT.Copy, scale=0.5)
                        fn(vc[0:NCMP, n - 1, :], psum[0:NCMP, 5, 256:256 + HD], ACT.Copy, scale=0.5).then_inc(kc_done, 1)
                elif kind == "zcols":
                    act.wait_ge(zc_mm, 1)
                    fn(gT[:, :, :], psum[:, 4, 0:QT * NGATE].rearrange("p (a b) -> p a b", a=QT), ACT.Tanh, scale=0.5).then_inc(gate_t, 1)
                    act.wait_ge(zc_mm, 2)
                    fn(Vn[:, 0, :, :], psum[:, 5, :].rearrange("p (a b) -> p a b", a=QT), ACT.Copy).then_inc(vn_done, 1)
                elif kind == "zrow":
                    act.wait_ge(zr_mm, n + 1)
                    if n == 0:
                        fn(zs[:, 0, 0:NGATE], psum[0:B, 0, 0:NGATE], ACT.Copy)
                        fn(zs[:, 1:4, :], psum[0:B, 0, P:512].rearrange("p (a b) -> p a b", a=3), ACT.Copy).then_inc(bfree[0], 1)
                    else:
                        fn(zs[:, 4 * n:4 * n + 4, :], psum[0:B, n % 2, :].rearrange("p (a b) -> p a b", a=4), ACT.Copy).then_inc(bfree[n % 2], 1)
                elif kind == "vrow":
                    act.wait_ge(zc_mm, n + 3)
                    fn(Vn[:, n + 1, :, :], psum[:, n % 2, :].rearrange("p (a b) -> p a b", a=QT), ACT.Copy).then_inc(bfree[n % 2], 1)
                elif kind == "selv" and n % 2 == 1:
                    if n == 1:
                        act.wait_ge(ids_in, 16)
                        act.wait_ge(mm_done, N_IN_PANELS)
                    for p in range(n * 4, n * 4 + 4):
                        v = act.value_load(page_ids[0:1, p:p + 1])
                        act.dma_start(selV[p // PAGES][:, p % PAGES, :],
                                      a["selv_pages"][bass.ds(v, 1)].rearrange("a p n -> (a p) n")).then_inc(selv_in, 16)
                elif kind == "att":
                    if n < NU:
                        u = n
                        ukind, h, i = UNITS[u]
                        m = NCMP_P if ukind == "cmp" else P * (i + 1)
                        act.wait_ge(max_done, u + 1)
                        if u >= 2:
                            act.wait_ge(tr_done, u - 1)
                            act.wait_ge(r_done, u - 1)
                        fn(PB[:, u % 2, 0:m], psum[:, 4 + u % 2, 0:m], ACT.Exp, bias=ps_small[:, u % 2:u % 2 + 1],
                           accum_out=ps_small[:, 4 + u % 2:5 + u % 2]).then_inc(exp_done, 1)
                    if 2 <= n < NU + 2:
                        u = n - 2
                        ukind, h, i = UNITS[u]
                        act.wait_ge(tr_done, u + 1)
                        if u >= 2:
                            act.wait_ge(pv_done, u - 1)
                        if ukind == "cmp":
                            fn(PT[0:NCMP_P, u % 2, 0:P], psum[0:NCMP_P, 6, 0:P], ACT.Copy).then_inc(pt_done, 1)
                        else:
                            fn(PT[:, u % 2, 0:P * (i + 1)], psum[:, 6, 0:P * (i + 1)], ACT.Copy).then_inc(pt_done, 1)
                    if n >= 3 and LAST[n - 3]:
                        u = n - 3
                        ukind, h, i = UNITS[u]
                        base = HD * (h % 2)
                        slot = (S_MQ if ukind == "moba" else S_Q) + h // 2
                        act.wait_ge(pv_done, u + 1)
                        fn(zT[base:base + HD, slot, i * P:(i + 1) * P], psum[base:base + HD, 7, 0:P], ACT.Copy).then_inc(o_done, 1)
                elif kind == "pool":
                    act.wait_ge(pool_mm, n + 1)
                    act.wait_ge(out_early, 32)
                    fn(zview(zT[:, S_PO + n, :]), acc(step)[:, :, 0:HALF], ACT.Copy, scale=vec[:, V_PS + n:V_PS + n + 1]).then_inc(acc_read[0], 1)
                elif kind == "cmean":
                    read(act, step)
                    for t in range(2):
                        last = fn(zT[:, S_CG + t, :], yc[:, t, :], ACT.Square)
                    last.then_inc(csq_done, 1)
                elif kind == "cvar":
                    act.wait_ge(cv_mm, 1)
                    act.wait_ge(const_done, NCONSTS)
                    fn(zview(zT[:, S_CG, :]), acc(step)[:, :, 0:HALF], ACT.Sqrt, bias=epsc).then_inc(acc_read[0], 1)
                    act.wait_ge(cn_done, 1)
                    fn(zT[:, S_CG:S_CG + 2, :], yc[:, :, :], ACT.Tanh, scale=0.5).then_inc(cth, 1)
                elif kind == "cpw":
                    for m in range(2):
                        act.wait_ge(cpw_mm, m + 1)
                        fn(zview(zT[:, S_CA + m, :]), acc(("cpw", m))[:, :, 0:HALF], ACT.Copy, scale=0.5).then_inc(acc_read[0], 1)
                elif kind == "csc":
                    bank_read(act, 0, step)
                    fn(Pc[:, :, 0:NCMP], Pc[:, :, 0:NCMP], ACT.Exp).then_inc(csc_exp, 1)
                elif kind == "cimp":
                    act.wait_ge(cimp_mm, 1)
                    fn(oc[:, :, :], psum[:, 1, 0:P].rearrange("p (a b) -> p a b", a=2), ACT.Copy).then_inc(bfree[1], 1)
                elif kind == "win":
                    bank_read(act, 0, step)
                    bank_read(act, 1, step)
                    fn(Pwin[:, :, :], Pwin[:, :, :], ACT.Exp).then_inc(win_exp, 1)
                elif kind == "mu":
                    u = n
                    if u < MU:
                        act.wait_ge(mmax, u + 1)
                        if u == 0:
                            act.wait_ge(out_early, 32)
                        if u >= 2:
                            act.wait_ge(mt_mm, u - 1)
                        fn(Pm[:, u % 2, :], psum[:, 0, 0:P], ACT.Exp, bias=nmM[:, u:u + 1],
                           accum_out=lM[:, u:u + 1]).then_inc(bfree[0], 1)
                elif kind == "comb" and n == 0:
                    act.wait_ge(comb_sub, 1)
                    fn(sm[:, 0:NGATE], zs[:, 0, 0:NGATE], ACT.Tanh, scale=0.5)
                    fn(eb[:, 2].rearrange("p h s -> p (h s)"), eb[:, 2].rearrange("p h s -> p (h s)"), ACT.Exp).then_inc(comb_exp, 1)
                elif kind == "back":
                    act.wait_ge(back_mm, 1)
                    fn(Wt[:, :, :], psum[:, 0, 0:13 * B].rearrange("p (s b) -> p s b", b=B), ACT.Copy).then_inc(bfree[0], 1)
                    fn(g0, psum[:, 1, 0:2], ACT.Copy).then_inc(bfree[1], 1)
                elif kind == "spv" and n < B:
                    act.wait_ge(st_mm, n + 1)
                    if n >= 2:
                        act.wait_ge(spv_mm, n - 1)
                    fn(PTw[:, n % 2, :, :], psum[:, 2, 0:P].rearrange("p (j h) -> p j h", j=4)[:, :, 0:H], ACT.Copy).then_inc(bfree[2], 1)
                elif kind == "fin":
                    act.wait_ge(fin_mm, 1)
                    for h in range(H):
                        base = HD * (h % 2)
                        last = fn(zT[base:base + HD, S_Q + h // 2, T:NT],
                                  psum[0:HD, 0, 0:256].rearrange("p (b x) -> p b x", x=32)[:, :, h], ACT.Copy)
                    last.then_inc(bfree[0], 1)
                elif kind == "msplit":
                    if n == 0:
                        act.wait_ge(mm_done, N_IN_PANELS)
                        read(act, ACC[NACC1 - 1])
                    if n == 4:
                        act.wait_ge(o_done, NGROUP)
                        bank_read(act, 0, ("fin", 0))
                        bank_read(act, 1, ("fin", 0))
                    k = MIX_ORDER[n]
                    fn(opH[:, k, :], zT[:, MIX_SLOT[k], :], ACT.Copy).then_inc(mixh, 1)
                elif kind == "evac" and n >= FF0 and FFN[n - FF0][0] == "up":
                    g, m = FFN[n - FF0][1:]
                    act.wait_ge(mm_done, n + 1)
                    if up_no >= 2:
                        act.wait_ge(hid_l_done, up_no - 1)
                    chain_to = nread(("mm", n))
                    fn(zview(relu[:, up_no % 2, :]), acc(("mm", n))[:, :, 0:HALF], ACT.Relu).then_inc(acc_read[0], 1)
                    act.wait_ge(acc_read[0], chain_to)
                    if m == 0 and g >= 2:
                        act.wait_ge(mm_done, FF0 + FFN.index(("down", g - 2, KT - 1)) + 1)
                    fn(hidH[g % 2][:, m, :], relu[:, up_no % 2, :], ACT.Square).then_inc(hidh_done, 1)
                    up_no += 1
                elif kind == "ln":
                    for k in range(KT):
                        act.wait_ge(ln_d, n * KT + k + 1)
                        if k >= 2:
                            act.wait_ge(lnv_mm, n * KT + k - 1)
                        fn(sqb[:, k % 2, :], xres[:, k, :], ACT.Square).then_inc(ln_sq, 1)
                    act.wait_ge(lnv_mm, (n + 1) * KT)
                    fn(zview(std[:, :]), psum[:, 6:8, 0:HALF], ACT.Sqrt, bias=epsc).then_inc(ln_std, 1)
                    for k in range(KT):
                        act.wait_ge(vln, n * KT + k + 1)
                        b = vec[:, (V_B1, V_B2)[n] + k:(V_B1, V_B2)[n] + k + 1]
                        if n == 0:
                            fn(opH[:, k, :], lnt[:, k % 4, :], ACT.Identity, bias=b).then_inc(ln_h, 1)
                        else:
                            fn(xres[:, k, :], lnt[:, k % 4, :], ACT.Identity, bias=b).then_inc(ln_n, 1)

        @block.gpsimd
        def _(pool):
            steps = [0]

            def chain(ins):
                steps[0] += 1
                ins.then_inc(pch, 1)
                pool.wait_ge(pch, steps[0])

            for buf, value in ((mean1024[:, :], 1.0 / D), (mean256[:, :], 1.0 / 256), (onesc, 1.0), (epsc, EPS),
                               (QNa[:, :, :], 0.0), (QNb[:, :, :], 0.0), (QM[:, :, :, :], 0.0)):
                nc.gpsimd.memset(buf, value).then_inc(const_done, 1)
            up_no = 0
            for kind, n, *part in TL:
                if kind == "pdiff":
                    read(pool, ("mm", PANEL_SLOT.index(S_PO + 1)))
                    tt, copy = nc.gpsimd.tensor_tensor, nc.gpsimd.tensor_copy
                    x = zT[:, S_PO + n, :]
                    if n == 0:
                        pool.wait_ge(small_in, 32)
                        pool.wait_ge(state_in, 32)
                        for t in range(2):
                            copy(sp[:, t, :, 15], zT[:, S_PO + t, T:NT])
                    else:
                        pool.wait_ge(pool_mm, 1)

                    def double(dst, src, w):
                        copy(dst[:, 0:w], src[:, 0:w])
                        chain(tt(dst[:, w:T], src[:, w:T], src[:, 0:T - w], ALU.add))

                    double(pa, x, 1)
                    double(pb, pa, 2)
                    if n == 1:
                        double(pa, pb, 4)
                        double(pb, pa, 8)
                    w0, w1_ = ((2, 4), (8, 16))[n]
                    for lo, s in ((0, pa), (HD, pb)):
                        q = slice(lo, lo + HD)
                        tt(pb[q, 0:16], s[q, 0:16], cst[q, C_INVC + 16 * n:C_INVC + 16 * n + 16], ALU.mult)
                        chain(nc.gpsimd.tensor_scalar(pb[q, 16:T], s[q, 16:T], cst[q, C_INVW + n:C_INVW + n + 1], None, ALU.mult))
                    for lo, w in ((0, w0), (HD, w1_)):
                        rows = slice(lo, lo + HD)
                        chain(copy(pb[rows, T:NT], sp[rows, n, :, 15]))
                        for k in range(1, w):
                            chain(tt(pb[rows, T:NT], pb[rows, T:NT], sp[rows, n, :, 15 - k], ALU.add))
                    chain(nc.gpsimd.tensor_scalar(pb[:, T:NT], pb[:, T:NT], cst[:, C_INVW + n:C_INVW + n + 1], None, ALU.mult))
                    tt(pb[:, :], pb[:, :], x, ALU.subtract).then_inc(pool_d, 1)
                if kind == "att" and 1 <= n <= NU:
                    u = n - 1
                    ukind, h, i = UNITS[u]
                    m = NCMP_P if ukind == "cmp" else P * (i + 1)
                    pool.wait_ge(r_done, u + 1)
                    nc.gpsimd.tensor_scalar(PB[:, u % 2, 0:m], PB[:, u % 2, 0:m], ps_small[:, 8 + u % 2:9 + u % 2], None, ALU.mult).then_inc(scaled, 1)
                elif kind == "ln" and n == 0:
                    for k in range(KT):
                        pool.wait_ge(vln, k + 1)
                        nc.gpsimd.tensor_scalar(xres[:, k, :], lnt[:, k % 4, :], vec[:, V_B1 + k:V_B1 + k + 1], None, ALU.add).then_inc(ln_n, 1)
                elif kind == "evac" and n >= FF0 and FFN[n - FF0][0] == "up":
                    read(pool, ("mm", n))
                    if up_no >= 2:
                        pool.wait_ge(hid_l_done, up_no - 1)
                    nc.gpsimd.tensor_tensor(hsq[:, up_no % 2, :], relu[:, up_no % 2, :], relu[:, up_no % 2, :], ALU.mult).then_inc(sq_done, 1)
                    up_no += 1

        @block.vector
        def _(dve):
            tt, ts, stt, red = nc.vector.tensor_tensor, nc.vector.tensor_scalar, nc.vector.scalar_tensor_tensor, nc.vector.tensor_reduce
            steps = [0]

            def chain(ins):
                steps[0] += 1
                ins.then_inc(vch, 1)
                dve.wait_ge(vch, steps[0])

            def zview(ap):
                return ap.rearrange("p (a b) -> p a b", a=2)

            def spread(ap, m):
                return ap.unsqueeze(len(ap.shape)).to_broadcast(list(ap.shape) + [m])

            def spread_at(ap, axis, m):
                shape = list(ap.shape)
                return ap.unsqueeze(axis).to_broadcast(shape[:axis] + [m] + shape[axis:])

            up_no = 0
            taps = 0
            for step in TL:
                kind, n, *part = step
                if kind == "xsplit":
                    dve.wait_ge(xh_done, n + 1)
                    tt(opL[:, n, :], xres[:, n, :], opH[:, n, :].bitcast(F32), ALU.subtract).then_inc(xl_done, 1)
                elif kind == "split":
                    dve.wait_ge(h_done, n + 1)
                    m = KT * (NGATE if n == GATE_PANEL else P)
                    tt(wL[:, n % NW].rearrange("p a b -> p (a b)")[:, 0:m], raw[:, n % NRAW, 0:m],
                       wH[:, n % NW].rearrange("p a b -> p (a b)")[:, 0:m].bitcast(F32), ALU.subtract).then_inc(l_done, 1)
                elif kind == "cmpp" or kind == "nsa":
                    idx = 0 if kind == "cmpp" else n + 1
                    m = NCMP if idx else NCMP_P
                    if idx == 0:
                        read(dve, ("mm", 0))
                        dve.wait_ge(small_in, 32)
                        nc.vector.tensor_copy(xc[:, :, 0:32], zT[:, S_CMP, 0:T].rearrange("p (c r) -> p r c", r=16))
                        nc.vector.tensor_copy(xc[:, :, 32], vec[:, V_POS:V_POS + 16])
                        nc.vector.tensor_copy(xc[:, :, 33], vec[:, V_POS + 16:V_POS + 32]).then_inc(xc_done, 1)
                    dve.wait_ge(cmp_t1, idx + 1)
                    tt(hu[:, 2, 0:m], psum[:, 4, 0:m], hu[:, 1, 0:m], ALU.add).then_inc(cmp_u, 1)
                    if kind == "nsa":
                        dve.wait_ge(ssel_mm, n + 1)
                        s = psum[:, 6 + n % 2, :].rearrange("p (s r) -> p s r", s=8)
                        chain(red(nmS[:, n, :], s, AX.X, ALU.max, negate=True))
                        if n == 0:
                            dve.wait_ge(xh_done, KT)
                            dve.wait_ge(xl_done, KT)
                        tt(Psel[:, n, :].rearrange("p (s r) -> p s r", s=8), s, spread(nmS[:, n, :], HD), ALU.add).then_inc(ssel_sub, 1)
                    dve.wait_ge(cmp_th, idx + 1)
                    if idx:
                        dve.wait_ge(kv_mm, idx)
                    stt(hu[:, 0, 0:m], hu[:, 1, 0:m], 1.0, hu[:, 2, 0:m], ALU.add, ALU.mult).then_inc(hid_done, 1)
                elif kind == "kv" and n:
                    dve.wait_ge(ssel_exp, n)
                    red(lS[:, n - 1, :], Psel[:, n - 1, :].rearrange("p (s r) -> p s r", s=8), AX.X, ALU.add)
                elif kind in ("qn", "qm"):
                    read(dve, ("mm", PANEL_SLOT.index(S_Q + 1) if kind == "qn" else PANEL_SLOT.index(S_MQ + 1)))
                    dve.wait_ge(const_done, NCONSTS)
                    for h in range(H):
                        base = HD * (h % 2)
                        if kind == "qn":
                            nc.vector.tensor_copy(QNa[0:HD, :, h], zT[base:base + HD, S_Q + h // 2, T:NT])
                            last = nc.vector.tensor_copy(QNb[HD:P, :, h], zT[base:base + HD, S_Q + h // 2, T:NT])
                        else:
                            last = nc.vector.tensor_copy(QM[base:base + HD, h // 2, :, h], zT[base:base + HD, S_MQ + h // 2, T:NT])
                    last.then_inc(qn_done if kind == "qn" else qm_done, 1)
                elif kind == "glu":
                    read(dve, ("mm", PANEL_SLOT.index(S_CG + 1)))
                    dve.wait_ge(state_in, 32)
                    nc.vector.memset(zc[:, :, 0:CW - 1], 0.0)
                    for t in range(2):
                        stt(zc[:, t, CW - 1:], zT[:, S_CG + t, 0:T], 1.0, zT[:, S_CA + t, 0:T], ALU.add, ALU.mult)
                        stt(sc[:, t, :, CW - 1], zT[:, S_CG + t, T:NT], 1.0, zT[:, S_CA + t, T:NT], ALU.add, ALU.mult).then_inc(glu_done, 1)
                    dve.wait_ge(glu_done, 2)
                elif kind == "taps":
                    for k, t in TAPS[n[0]:n[1]]:
                        w = vec[:, V_DW + t * CW + k:V_DW + t * CW + k + 1]
                        if k == 0:
                            ts(yc[:, t, 0:T], zc[:, t, 0:T], w, vec[:, V_DWB + t:V_DWB + t + 1], ALU.mult, ALU.add).then_inc(vtap, 1)
                        else:
                            dve.wait_ge(vtap, taps - 1)
                            stt(yc[:, t, 0:T], zc[:, t, k:k + T], w, yc[:, t, 0:T], ALU.mult, ALU.add).then_inc(vtap, 1)
                        taps += 1
                    if n[1] == len(TAPS):
                        tmp = Vn[:, 0, :, :].rearrange("p a b -> p (a b)")[:, 0:B * CW].rearrange("p (b k) -> p b k", b=B)
                        for t in range(2):
                            chain(tt(tmp, sc[:, t], spread_at(vec[:, V_DW + t * CW:V_DW + (t + 1) * CW], 1, B), ALU.mult))
                            chain(red(yc[:, t, T:NT], tmp, AX.X, ALU.add))
                            last = ts(yc[:, t, T:NT], yc[:, t, T:NT], vec[:, V_DWB + t:V_DWB + t + 1], None, ALU.add)
                        last.then_inc(conv_done, 1)
                elif kind == "zcols":
                    dve.wait_ge(gate_t, 1)
                    ts(gT[:, :, :], gT[:, :, :], 0.5, 0.5, ALU.mult, ALU.add).then_inc(gate_done, 1)
                elif kind == "att":
                    if n < NU:
                        u = n
                        ukind, h, i = UNITS[u]
                        bk = psum[:, 4 + u % 2, :]
                        nm = ps_small[:, u % 2:u % 2 + 1]
                        dve.wait_ge(qk_done, u + 1)
                        if ukind == "cmp":
                            chain(tt(bk[:, 0:NCMP_P], bk[:, 0:NCMP_P], cst[:, C_CMPM + i * NCMP_P:C_CMPM + (i + 1) * NCMP_P], ALU.add))
                            if u >= 2:
                                dve.wait_ge(exp_done, u - 1)
                            chain(red(nm, bk[:, 0:NCMP_P], AX.X, ALU.max, negate=True))
                            ts(nm, nm, 1e20, None, ALU.min).then_inc(max_done, 1)
                        else:
                            m = P * (i + 1)
                            chain(tt(bk[:, m - P:m], bk[:, m - P:m], cst[:, C_CAUS:C_CAUS + P], ALU.add))
                            if u >= 2:
                                dve.wait_ge(exp_done, u - 1)
                            red(nm, bk[:, 0:m], AX.X, ALU.max, negate=True).then_inc(max_done, 1)
                    if 1 <= n <= NU:
                        u = n - 1
                        ukind, h, i = UNITS[u]
                        l, r = ps_small[:, 4 + u % 2:5 + u % 2], ps_small[:, 8 + u % 2:9 + u % 2]
                        dve.wait_ge(exp_done, u + 1)
                        if u >= 2:
                            dve.wait_ge(scaled, u - 1)
                        if ukind == "cmp":
                            chain(ts(l, l, 1e-30, None, ALU.max))
                        if ukind == "moba":
                            nc.vector.reciprocal(r, l).then_inc(r_done, 1)
                        else:
                            if u == 0:
                                dve.wait_ge(gate_done, 1)
                            c = {"cmp": 0, "sel": H, "win": 2 * H}[ukind] + h
                            chain(nc.vector.reciprocal(r, l))
                            ts(r, r, gT[:, i, c:c + 1], None, ALU.mult).then_inc(r_done, 1)
                elif kind == "cmean":
                    dve.wait_ge(cm_mm, 1)
                    for t in range(2):
                        last = tt(zview(yc[:, t, :]), zview(yc[:, t, :]), acc(step)[:, :, 0:HALF], ALU.subtract)
                    last.then_inc(acc_read[1], 1)
                elif kind == "cvar":
                    read(dve, step)
                    chain(nc.vector.reciprocal(zT[:, S_CG, :], zT[:, S_CG, :]))
                    for t in range(2):
                        chain(stt(yc[:, t, :], yc[:, t, :], vec[:, V_CG + t:V_CG + t + 1], zT[:, S_CG, :], ALU.mult, ALU.mult))
                        last = ts(yc[:, t, :], yc[:, t, :], vec[:, V_CB + t:V_CB + t + 1], None, ALU.add)
                    last.then_inc(cn_done, 1)
                    dve.wait_ge(cth, 1)
                    stt(yc[:, :, :], zT[:, S_CG:S_CG + 2, :], 1.0, yc[:, :, :], ALU.add, ALU.mult).then_inc(cact, 1)
                elif kind == "csc":
                    dve.wait_ge(csc_mm, 1)
                    s = psum[:, 0, 0:2 * P].rearrange("p (c x) -> p c x", c=2)[:, :, 0:NCMP]
                    chain(red(nmC, s, AX.X, ALU.max, negate=True))
                    tt(Pc[:, :, 0:NCMP], s, spread(nmC, NCMP), ALU.add).then_inc(bfree[0], 1)
                    dve.wait_ge(csc_exp, 1)
                    chain(red(lC, Pc[:, :, 0:NCMP], AX.X, ALU.add))
                    chain(nc.vector.reciprocal(lC, lC))
                    tt(Pc[:, :, 0:NCMP], Pc[:, :, 0:NCMP], spread(lC, NCMP), ALU.mult).then_inc(csc_done, 1)
                elif kind == "ctr":
                    dve.wait_ge(ctr_mm, 1)
                    nc.vector.tensor_copy(PcT[0:NCMP, :, :], psum[0:NCMP, 1, 0:2 * P].rearrange("p (c x) -> p c x", c=2)).then_inc(bfree[1], 1)
                    bank_read(dve, 1, step)
                    red(ps_small[0:NCMP, 16:16 + B].rearrange("p (c j) -> p c j", c=2),
                        PcT[0:NCMP, :, :].rearrange("p c (j h) -> p c j h", j=4)[:, :, :, 0:H], AX.X, ALU.add).then_inc(ctr_done, 1)
                elif kind == "cimp":
                    dve.wait_ge(cimp_mm, 1)
                    imp, m8, imp2, imp3, nsel = sm[:, 16:49], sm[:, 56:64], sm[:, 64:97], sm[:, 100:133], sm[:, 136:169]
                    nc.vector.tensor_copy(imp, psum[0:B, 0, 0:NSELB]).then_inc(bfree[0], 1)
                    bank_read(dve, 0, step)
                    nc.vector.memset(imp[:, 0:1], 1e30)
                    chain(nc.vector.memset(imp[:, NSELB - 2:NSELB], 1e30))
                    chain(nc.vector.max(m8, imp))
                    chain(nc.vector.match_replace(imp2, m8, imp, -1.0))
                    chain(nc.vector.max(m8, imp2))
                    chain(nc.vector.match_replace(imp3, m8, imp2, -1.0))
                    chain(tt(nsel, imp3, imp, ALU.is_equal))
                    chain(ts(nsel, nsel, -NEG, None, ALU.mult))
                elif kind == "win":
                    dve.wait_ge(win_mm, 1)
                    dve.wait_ge(csc_mm, 1)
                    for c in range(2):
                        s = psum[:, c, :].rearrange("p (b x) -> p b x", b=4)
                        chain(red(nmW[:, 4 * c:4 * c + 4], s, AX.X, ALU.max, negate=True))
                        tt(Pwin[:, 4 * c:4 * c + 4, :], s, spread(nmW[:, 4 * c:4 * c + 4], P), ALU.add).then_inc(bfree[c], 1)
                    dve.wait_ge(win_exp, 1)
                    red(lW, Pwin[:, :, :], AX.X, ALU.add).then_inc(win_l, 1)
                elif kind == "mu":
                    u = n
                    if u < MU:
                        dve.wait_ge(ms_mm, u + 1)
                        red(nmM[:, u:u + 1], psum[:, 0, 0:P], AX.X, ALU.max, negate=True)
                        red(gM[:, u:u + 1], psum[:, 0, 0:P], AX.X, ALU.add).then_inc(mmax, 1)
                    if u >= 1:
                        dve.wait_ge(mt_mm, u)
                        nc.vector.tensor_copy(PTm2[:, (u - 1) % 2, :], psum[:, 1, 0:P]).then_inc(bfree[1], 1)
                elif kind == "mp":
                    dve.wait_ge(mp_mm, n + 1)
                    if n == 0:
                        dve.wait_ge(kv_mm, B + 1)
                    tt(own[:, :].rearrange("p (h d) -> p h d", h=H), psum[:, 1, 0:256].rearrange("p (h d) -> p h d", h=H),
                       spread(cst[:, C_HM:C_HM + H], HD), ALU.mult).then_inc(bfree[1], 1)
                    bank_read(dve, 1, step)
                    red(OM[:, n, :], own[:, :].rearrange("p (h d) -> p d h", h=H), AX.X, ALU.add).then_inc(om_done, 1)
                    dve.wait_ge(om_done, n + 1)
                elif kind == "stat":
                    NM, LL = eb[:, 0], eb[:, 1]
                    G4 = sm[:, 176:240].rearrange("p (h s) -> p h s", h=H)
                    dve.wait_ge(stat_mm, n + 1)

                    def seg(k, q):
                        return psum[0:B, k, q * P:(q + 1) * P].rearrange("p (j x) -> p j x", j=4)[:, :, 0:H]

                    if n == 0:
                        for k in range(4):
                            for half in range(2):
                                s = psum[0:B, k, :].rearrange("p (s j x) -> p s j x", s=4, j=4)[:, :, 2 * half:2 * half + 2, 0:H]
                                lo = half * 16 + (k % 2) * 8
                                dst = (NM if k < 2 else LL)[:, :, lo:lo + 8].rearrange("p h (s g) -> p s g h", g=2)
                                if k < 2:
                                    blk = sm[:, 136 + half:136 + half + 32:2].rearrange("p (g s) -> p s g", g=2)[:, 4 * k:4 * k + 4, :]
                                    last = tt(dst, s, spread(blk, H), ALU.add)
                                else:
                                    last = nc.vector.tensor_copy(dst, s)
                            last.then_inc(bfree[k], 1)
                    elif n == 1:
                        items = [(NM, 50), (LL, 50)] + [(NM, 33 + 4 * k) for k in range(4)] + [(G4, 4 * k) for k in range(4)]
                        for q, (dst, lo) in enumerate(items):
                            last = nc.vector.tensor_copy(dst[:, :, lo:lo + 4].rearrange("p h j -> p j h"), seg(q // 4, q % 4))
                            if q % 4 == 3 or q == len(items) - 1:
                                last.then_inc(bfree[q // 4], 1)
                    else:
                        for k in range(4):
                            last = nc.vector.tensor_copy(LL[:, :, 33 + 4 * k:37 + 4 * k].rearrange("p h j -> p j h"), seg(0, k))
                        last.then_inc(bfree[0], 1)
                elif kind == "own":
                    NM, LL = eb[:, 0], eb[:, 1]
                    dve.wait_ge(mm_done, N_IN_PANELS)
                    tmp = WB[:, 0:2, :].rearrange("p a b -> p (a b)").rearrange("p (h d) -> p h d", h=H)
                    q = zs[:, 4:6, :].rearrange("p a b -> p (a b)").rearrange("p (h d) -> p h d", h=H)
                    mq = zs[:, 6:8, :].rearrange("p a b -> p (a b)").rearrange("p (h d) -> p h d", h=H)
                    mk = zs[:, 8:10, :].rearrange("p a b -> p (a b)").rearrange("p (h d) -> p h d", h=H)
                    bank_read(dve, 0, ("zrow", 2))
                    bank_read(dve, 1, ("zrow", 1))
                    for x, k, at_ in ((q, spread_at(zs[:, 1, 0:HD], 1, H), 32), (mq, mk, 49), (q, spread_at(zs[:, 3, 0:HD], 1, H), 54)):
                        chain(tt(tmp, x, k, ALU.mult))
                        chain(red(NM[:, :, at_], tmp, AX.X, ALU.add, negate=True))
                        nc.vector.memset(LL[:, :, at_], 1.0)
                elif kind == "comb":
                    NM, LL, E = eb[:, 0], eb[:, 1], eb[:, 2]
                    G4 = sm[:, 176:240].rearrange("p (h s) -> p h s", h=H)
                    G13 = sm[:, 240:292].rearrange("p (h s) -> p h s", h=H)
                    R13 = sm[:, 292:344].rearrange("p (h s) -> p h s", h=H)
                    m8, MN, L3 = sm[:, 344:352], sm[:, 352:364].rearrange("p (a h) -> p a h", a=3), sm[:, 364:376].rearrange("p (a h) -> p a h", a=3)
                    parts = ((0, 33), (33, 50), (50, 55))
                if kind == "comb" and n == 0:
                    bank_read(dve, 0, ("stat", 2))
                    nc.vector.memset(G13[:, :, 8:13], 3e38)
                    g2 = G4.rearrange("p h (s e) -> p h s e", e=2)
                    chain(tt(G13[:, :, 0:8], g2[:, :, :, 0], g2[:, :, :, 1], ALU.add))
                    for h in range(H):
                        chain(nc.vector.max(m8, G13[:, h, :]))
                        chain(nc.vector.match_replace(R13[:, h, :], m8, G13[:, h, :], -3e38))
                    chain(tt(R13[:, :, 0:8], R13[:, :, 0:8], G13[:, :, 0:8], ALU.is_equal))
                    chain(ts(R13[:, :, 0:8], R13[:, :, 0:8], -NEG, None, ALU.mult))
                    mm_ = NM[:, :, 33:49].rearrange("p h (s e) -> p h s e", e=2)
                    for e in range(2):
                        last = tt(mm_[:, :, :, e], mm_[:, :, :, e], R13[:, :, 0:8], ALU.add)
                    chain(last)
                    for br, (lo, hi) in enumerate(parts):
                        last = red(MN[:, br, :], NM[:, :, lo:hi], AX.X, ALU.min)
                    chain(last)
                    for br, (lo, hi) in enumerate(parts):
                        last = tt(E[:, :, lo:hi], spread(MN[:, br, :], hi - lo), NM[:, :, lo:hi], ALU.subtract)
                    last.then_inc(comb_sub, 1)
                if kind == "comb" and n == 1:
                    dve.wait_ge(comb_exp, 1)
                    nc.vector.memset(WB[:, :, :], 0.0)
                    nc.vector.memset(gdiag[:, :, :], 0.0)
                    ts(sm[:, 0:NGATE], sm[:, 0:NGATE], 0.5, 0.5, ALU.mult, ALU.add)
                    chain(tt(NM, E, LL, ALU.mult))
                    for br, (lo, hi) in enumerate(parts):
                        last = red(L3[:, br, :], NM[:, :, lo:hi], AX.X, ALU.add)
                    chain(last)
                    chain(nc.vector.reciprocal(L3, L3))
                    tt(L3[:, 0, :], L3[:, 0, :], sm[:, H:2 * H], ALU.mult)
                    chain(tt(L3[:, 2, :], L3[:, 2, :], sm[:, 2 * H:3 * H], ALU.mult))
                    for br, (lo, hi) in enumerate(parts):
                        last = tt(E[:, :, lo:hi], E[:, :, lo:hi], spread(L3[:, br, :], hi - lo), ALU.mult)
                    chain(last)
                    for half in range(2):
                        nc.vector.tensor_copy(
                            WB[:, 0:8, 64 * half:64 * half + 64].rearrange("p s (g x) -> p s g x", g=2)[:, :, :, 0:H],
                            E[:, :, 16 * half:16 * half + 16].rearrange("p h (s g) -> p s g h", g=2))
                    nc.vector.tensor_copy(WB[:, 8, :].rearrange("p (j x) -> p j x", j=4)[:, :, 0:H], E[:, :, 50:54].rearrange("p h j -> p j h"))
                    nc.vector.tensor_copy(WB[:, 9:13, :].rearrange("p s (j x) -> p s j x", j=4)[:, :, :, 0:H],
                                          E[:, :, 33:49].rearrange("p h (s j) -> p s j h", j=4))
                    delta = cst[0:B, C_DELTA:C_DELTA + B]
                    for br, at_ in enumerate((32, 49, 54)):
                        tt(wnew[:, br, :, :], spread_at(E[:, :, at_], 1, B), spread(delta, H), ALU.mult)
                    tt(gdiag[:, :, 0:H], spread_at(sm[:, 0:H], 1, B), spread(delta, H), ALU.mult).then_inc(wb_done, 1)
                elif kind == "back":
                    bank_read(dve, 0, step)
                    nc.vector.memset(zeros[:, :], 0.0)
                    wv = Wt[:, :, :].rearrange("p s b -> p b s")
                    tt(Pwin[:, :, :], Pwin[:, :, :], spread(Wt[:, 8, :], P), ALU.mult)
                    for b in range(B):
                        rows = Psel[:, b, :].rearrange("p (s r) -> p s r", s=8)
                        tt(rows, rows, spread(wv[:, b, 0:8], HD), ALU.mult).then_inc(pscaled, 1)
                    hm = cst[:, C_HM:C_HM + H]
                    for b in range(B):
                        last = tt(Wd[:, b, :, :], spread(wv[:, b, 9:13], H), spread_at(hm, 1, 4), ALU.mult)
                    last.then_inc(md_done, 1)
                elif kind == "spv" and n < B:
                    dve.wait_ge(st_mm, n + 1)
                    if n >= 2:
                        dve.wait_ge(spv_mm, n - 1)
                    for k in range(2):
                        s = psum[0:HD, k, :].rearrange("p (s j x) -> p s j x", s=4, j=4)
                        for half in range(2):
                            last = nc.vector.tensor_copy(
                                PTs[HD * half:HD * half + HD, n % 2, :, 4 * k:4 * k + 4, :].rearrange("p g s h -> p s g h"),
                                s[:, :, 2 * half:2 * half + 2, 0:H])
                        last.then_inc(bfree[k], 1)
                elif kind == "mpv":
                    dve.wait_ge(spv_mm, B)
                    bank_read(dve, 1, ("back", 0))
                    bank_read(dve, 1, ("cimp", 0))
                    for c in range(2):
                        last = stt(On[:, c, :], oc[:, c, :], g0[:, c:c + 1], psum[:, 3, c * HD:(c + 1) * HD], ALU.mult, ALU.add)
                    last.then_inc(fin_o, 1)
                    dve.wait_ge(mpv_mm, 1)
                    tt(newV[:, :, :].rearrange("p c (h d) -> p c h d", h=H), psum[:, 1, :].rearrange("p (c h d) -> p c h d", c=2, h=H),
                       spread_at(spread(cst[:, C_HM:C_HM + H], HD), 1, 2), ALU.mult).then_inc(bfree[1], 1)
                    bank_read(dve, 1, step)
                    chain(red(Om[:, :, :], newV[:, :, :].rearrange("p c (h d) -> p c d h", h=H), AX.X, ALU.add))
                    tt(Om[:, :, :], Om[:, :, :], psum[:, 2, 0:P].rearrange("p (c d) -> p c d", c=2), ALU.add).then_inc(bfree[2], 1)
                elif kind == "fin":
                    dve.wait_ge(fin_mm, 1)
                    for h in range(H):
                        base = HD * (h % 2)
                        last = nc.vector.tensor_copy(zT[base:base + HD, S_MQ + h // 2, T:NT],
                                                     psum[0:HD, 1, 0:256].rearrange("p (b x) -> p b x", x=32)[:, :, h])
                    last.then_inc(bfree[1], 1)
                elif kind == "msplit":
                    dve.wait_ge(mixh, n + 1)
                    k = MIX_ORDER[n]
                    tt(opL[:, k, :], zT[:, MIX_SLOT[k], :], opH[:, k, :].bitcast(F32), ALU.subtract).then_inc(mixl, 1)
                elif kind == "evac" and OUT0 <= n < FF0:
                    dve.wait_ge(mm_done, n + 1)
                    dve.wait_ge(x_in, 16)
                    x = zview(xres[:, n - OUT0, :])
                    stt(x, x, ALPHA, acc(("mm", n))[:, :, 0:HALF], ALU.mult, ALU.add).then_inc(acc_read[1], 1)
                elif kind == "evac" and n >= FF0:
                    fkind, g, m = FFN[n - FF0]
                    if fkind == "up":
                        dve.wait_ge(sq_done, up_no + 1)
                        dve.wait_ge(hidh_done, up_no + 1)
                        tt(hidL[g % 2][:, m, :], hsq[:, up_no % 2, :], hidH[g % 2][:, m, :].bitcast(F32), ALU.subtract).then_inc(hid_l_done, 1)
                        up_no += 1
                    else:
                        dve.wait_ge(mm_done, n + 1)
                        dve.wait_ge(acc_read[1], nread(("mm", n)) - 1)
                        if g == 0 and m == 0:
                            dve.wait_ge(ln_n, KT)
                        x = zview(xres[:, m, :])
                        stt(x, x, ALPHA if g == 0 else 1.0, acc(("mm", n))[:, :, 0:HALF], ALU.mult, ALU.add).then_inc(acc_read[1], 1)
                elif kind == "ln":
                    G = (V_G1, V_G2)[n]
                    dve.wait_ge(ln_mm, n + 1)
                    read(dve, ("mm", FF0 - 1 if n == 0 else N_PANELS - 1))
                    for k in range(KT):
                        tt(zview(xres[:, k, :]), zview(xres[:, k, :]), psum[:, 4:6, 0:HALF], ALU.subtract).then_inc(ln_d, 1)
                    dve.wait_ge(ln_std, n + 1)
                    dve.wait_ge(ln_sq, (n + 1) * KT)
                    dve.wait_ge(ln_d, (n + 1) * KT)
                    chain(nc.vector.reciprocal(std[:, :], std[:, :]))
                    for k in range(KT + 2):
                        if k < KT:
                            if k >= 4:
                                dve.wait_ge(ln_n, n * KT + k - 3)
                                if n == 0:
                                    dve.wait_ge(ln_h, k - 3)
                            stt(lnt[:, k % 4, :], xres[:, k, :], vec[:, G + k:G + k + 1], std[:, :], ALU.mult, ALU.mult).then_inc(vln, 1)
                        if k >= 2 and n == 0:
                            dve.wait_ge(ln_h, k - 1)
                            dve.wait_ge(ln_n, k - 1)
                            tt(opL[:, k - 2, :], xres[:, k - 2, :], opH[:, k - 2, :].bitcast(F32), ALU.subtract).then_inc(ln_l, 1)


def layouts(x):
    f = lambda v: np.ascontiguousarray(v)
    xT = np.concatenate([x["x_prompt"].reshape(T, D), x["x_sample"].reshape(B, D)], 0).T
    w_in = x["w_in"][0]
    c0 = np.cumsum([0, 512, 256, 384, 12, 768, 256])
    kv, mo = c0[2], c0[4]
    r = lambda lo, n=P: list(range(lo, lo + n))
    cols = {S_CMP: r(kv), S_KSEL: r(kv + 128, 64) + r(kv + 256, 64), S_V: r(kv + 192, 64) + r(kv + 320, 64)}
    for t in range(2):
        cols[S_Q + t] = r(c0[1] + t * P)
        cols[S_CA + t] = r(c0[0] + t * P)
        cols[S_CG + t] = r(c0[0] + 256 + t * P)
        cols[S_PO + t] = r(c0[5] + t * P)
        for s, base in ((S_MQ, 0), (S_MK, 256), (S_MV, 512)):
            cols[s + t] = r(mo + base + t * P)

    def panel(w, rows, c):
        return w[rows][:, c].reshape(KT, P, len(c)).transpose(1, 0, 2)

    allr = slice(0, D)
    panels = [panel(w_in, allr, cols[s]) for s in PANEL_SLOT if s != S_GATE]
    panels += [panel(x["w_out"][0], allr, r(t * P)) for t in range(KT)]
    for kind, g, n in FFN:
        if kind == "up":
            panels.append(panel(x["w_up"][0], allr, r((g * KT + n) * P)))
        else:
            panels.append(panel(x["w_down"][0], slice(g * D, (g + 1) * D), r(n * P)))
    nsa = x["cache_nsa_kv"][0]
    cmpT = nsa[:, :, 0:2].reshape(NPOOL, 8, 16, 2, HD).transpose(0, 3, 4, 2, 1).reshape(NPOOL, P, P)
    selK = nsa[:, :, 2].reshape(NPOOL, 2, HD, HD).transpose(0, 1, 3, 2).reshape(NPOOL, P, HD)
    mob = x["cache_moba_kv"][0]
    mK = mob[:, :, 0].transpose(0, 2, 3, 1).reshape(NPOOL, 2, P, PAGE).transpose(0, 2, 1, 3).reshape(NPOOL, P, 256)
    mV = mob[:, :, 1].reshape(NPOOL, PAGE, 256)
    win = x["state_nsa_win"][0]
    winK = win[:, :, 0].reshape(B, 2, 256, HD).transpose(1, 3, 0, 2).reshape(P, B, 256)
    winV = win[:, :, 1].reshape(B, 4, P, HD).transpose(2, 0, 1, 3)
    w1 = x["nsa_cmp_w1"][0].reshape(2, 32, HD, HD)
    w1d = np.zeros((P, 32, P), np.float32)
    w1d[0:HD, :, 0:HD] = w1[0].transpose(1, 0, 2)
    w1d[HD:P, :, HD:P] = w1[1].transpose(1, 0, 2)
    vec = np.zeros((P, NVEC), np.float32)

    def put(at, v, rows=slice(0, P)):
        v = np.asarray(v).reshape(v.shape[0], -1)
        vec[rows, at:at + v.shape[1]] = v

    tiles = lambda v: v.reshape(-1, P).T
    put(V_DW, x["conv_dw"][0].T.reshape(2, P, CW).transpose(1, 0, 2))
    put(V_DWB, tiles(x["conv_dw_b"][0]))
    put(V_CG, tiles(x["conv_ln_g"][0]))
    put(V_CB, tiles(x["conv_ln_b"][0]))
    put(V_PS, tiles(x["pool_scale"][0]))
    put(V_G1, tiles(x["ln1_g"][0]))
    put(V_B1, tiles(x["ln1_b"][0]))
    put(V_G2, tiles(x["ln2_g"][0]))
    put(V_B2, tiles(x["ln2_b"][0]))
    put(V_POS, x["nsa_cmp_pos"][0].transpose(0, 2, 1).reshape(P, 32))
    put(V_W2, x["nsa_cmp_w2"][0].reshape(P, HD))
    put(V_PW, x["conv_pw"][0].reshape(2, P, 256).transpose(1, 0, 2))
    for g in range(4):
        lo = HD * (g % 2)
        put(V_PO + g // 2 * P + lo, x["pool_w"][0, g], slice(lo, lo + HD))
    cst = np.zeros((P, NCONST), np.float32)
    p_ = np.arange(P)
    cst[:, C_ID:C_ID + P] = np.eye(P)
    cst[:, C_CAUS:C_CAUS + P] = np.where(p_[None, :] <= p_[:, None], 0.0, NEG)
    for i in range(QT):
        last = 16 * np.arange(NCMP_P) + 31
        cst[:, C_CMPM + i * NCMP_P:C_CMPM + (i + 1) * NCMP_P] = np.where(last[None, :] <= (i * P + p_)[:, None], 0.0, NEG)
    j, s = np.arange(NCMP)[:, None], np.arange(NSELB)[None, :]
    cst[0:NCMP, C_COVER:C_COVER + NSELB] = (j * 16 < (s + 1) * 64) & (j * 16 + 32 > s * 64)
    cst[0:B, C_DELTA:C_DELTA + B] = np.eye(B)
    for h in range(H):
        cst[:, C_HM + h] = p_ % 32 == h
    for n in range(2):
        w = np.where(p_ < HD, 2 * 4 ** n, 4 * 4 ** n)
        cst[:, C_INVC + 16 * n:C_INVC + 16 * n + 16] = 1.0 / np.minimum(w[:, None], np.arange(16)[None, :] + 1)
        cst[:, C_INVW + n] = 1.0 / w
    return {
        "xT": f(xT.reshape(KT, P, NT).transpose(1, 0, 2)),
        "panels": f(np.stack([p.reshape(P, D) for p in panels])),
        "w_gate": f(panel(w_in, allr, r(c0[3], NGATE)).reshape(P, KT * NGATE)),
        "nsa_pages": f(np.concatenate([cmpT, selK], 2)),
        "selv_pages": f(nsa[:, :, 3]),
        "moba_pages": f(np.concatenate([mK, mV], 2)),
        "winK": f(winK), "winV": f(winV), "state_win": f(win.reshape(B, T, P)),
        "state_convT": f(x["state_conv"][0].transpose(2, 0, 1).reshape(2, P, B, CW - 1).transpose(1, 0, 2, 3)),
        "state_poolT": f(x["state_pool"][0].transpose(2, 0, 1).reshape(2, P, B, 15).transpose(1, 0, 2, 3)),
        "page_table": f(x["page_table"].reshape(1, B * PAGES).astype(np.int32)),
        "w1": w1d, "vecs": vec, "consts": cst,
    }


OUTS = {"y": (P, KT, NT), "z_cmp": (P, NT), "z_ksel": (HD, NT), "z_kwin": (HD, NT), "z_v": (P, NT), "z_moba": (P, 4, NT),
        "win_sample": (B, T, P), "conv_prompt": (P, 2, CW - 1), "conv_sample": (P, 2, B, CW - 1),
        "pool_prompt": (P, 2, 15), "pool_sample": (P, 2, B, 15)}


def kernel(**inputs):
    import concourse.bacc as bacc
    from concourse.bass_utils import run_bass_kernel_spmd

    x = {k: np.asarray(v) for k, v in inputs.items()}
    arrays = {"in_" + k: v for k, v in layouts(x).items()}
    nc = bacc.Bacc("TRN2", target_bir_lowering=False, num_devices=1)
    a = {k[3:]: nc.dram_tensor(k, v.shape, mybir.dt.from_np(v.dtype), kind="ExternalInput").ap() for k, v in arrays.items()}
    o = {k: nc.dram_tensor("out_" + k, s, F32, kind="ExternalOutput").ap() for k, s in OUTS.items()}
    build(nc, a, o)
    r = run_bass_kernel_spmd(nc, [arrays], core_ids=[0]).results[0]
    g = {k: np.asarray(r["out_" + k]) for k in OUTS}
    y = g["y"].transpose(2, 1, 0).reshape(NT, D)
    mz = g["z_moba"].transpose(2, 1, 0).reshape(NT, 2, H, HD)
    nz = np.stack([g["z_cmp"][0:HD].T, g["z_cmp"][HD:P].T, g["z_ksel"].T, g["z_v"][0:HD].T], 1)
    wz = np.stack([g["z_kwin"][:, 0:T].T, g["z_v"][HD:P, 0:T].T], 1)
    up = lambda v: np.ascontiguousarray(v)
    chan = lambda v: v.transpose(1, 0, *range(2, v.ndim)).reshape(2 * P, *v.shape[2:])
    return (up(y[:T].reshape(1, T, D)), up(y[T:].reshape(B, 1, D)),
            up(mz[:T].reshape(1, 1, T, 2, H, HD)), up(mz[T:].reshape(1, B, 1, 2, H, HD)),
            up(nz[:T].reshape(1, 1, T, 4, HD)), up(nz[T:].reshape(1, B, 1, 4, HD)),
            up(wz.reshape(1, 1, T, 2, HD)), up(g["win_sample"].reshape(1, B, T, 2, HD)),
            up(chan(g["conv_prompt"]).T.reshape(1, 1, CW - 1, 256)),
            up(chan(g["conv_sample"]).transpose(1, 2, 0).reshape(1, B, CW - 1, 256)),
            up(chan(g["pool_prompt"]).T.reshape(1, 1, 15, 256)),
            up(chan(g["pool_sample"]).transpose(1, 2, 0).reshape(1, B, 15, 256)))
```
